# Optimizing a Trainium2 kernel written in Bass

```python
import math
import jax, jax.numpy as jnp
from jax import lax
import numpy as np

D_MODEL = 1024
BATCH = 1
SEQ = 256
DEPTH = 2

HEAD_DIM = 64
ROPE_DIM = HEAD_DIM // 4
ROPE_THETA = 500000.0
NORM_EPS = 1e-6
Q_BLOCK = 128
SCALE = HEAD_DIM ** -0.5
NEG = -1e30
FORCE = 1e9

NSA_HEADS = 5
CMP_BLOCK = 32
CMP_STRIDE = 16
CMP_HIDDEN = 128
SLC_BLOCK = 64
SLC_TOPN = 16
WIN = 512

DSA_HEADS = 5
IDX_HEADS = 8
IDX_DIM = 32
IDX_ROPE_DIM = IDX_DIM // 4
DSA_TOPK_MAX = 256

DIL_PAIRS = ((128, 1), (512, 4), (2048, 16))
DIL_HEADS_PER_GROUP = 2
DIL_HEADS = len(DIL_PAIRS) * DIL_HEADS_PER_GROUP
DIL_KEYS = DIL_PAIRS[0][0] // DIL_PAIRS[0][1] + 1

D_MIX = (NSA_HEADS + DSA_HEADS + DIL_HEADS) * HEAD_DIM

D_FF = 2816
CONV_WIDTH = 3

IN_SPLITS = (
    NSA_HEADS * HEAD_DIM,
    HEAD_DIM, HEAD_DIM,
    HEAD_DIM, HEAD_DIM,
    HEAD_DIM, HEAD_DIM,
    3 * NSA_HEADS,
    DSA_HEADS * HEAD_DIM, HEAD_DIM, HEAD_DIM,
    IDX_HEADS * IDX_DIM, IDX_DIM, IDX_HEADS,
    DIL_HEADS * HEAD_DIM, DIL_HEADS * HEAD_DIM, DIL_HEADS * HEAD_DIM,
)
D_IN = sum(IN_SPLITS)
IN_OFFSETS = tuple(int(o) for o in np.cumsum(IN_SPLITS)[:-1])


def rmsnorm(x, g):
    xf = x.astype(jnp.float32)
    y = xf * lax.rsqrt(jnp.mean(xf * xf, axis=-1, keepdims=True) + NORM_EPS)
    return (y * g.astype(jnp.float32)).astype(x.dtype)

def rope_tables(L, rot_dim, dtype):
    inv = 1.0 / (ROPE_THETA ** (np.arange(0, rot_dim, 2, dtype=np.float32) / np.float32(rot_dim)))
    ang = np.arange(L, dtype=np.float32)[:, None] * inv[None, :]
    return jnp.asarray(np.cos(ang), dtype=dtype), jnp.asarray(np.sin(ang), dtype=dtype)

def apply_rope(x, cos, sin):
    r = 2 * cos.shape[-1]
    x1, x2, xp = x[..., : r // 2], x[..., r // 2 : r], x[..., r:]
    c, s = cos[None, :, None, :], sin[None, :, None, :]
    return jnp.concatenate([x1 * c - x2 * s, x2 * c + x1 * s, xp], axis=-1)

def rope1(k, cos, sin):
    return apply_rope(k[:, :, None], cos, sin)[:, :, 0]

def masked_softmax(s, mask):
    s = jnp.where(mask, s, NEG)
    m = jnp.max(s, axis=-1, keepdims=True)
    e = jnp.where(mask, jnp.exp(s - m), 0.0)
    den = jnp.maximum(jnp.sum(e, axis=-1, keepdims=True), 1e-30)
    return e / den, m + jnp.log(den)

def to_chunks(a):
    b, l = a.shape[:2]
    return jnp.moveaxis(a.reshape(b, l // Q_BLOCK, Q_BLOCK, *a.shape[2:]), 1, 0)

def from_chunks(a):
    a = jnp.moveaxis(a, 0, 1)
    return a.reshape(a.shape[0], a.shape[1] * a.shape[2], *a.shape[3:])

def q_positions(L):
    return jnp.arange(L).reshape(L // Q_BLOCK, Q_BLOCK)

def gather_rows(table, idx):
    return jax.vmap(lambda t, i: t[i])(table, idx)

def nsa_mixer(q, kc, vc, ks, vs, kw, vw, g, cmp_pos, cmp_w1, cmp_w2, cos, sin):
    B, L, H, D = q.shape
    t = jnp.arange(L)
    n_cmp = (L - CMP_BLOCK) // CMP_STRIDE + 1
    c_start = np.arange(n_cmp) * CMP_STRIDE
    blk_idx = c_start[:, None] + np.arange(CMP_BLOCK)[None, :]
    raw = jnp.stack([kc, vc], axis=0)[:, :, blk_idx] + cmp_pos[:, None, None]
    hid = jax.nn.gelu(jnp.einsum('cbnf,cfh->cbnh', raw.reshape(2, B, n_cmp, CMP_BLOCK * D), cmp_w1))
    kv_cmp = jnp.einsum('cbnh,chd->cbnd', hid, cmp_w2)
    k_cmp, v_cmp = kv_cmp[0], kv_cmp[1]
    s_c = jnp.einsum('bthd,bnd->bhtn', q, k_cmp).astype(jnp.float32) * SCALE
    mask_c = jnp.asarray(c_start + CMP_BLOCK - 1)[None, :] <= t[:, None]
    p_c, _ = masked_softmax(s_c, mask_c)
    o_cmp = jnp.einsum('bhtn,bnd->bthd', p_c.astype(v_cmp.dtype), v_cmp)
    n_slc = L // SLC_BLOCK
    s_start = np.arange(n_slc) * SLC_BLOCK
    overlap = ((c_start[:, None] < s_start[None, :] + SLC_BLOCK)
               & (c_start[:, None] + CMP_BLOCK > s_start[None, :])).astype(np.float32)
    imp = jnp.einsum('bhtn,nj->btj', p_c, jnp.asarray(overlap))
    cur = t // SLC_BLOCK
    j = jnp.arange(n_slc)
    valid_blk = j[None, :] <= cur[:, None]
    forced = (j[None, :] == 0) | (j[None, :] == cur[:, None]) | (j[None, :] == cur[:, None] - 1)
    imp = jnp.where(forced, FORCE, jnp.where(valid_blk, imp, NEG))
    n_top = min(SLC_TOPN, n_slc)
    top_s, sel = lax.top_k(imp, n_top)
    sel_ok = top_s > 0.5 * NEG
    q_r = apply_rope(q, cos, sin)
    ks_blocks = rope1(ks, cos, sin).reshape(B, n_slc, SLC_BLOCK, D)
    vs_blocks = vs.reshape(B, n_slc, SLC_BLOCK, D)
    in_blk = jnp.arange(SLC_BLOCK)

    def sel_chunk(args):
        qc, selc, okc, tc = args
        kg = gather_rows(ks_blocks, selc).reshape(B, Q_BLOCK, n_top * SLC_BLOCK, D)
        vg = gather_rows(vs_blocks, selc).reshape(B, Q_BLOCK, n_top * SLC_BLOCK, D)
        kpos = (selc[..., None] * SLC_BLOCK + in_blk).reshape(B, Q_BLOCK, -1)
        ok = jnp.broadcast_to(okc[..., None], okc.shape + (SLC_BLOCK,)).reshape(B, Q_BLOCK, -1)
        ok = ok & (kpos <= tc[None, :, None])
        s = jnp.einsum('bqhd,bqkd->bqhk', qc, kg).astype(jnp.float32) * SCALE
        p, _ = masked_softmax(s, ok[:, :, None, :])
        return jnp.einsum('bqhk,bqkd->bqhd', p.astype(vg.dtype), vg)

    o_slc = from_chunks(lax.map(sel_chunk, (to_chunks(q_r), to_chunks(sel), to_chunks(sel_ok), q_positions(L))))
    nb = L // Q_BLOCK
    kw_p = jnp.pad(rope1(kw, cos, sin), ((0, 0), (WIN, 0), (0, 0)))
    vw_p = jnp.pad(vw, ((0, 0), (WIN, 0), (0, 0)))
    span_idx = np.arange(nb)[:, None] * Q_BLOCK + np.arange(Q_BLOCK + WIN)[None, :]
    kband, vband = kw_p[:, span_idx], vw_p[:, span_idx]
    s_w = jnp.einsum('bnqhd,bnkd->bnhqk', q_r.reshape(B, nb, Q_BLOCK, H, D), kband).astype(jnp.float32) * SCALE
    key_pos = span_idx - WIN
    qpos = np.arange(nb)[:, None] * Q_BLOCK + np.arange(Q_BLOCK)[None, :]
    diff = qpos[:, :, None] - key_pos[:, None, :]
    mask_w = jnp.asarray((diff >= 0) & (diff < WIN) & (key_pos[:, None, :] >= 0))
    p_w, _ = masked_softmax(s_w, mask_w[None, :, None])
    o_win = jnp.einsum('bnhqk,bnkd->bnqhd', p_w.astype(vband.dtype), vband).reshape(B, L, H, D)
    gs = jax.nn.sigmoid(g)
    return gs[..., 0:1] * o_cmp + gs[..., 1:2] * o_slc + gs[..., 2:3] * o_win

def dsa_mixer(q, k, v, qi, ki, wi, cos_h, sin_h, cos_i, sin_i):
    B, L = q.shape[:2]
    q = apply_rope(q, cos_h, sin_h)
    k = rope1(k, cos_h, sin_h)
    qi = apply_rope(qi, cos_i, sin_i)
    ki = rope1(ki, cos_i, sin_i)
    top = min(DSA_TOPK_MAX, L // 4)
    keys = jnp.arange(L)

    def chunk(args):
        qc, qic, wc, tc = args
        dots = jnp.einsum('bqhi,bsi->bqhs', qic, ki).astype(jnp.float32) * IDX_DIM ** -0.5
        score = jnp.einsum('bqh,bqhs->bqs', wc.astype(jnp.float32) * IDX_HEADS ** -0.5, jax.nn.relu(dots))
        score = jnp.where(keys[None, None, :] <= tc[None, :, None], score, NEG)
        top_s, sel = lax.top_k(score, top)
        ok = top_s > 0.5 * NEG
        kg, vg = gather_rows(k, sel), gather_rows(v, sel)
        s = jnp.einsum('bqhd,bqkd->bqhk', qc, kg).astype(jnp.float32) * SCALE
        p, _ = masked_softmax(s, ok[:, :, None, :])
        return jnp.einsum('bqhk,bqkd->bqhd', p.astype(vg.dtype), vg)

    return from_chunks(lax.map(chunk, (to_chunks(q), to_chunks(qi), to_chunks(wi), q_positions(L))))

def dilated_mixer(q, k, v, cos, sin):
    B, L, _, D = q.shape
    G, Hg = len(DIL_PAIRS), DIL_HEADS_PER_GROUP
    q = apply_rope(q, cos, sin).reshape(B, L, G, Hg, D)
    k = apply_rope(k, cos, sin).reshape(B, L, G, Hg, D)
    v = v.reshape(B, L, G, Hg, D)
    offs = jnp.asarray(np.stack([np.arange(DIL_KEYS) * r for _, r in DIL_PAIRS]))
    gsel = jnp.arange(G)[None, :, None]

    def chunk(args):
        qc, tc = args
        kpos = tc[:, None, None] - offs[None]
        ok = kpos >= 0
        kidx = jnp.maximum(kpos, 0)
        kg, vg = k[:, kidx, gsel], v[:, kidx, gsel]
        s = jnp.einsum('bqghd,bqgkhd->bqghk', qc, kg).astype(jnp.float32) * SCALE
        p, lse = masked_softmax(s, ok[None, :, :, None, :])
        o = jnp.einsum('bqghk,bqgkhd->bqghd', p.astype(vg.dtype), vg)
        return o, lse[..., 0]

    o, lse = lax.map(chunk, (to_chunks(q), q_positions(L)))
    o, lse = from_chunks(o), from_chunks(lse)
    alpha = jax.nn.softmax(lse, axis=2)
    return (alpha[..., None].astype(o.dtype) * o).reshape(B, L, G * Hg, D)

def hybrid_mixer(h, w_in, cmp_pos, cmp_w1, cmp_w2, cos_h, sin_h, cos_i, sin_i):
    B, L, _ = h.shape
    (a_q, a_kc, a_vc, a_ks, a_vs, a_kw, a_vw, a_g,
     b_q, b_k, b_v, b_iq, b_ik, b_iw,
     c_q, c_k, c_v) = jnp.split(h @ w_in, IN_OFFSETS, axis=-1)
    heads = lambda a, n: a.reshape(B, L, n, -1)
    o_a = nsa_mixer(heads(a_q, NSA_HEADS), a_kc, a_vc, a_ks, a_vs, a_kw, a_vw, heads(a_g, NSA_HEADS),
                    cmp_pos, cmp_w1, cmp_w2, cos_h, sin_h)
    o_b = dsa_mixer(heads(b_q, DSA_HEADS), b_k, b_v, heads(b_iq, IDX_HEADS), b_ik, b_iw,
                    cos_h, sin_h, cos_i, sin_i)
    o_c = dilated_mixer(heads(c_q, DIL_HEADS), heads(c_k, DIL_HEADS), heads(c_v, DIL_HEADS), cos_h, sin_h)
    return jnp.concatenate([o_a.reshape(B, L, -1), o_b.reshape(B, L, -1), o_c.reshape(B, L, -1)], axis=-1)

def conv_glu_ffn(h, w_up, conv_w, conv_b, w_down):
    a, u = jnp.split(h @ w_up, 2, axis=-1)
    a = lax.conv_general_dilated(a, conv_w[:, None, :], window_strides=(1,),
                                 padding=((CONV_WIDTH - 1, 0),),
                                 dimension_numbers=('NWC', 'WIO', 'NWC'),
                                 feature_group_count=D_FF) + conv_b
    return (jax.nn.silu(a) * u) @ w_down

def first_inputs(seed: int = 0) -> dict:
    key = jax.random.key(seed)
    ks = jax.random.split(key, 13)
    nrm = lambda k, shape, scale: jax.random.normal(k, shape, jnp.float32) * scale
    return {
        'x': nrm(ks[0], (BATCH, SEQ, D_MODEL), 1.0),
        'norm1_g': 1.0 + nrm(ks[1], (DEPTH, D_MODEL), 0.01),
        'w_in': nrm(ks[2], (DEPTH, D_MODEL, D_IN), D_MODEL ** -0.5),
        'cmp_pos': nrm(ks[3], (DEPTH, 2, CMP_BLOCK, HEAD_DIM), 0.02),
        'cmp_w1': nrm(ks[4], (DEPTH, 2, CMP_BLOCK * HEAD_DIM, CMP_HIDDEN), (CMP_BLOCK * HEAD_DIM) ** -0.5),
        'cmp_w2': nrm(ks[5], (DEPTH, 2, CMP_HIDDEN, HEAD_DIM), CMP_HIDDEN ** -0.5),
        'w_out': nrm(ks[6], (DEPTH, D_MIX, D_MODEL), D_MIX ** -0.5),
        'norm2_g': 1.0 + nrm(ks[7], (DEPTH, D_MODEL), 0.01),
        'w_up': nrm(ks[8], (DEPTH, D_MODEL, 2 * D_FF), D_MODEL ** -0.5),
        'conv_w': nrm(ks[9], (DEPTH, CONV_WIDTH, D_FF), CONV_WIDTH ** -0.5),
        'conv_b': nrm(ks[10], (DEPTH, D_FF), 0.01),
        'w_down': nrm(ks[11], (DEPTH, D_FF, D_MODEL), D_FF ** -0.5),
        'final_g': 1.0 + nrm(ks[12], (D_MODEL,), 0.01),
    }

def first_block(x, norm1_g, w_in, cmp_pos, cmp_w1, cmp_w2, w_out, norm2_g, w_up, conv_w, conv_b, w_down, final_g):
    L = x.shape[1]
    cos_h, sin_h = rope_tables(L, ROPE_DIM, x.dtype)
    cos_i, sin_i = rope_tables(L, IDX_ROPE_DIM, x.dtype)
    for i in range(DEPTH):
        h = rmsnorm(x, norm1_g[i])
        mix = hybrid_mixer(h, w_in[i], cmp_pos[i], cmp_w1[i], cmp_w2[i], cos_h, sin_h, cos_i, sin_i)
        x = x + mix @ w_out[i]
        h = rmsnorm(x, norm2_g[i])
        x = x + conv_glu_ffn(h, w_up[i], conv_w[i], conv_b[i], w_down[i])
    return rmsnorm(x, final_g)


H_GDN = (3 * D_MODEL) // (8 * HEAD_DIM)
H_MOBA = D_MODEL // (4 * HEAD_DIM)
H_MLSTM = D_MODEL // HEAD_DIM - H_GDN - H_MOBA
W_GDN = H_GDN * HEAD_DIM
W_MOBA = H_MOBA * HEAD_DIM
W_MLSTM = H_MLSTM * HEAD_DIM
MIX_WIDTH = W_GDN + W_MOBA + W_MLSTM
CONV_WIDTH_2 = 4
GDN_CHUNK = 64
MLSTM_CHUNK = 64
MOBA_BLOCK = 256
MOBA_TOPK = 3
MOBA_Q_BLOCK = 128
N_SUB = 3
ALPHA = (2 * DEPTH) ** 0.25
BETA_INIT = (8 * DEPTH) ** -0.25
ADA_INIT = 0.1
LN_EPS = 1e-5

IN_SIZES = [3 * W_GDN, H_GDN, H_GDN, W_GDN,
            3 * W_MOBA,
            2 * W_MLSTM, W_MLSTM, H_MLSTM, H_MLSTM, W_MLSTM]
IN_SPLITS_2 = [int(s) for s in np.cumsum(IN_SIZES)[:-1]]
D_IN_2 = int(sum(IN_SIZES))


def layer_norm(x, g, b):
    xf = x.astype(jnp.float32)
    mu = jnp.mean(xf, -1, keepdims=True)
    var = jnp.mean(jnp.square(xf - mu), -1, keepdims=True)
    return ((xf - mu) * lax.rsqrt(var + LN_EPS) * g + b).astype(x.dtype)

def modulate(x, shift, scale):
    return x * (1 + scale[:, None, :]) + shift[:, None, :]

def swiglu(h, w13, w2):
    a, b = jnp.split(h @ w13, 2, axis=-1)
    return (jax.nn.silu(a) * b) @ w2

def causal_conv_silu(x, w):
    y = lax.conv_general_dilated(x, w[:, None, :], window_strides=(1,), padding=[(CONV_WIDTH_2 - 1, 0)],
                                 dimension_numbers=('NWC', 'WIO', 'NWC'), feature_group_count=x.shape[-1])
    return jax.nn.silu(y)

def split_heads(t):
    b_, t_, w = t.shape
    return t.reshape(b_, t_, w // HEAD_DIM, HEAD_DIM).transpose(0, 2, 1, 3)

def l2norm(x):
    return x * lax.rsqrt(jnp.sum(x * x, -1, keepdims=True) + NORM_EPS)

def to_chunks_2(a, size):
    b_, h_, t_ = a.shape[:3]
    return jnp.moveaxis(a.reshape(b_, h_, t_ // size, size, *a.shape[3:]), 2, 0)

def from_chunks_2(a):
    n, b_, h_, l, d = a.shape
    return jnp.moveaxis(a, 0, 2).reshape(b_, h_, n * l, d)

def gated_delta_rule(q, k, v, g, beta):
    b_, h_, t_, dk = q.shape
    dv = v.shape[-1]
    L = GDN_CHUNK
    q = to_chunks_2(q * dk ** -0.5, L); k = to_chunks_2(k, L); v = to_chunks_2(v, L)
    g = to_chunks_2(g, L); beta = to_chunks_2(beta, L)
    G = jnp.cumsum(g, axis=-1)
    incl = jnp.tril(jnp.ones((L, L), dtype=bool))
    strict = jnp.tril(jnp.ones((L, L), dtype=bool), -1)
    decay = jnp.exp(jnp.where(incl, G[..., :, None] - G[..., None, :], -jnp.inf))
    kb = k * beta[..., None]
    A = jnp.where(strict, jnp.einsum('nbhid,nbhjd->nbhij', kb, k) * decay, 0.0)
    M = A + jnp.eye(L, dtype=A.dtype)
    u = lax.linalg.triangular_solve(M, v * beta[..., None], left_side=True, lower=True, unit_diagonal=True)
    w = lax.linalg.triangular_solve(M, kb * jnp.exp(G)[..., None], left_side=True, lower=True, unit_diagonal=True)
    attn = jnp.einsum('nbhid,nbhjd->nbhij', q, k) * decay
    q_dec = q * jnp.exp(G)[..., None]
    k_dec = k * jnp.exp(G[..., -1:] - G)[..., None]
    g_last = jnp.exp(G[..., -1])

    def step(S, inp):
        q_i, w_i, u_i, k_i, a_i, gl_i = inp
        v_new = u_i - jnp.einsum('bhld,bhde->bhle', w_i, S)
        o = jnp.einsum('bhld,bhde->bhle', q_i, S) + jnp.einsum('bhls,bhse->bhle', a_i, v_new)
        S = S * gl_i[..., None, None] + jnp.einsum('bhld,bhle->bhde', k_i, v_new)
        return S, o

    S0 = jnp.zeros((b_, h_, dk, dv), q.dtype)
    _, o = lax.scan(step, S0, (q_dec, w, u, k_dec, attn, g_last))
    return from_chunks_2(o)

def moba_attention(q, k, v):
    b_, h_, t_, d = q.shape
    n_blk = -(-t_ // MOBA_BLOCK)
    top_k = min(MOBA_TOPK, n_blk)
    pad = n_blk * MOBA_BLOCK - t_
    kp = jnp.pad(k, ((0, 0), (0, 0), (0, pad), (0, 0)))
    vp = jnp.pad(v, ((0, 0), (0, 0), (0, pad), (0, 0)))
    k_blk = kp.reshape(b_, h_, n_blk, MOBA_BLOCK, d)
    v_blk = vp.reshape(b_, h_, n_blk, MOBA_BLOCK, d)
    k_mean = jnp.mean(k_blk, axis=3)
    scale = d ** -0.5
    bi = jnp.arange(b_)[:, None, None, None]
    hi = jnp.arange(h_)[None, :, None, None]
    blk_ids = jnp.arange(n_blk)
    n_sel = top_k * MOBA_BLOCK

    def one_block(qb):
        q0 = qb * MOBA_Q_BLOCK
        own = q0 // MOBA_BLOCK
        qc = lax.dynamic_slice_in_dim(q, q0, MOBA_Q_BLOCK, axis=2)
        gate = jnp.einsum('bhqd,bhnd->bhqn', qc, k_mean)
        gate = jnp.where(blk_ids < own, gate, -jnp.inf)
        _, sel = lax.top_k(gate, top_k)
        sel_ok = jnp.repeat(jnp.arange(top_k) < own, MOBA_BLOCK)
        k_sel = k_blk[bi, hi, sel].reshape(b_, h_, MOBA_Q_BLOCK, n_sel, d)
        v_sel = v_blk[bi, hi, sel].reshape(b_, h_, MOBA_Q_BLOCK, n_sel, d)
        s_sel = jnp.where(sel_ok, jnp.einsum('bhqd,bhqkd->bhqk', qc, k_sel) * scale, -jnp.inf)
        k_own = lax.dynamic_slice_in_dim(kp, own * MOBA_BLOCK, MOBA_BLOCK, axis=2)
        v_own = lax.dynamic_slice_in_dim(vp, own * MOBA_BLOCK, MOBA_BLOCK, axis=2)
        q_pos = q0 + jnp.arange(MOBA_Q_BLOCK)
        k_pos = own * MOBA_BLOCK + jnp.arange(MOBA_BLOCK)
        s_own = jnp.where(k_pos[None, :] <= q_pos[:, None],
                          jnp.einsum('bhqd,bhkd->bhqk', qc, k_own) * scale, -jnp.inf)
        p = jax.nn.softmax(jnp.concatenate([s_sel, s_own], -1).astype(jnp.float32), axis=-1).astype(q.dtype)
        return (jnp.einsum('bhqk,bhqkd->bhqd', p[..., :n_sel], v_sel)
                + jnp.einsum('bhqk,bhkd->bhqd', p[..., n_sel:], v_own))

    out = lax.map(one_block, jnp.arange(t_ // MOBA_Q_BLOCK))
    return from_chunks_2(out)

def mlstm_chunkwise(q, k, v, i_pre, logf):
    b_, h_, t_, d = q.shape
    L = MLSTM_CHUNK
    q = to_chunks_2(q, L); k = to_chunks_2(k * d ** -0.5, L); v = to_chunks_2(v, L)
    i_pre = to_chunks_2(i_pre, L); logf = to_chunks_2(logf, L)
    bcum = jnp.cumsum(logf, axis=-1)
    incl = jnp.tril(jnp.ones((L, L), dtype=bool))
    D = jnp.where(incl, bcum[..., :, None] - bcum[..., None, :] + i_pre[..., None, :], -jnp.inf)
    D_max = jnp.max(D, axis=-1)
    w_end = bcum[..., -1:] - bcum + i_pre
    qk = jnp.einsum('nbhtd,nbhsd->nbhts', q, k)

    def step(carry, inp):
        C, n, m = carry
        q_i, k_i, v_i, b_i, D_i, Dm_i, qk_i, we_i = inp
        inter = b_i + m[..., None]
        m_t = jnp.maximum(inter, Dm_i)
        a_inter = jnp.exp(inter - m_t)
        P = qk_i * jnp.exp(D_i - m_t[..., None])
        num = a_inter[..., None] * jnp.einsum('bhld,bhde->bhle', q_i, C) + jnp.einsum('bhls,bhse->bhle', P, v_i)
        den = a_inter * jnp.einsum('bhld,bhd->bhl', q_i, n) + jnp.sum(P, -1)
        h = num / jnp.maximum(jnp.abs(den), jnp.exp(-m_t))[..., None]
        inter_end = b_i[..., -1] + m
        m_new = jnp.maximum(inter_end, jnp.max(we_i, -1))
        s = jnp.exp(we_i - m_new[..., None])
        decay = jnp.exp(inter_end - m_new)
        C = decay[..., None, None] * C + jnp.einsum('bhl,bhld,bhle->bhde', s, k_i, v_i)
        n = decay[..., None] * n + jnp.einsum('bhl,bhld->bhd', s, k_i)
        return (C, n, m_new), h

    init = (jnp.zeros((b_, h_, d, d), q.dtype), jnp.zeros((b_, h_, d), q.dtype), jnp.zeros((b_, h_), q.dtype))
    _, h = lax.scan(step, init, (q, k, v, bcum, D, D_max, qk, w_end))
    return from_chunks_2(h)

def token_mixer(h, w_in, w_out, gdn_conv, gdn_a_log, gdn_dt_bias, gdn_norm,
                mlstm_conv, mlstm_i_bias, mlstm_f_bias, mlstm_norm):
    b_, t_, _ = h.shape
    dt = h.dtype
    f32 = jnp.float32
    qkv_a, a_a, b_a, z_a, qkv_b, qk_c, v_c, i_c, f_c, o_c = jnp.split(h @ w_in, IN_SPLITS_2, axis=-1)
    qa, ka, va = jnp.split(causal_conv_silu(qkv_a, gdn_conv), 3, axis=-1)
    qa = l2norm(split_heads(qa).astype(f32))
    ka = l2norm(split_heads(ka).astype(f32))
    va = split_heads(va).astype(f32)
    g = -jnp.exp(gdn_a_log.astype(f32)) * jax.nn.softplus((a_a + gdn_dt_bias).astype(f32))
    beta = jax.nn.sigmoid(b_a.astype(f32))
    oa = gated_delta_rule(qa, ka, va, g.transpose(0, 2, 1), beta.transpose(0, 2, 1)).transpose(0, 2, 1, 3)
    oa = oa * lax.rsqrt(jnp.mean(oa * oa, -1, keepdims=True) + NORM_EPS) * gdn_norm
    oa = (oa.reshape(b_, t_, W_GDN) * jax.nn.silu(z_a.astype(f32))).astype(dt)
    qb, kb, vb = jnp.split(qkv_b, 3, axis=-1)
    ob = moba_attention(split_heads(qb), split_heads(kb), split_heads(vb))
    ob = ob.transpose(0, 2, 1, 3).reshape(b_, t_, W_MOBA).astype(dt)
    qc, kc = jnp.split(causal_conv_silu(qk_c, mlstm_conv), 2, axis=-1)
    i_pre = (i_c + mlstm_i_bias).astype(f32).transpose(0, 2, 1)
    logf = jax.nn.log_sigmoid((f_c + mlstm_f_bias).astype(f32)).transpose(0, 2, 1)
    hc = mlstm_chunkwise(split_heads(qc).astype(f32), split_heads(kc).astype(f32),
                         split_heads(v_c).astype(f32), i_pre, logf).transpose(0, 2, 1, 3)
    hc = hc * jax.nn.sigmoid(o_c.astype(f32)).reshape(b_, t_, H_MLSTM, HEAD_DIM)
    mu = jnp.mean(hc, -1, keepdims=True)
    var = jnp.mean(jnp.square(hc - mu), -1, keepdims=True)
    hc = (hc - mu) * lax.rsqrt(var + NORM_EPS) * mlstm_norm.reshape(H_MLSTM, HEAD_DIM)
    hc = hc.reshape(b_, t_, W_MLSTM).astype(dt)
    return jnp.concatenate([oa, ob, hc], axis=-1) @ w_out

def second_inputs(seed: int = 0) -> dict:
    key = jax.random.key(seed)
    ks = jax.random.split(key, 18)
    nrm = lambda k, shape, s: jax.random.normal(k, shape, jnp.float32) * s
    dt_init = jnp.exp(jax.random.uniform(ks[10], (DEPTH, H_GDN), jnp.float32,
                                         float(np.log(1e-3)), float(np.log(1e-1))))
    return {
        "x": nrm(ks[0], (BATCH, SEQ, D_MODEL), 1.0),
        "c": nrm(ks[1], (BATCH, D_MODEL), 1.0),
        "ada_w": nrm(ks[2], (DEPTH, D_MODEL, N_SUB * 3 * D_MODEL), ADA_INIT * D_MODEL ** -0.5),
        "ada_b": nrm(ks[3], (DEPTH, N_SUB * 3 * D_MODEL), 0.01),
        "ffn_w13": nrm(ks[4], (DEPTH, 2, D_MODEL, 2 * D_FF), D_MODEL ** -0.5),
        "ffn_w2": nrm(ks[5], (DEPTH, 2, D_FF, D_MODEL), BETA_INIT * D_FF ** -0.5),
        "w_in": nrm(ks[6], (DEPTH, D_MODEL, D_IN_2), D_MODEL ** -0.5),
        "w_out": nrm(ks[7], (DEPTH, MIX_WIDTH, D_MODEL), BETA_INIT * MIX_WIDTH ** -0.5),
        "gdn_conv": nrm(ks[8], (DEPTH, CONV_WIDTH_2, 3 * W_GDN), CONV_WIDTH_2 ** -0.5),
        "gdn_a_log": jnp.log(jax.random.uniform(ks[9], (DEPTH, H_GDN), jnp.float32, 1.0, 16.0)),
        "gdn_dt_bias": dt_init + jnp.log(-jnp.expm1(-dt_init)),
        "gdn_norm": 1.0 + nrm(ks[11], (DEPTH, HEAD_DIM), 0.02),
        "mlstm_conv": nrm(ks[12], (DEPTH, CONV_WIDTH_2, 2 * W_MLSTM), CONV_WIDTH_2 ** -0.5),
        "mlstm_i_bias": nrm(ks[13], (DEPTH, H_MLSTM), 0.1),
        "mlstm_f_bias": jnp.linspace(3.0, 6.0, H_MLSTM, dtype=jnp.float32)[None, :] + nrm(ks[14], (DEPTH, H_MLSTM), 0.1),
        "mlstm_norm": 1.0 + nrm(ks[15], (DEPTH, W_MLSTM), 0.02),
        "ln_g": 1.0 + nrm(ks[16], (DEPTH, N_SUB, D_MODEL), 0.02),
        "ln_b": nrm(ks[17], (DEPTH, N_SUB, D_MODEL), 0.02),
    }

def second_block(x, c, ada_w, ada_b, ffn_w13, ffn_w2, w_in, w_out, gdn_conv, gdn_a_log, gdn_dt_bias,
              gdn_norm, mlstm_conv, mlstm_i_bias, mlstm_f_bias, mlstm_norm, ln_g, ln_b):
    b_ = x.shape[0]
    for l in range(DEPTH):
        mod = (jax.nn.silu(c) @ ada_w[l] + ada_b[l]).reshape(b_, N_SUB, 3, D_MODEL)
        y = swiglu(modulate(x, mod[:, 0, 0], mod[:, 0, 1]), ffn_w13[l, 0], ffn_w2[l, 0])
        x = layer_norm(ALPHA * x + 0.5 * (1 + mod[:, 0, 2])[:, None, :] * y, ln_g[l, 0], ln_b[l, 0])
        y = token_mixer(modulate(x, mod[:, 1, 0], mod[:, 1, 1]), w_in[l], w_out[l], gdn_conv[l], gdn_a_log[l],
                        gdn_dt_bias[l], gdn_norm[l], mlstm_conv[l], mlstm_i_bias[l], mlstm_f_bias[l], mlstm_norm[l])
        x = layer_norm(ALPHA * x + (1 + mod[:, 1, 2])[:, None, :] * y, ln_g[l, 1], ln_b[l, 1])
        y = swiglu(modulate(x, mod[:, 2, 0], mod[:, 2, 1]), ffn_w13[l, 1], ffn_w2[l, 1])
        x = layer_norm(ALPHA * x + 0.5 * (1 + mod[:, 2, 2])[:, None, :] * y, ln_g[l, 2], ln_b[l, 2])
    return x


def setup_inputs(seed=0):
    out = dict(first_inputs(seed))
    for name, value in second_inputs(seed + 1).items():
        if name != "x":
            out[name + "_2"] = value
    return out


def reference(
    x, norm1_g, w_in, cmp_pos, cmp_w1, cmp_w2, w_out, norm2_g, w_up, conv_w, conv_b, w_down,
    final_g, c_2, ada_w_2, ada_b_2, ffn_w13_2, ffn_w2_2, w_in_2, w_out_2, gdn_conv_2,
    gdn_a_log_2, gdn_dt_bias_2, gdn_norm_2, mlstm_conv_2, mlstm_i_bias_2, mlstm_f_bias_2,
    mlstm_norm_2, ln_g_2, ln_b_2,
):
    x = first_block(
        x, norm1_g, w_in, cmp_pos, cmp_w1, cmp_w2, w_out, norm2_g, w_up, conv_w, conv_b, w_down,
        final_g,
    )
    return second_block(
        x, c_2, ada_w_2, ada_b_2, ffn_w13_2, ffn_w2_2, w_in_2, w_out_2, gdn_conv_2, gdn_a_log_2,
        gdn_dt_bias_2, gdn_norm_2, mlstm_conv_2, mlstm_i_bias_2, mlstm_f_bias_2, mlstm_norm_2,
        ln_g_2, ln_b_2,
    )


_drawn_inputs = setup_inputs


def setup_inputs(seed=0):
    import zlib

    import numpy as np

    out = dict(_drawn_inputs(seed))
    spreads = {}
    factors = {'cmp_pos': 6.229,
     'norm2_g': 3.509,
     'conv_b': 4.936,
     'final_g': 5.023,
     'ada_b_2': 3.641,
     'gdn_norm_2': 26.247,
     'mlstm_i_bias_2': 64.0,
     'mlstm_norm_2': 8.0}
    for name, (base, spread) in spreads.items():
        noise = np.random.default_rng([zlib.crc32(name.encode()), seed]).standard_normal(out[name].shape)
        drawn = base * np.exp(spread * noise) if base else spread * noise
        out[name] = __import__('jax').numpy.asarray(drawn.astype(out[name].dtype))
    for name, factor in factors.items():
        out[name] = (out[name] * factor).astype(out[name].dtype)
    return out
```

```python
from contextlib import ExitStack

import numpy as np

import concourse.bass as bass
from concourse import mybir

F32 = mybir.dt.float32
F32R = mybir.dt.float32r
ACT = mybir.ActivationFunctionType
ALU = mybir.AluOpType
AX = mybir.AxisListType

P = 128
SEQ, DM, DEPTH = 256, 1024, 2
TT = SEQ // P
KT = DM // P
HD = 64
SCALE = HD ** -0.5
NEG = -1e30
DFF = 2816
FT = DFF // P
NORM_EPS, LN_EPS = 1e-6, 1e-5
ALPHA = (2 * DEPTH) ** 0.25
CW = 2048
RING = 3
CAUS = P + SEQ

NSA_H, DSA_H, DIL_H, IDX_H, IDX_D = 5, 5, 6, 8, 32
SRC = {}
_o = 0
for _n, _w in (("aq", 320), ("kc", 64), ("vc", 64), ("ks", 64), ("vs", 64), ("kw", 64), ("vw", 64), ("ag", 15),
               ("bq", 320), ("bk", 64), ("bv", 64), ("iq", 256), ("ik", 32), ("iw", 8),
               ("cq", 384), ("ck", 384), ("cv", 384)):
    SRC[_n] = (_o, _w)
    _o += _w
D_IN = _o
COL = {}
_o = 0
for _n in ("aq", "ks", "kw", "bq", "bk", "cq", "ck", "iq", "ik", "kc", "vc", "vs", "vw", "bv", "cv", "ag", "iw"):
    COL[_n] = _o
    _o += SRC[_n][1]
ROT_H = 25
ROT_I = IDX_H + 1
GW = 256
PJW = D_IN + D_IN % 2
WIN_A = [min(GW, PJW - c) for c in range(0, PJW, GW)]
NCMP, CBLK, CSTR = 15, 32, 16
TOPK = SEQ // 4

A_WIN, A_CMP, A_ADA, A_WOUT, FFN_N = len(WIN_A), 3, 36, 4, 33
A_N0 = {"win": 0, "cmp": A_WIN, "ada": A_WIN + A_CMP, "wout": A_WIN + A_CMP + A_ADA}
A_N0["ffn"] = A_N0["wout"] + A_WOUT
A_N = A_N0["ffn"] + FFN_N
A_S = A_WIN + A_WOUT + FFN_N
A_D = A_CMP + A_ADA
assert A_N % RING == 0 and A_S % RING == 0 and A_N0["ffn"] % RING == 0 and (A_WIN + A_WOUT) % RING == 0

TB = [("aq", 0, 128, 1), ("aq", 128, 128, 1), ("aq", 256, 128, 1), ("kc", 0, 128, 1),
      ("iq", 0, 128, 1), ("iq", 128, 128, 1), ("ik", 0, 32, 4), ("bk", 0, 64, 2),
      ("bq", 0, 128, 1), ("bq", 128, 128, 1), ("bq", 256, 128, 1), ("ks", 0, 64, 2), ("kw", 0, 64, 2),
      ("aq", 0, 128, 1), ("aq", 128, 128, 1), ("aq", 256, 128, 1),
      ("cq", 0, 128, 1), ("cq", 128, 128, 1), ("cq", 256, 128, 1),
      ("ck", 0, 128, 1), ("ck", 128, 128, 1), ("ck", 256, 128, 1)]
T_AQR, T_KCVC, T_IQ, T_IK, T_BK, T_BQ, T_KS, T_KW, T_AQ, T_CQ, T_CK = 0, 3, 4, 6, 7, 8, 11, 12, 13, 16, 19

CST = {}


def _constants():
    parts, at = [], 0

    def put(name, a):
        nonlocal at
        a = np.asarray(a, np.float32).reshape(a.shape[0], -1)
        if a.shape[0] < P:
            a = np.concatenate([a, np.zeros((P - a.shape[0], a.shape[1]), np.float32)])
        CST[name] = (at, a.shape[1])
        parts.append(a)
        at += a.shape[1]

    i, j = np.arange(P)[:, None], np.arange(P)[None, :]
    put("ident", np.eye(P))
    put("ones", np.ones((P, P)))
    put("upto", (i <= j).astype(np.float32))
    add = lambda ok: np.where(ok, 0.0, NEG)
    full = np.ones((P, P), bool)
    put("causal", np.concatenate([add(j <= i), add(full), add(j <= i)], 1))
    put("causalT", np.concatenate([add(i <= j), add(full), add(i <= j)], 1))
    put("dil0", np.concatenate([add(j <= i), add(j >= i), add(j <= i)], 1))
    for g, r in ((1, 4), (2, 16)):
        step = (i - j) % r == 0
        put(f"dil{g}", np.concatenate([add((j <= i) & step), add(step), add((j <= i) & step)], 1))
    t = np.arange(SEQ).reshape(TT, P).T[:, :, None]
    ok = (np.arange(NCMP) * CSTR + CBLK - 1)[None, None, :] <= t
    put("cmp_add", add(ok))
    put("cmp_keep", ok.astype(np.float32))
    for name, rot in (("h", 16), ("i", 8)):
        inv = 1.0 / (500000.0 ** (np.arange(0, rot, 2, dtype=np.float32) / np.float32(rot)))
        ang = np.arange(SEQ, dtype=np.float32)[:, None] * inv[None, :].astype(np.float32)
        for f, fn in (("cos", np.cos), ("sin", np.sin)):
            put(f + name, fn(ang).astype(np.float32).reshape(TT, P, rot // 2).transpose(1, 0, 2))
    for b in range(7):
        s = 1 << b
        put(f"lev{b}", ((i // (2 * s) == j // (2 * s)) & (j % (2 * s) >= s) & (i % (2 * s) < s)).astype(np.float32))
    pair = np.zeros((6, 3, P), np.float32)
    for h in range(6):
        pair[h, h // 2, 64 * (h % 2):64 * (h % 2) + 64] = 1
    put("pair", pair)
    pair12 = np.zeros((12, 6, P), np.float32)
    for h in range(12):
        pair12[h, h // 2, 64 * (h % 2):64 * (h % 2) + 64] = 1
    put("pair12", pair12)
    half = np.zeros((P, 6, 12), np.float32)
    for f in range(6):
        half[:64, f, 2 * f] = 1
        half[64:, f, 2 * f + 1] = 1
    put("half", half)
    return np.ascontiguousarray(np.concatenate(parts, 1))


CONST = _constants()


def a_chunk(n):
    if n < A_N0["cmp"]:
        return "split", n
    if n < A_N0["wout"]:
        return "direct", n - A_N0["cmp"]
    return "split", n - A_D


def a_width(n):
    if n < A_WIN:
        return KT * WIN_A[n]
    return {A_N0["cmp"] + 1: CW // 2, A_N0["cmp"] + 2: CW // 2}.get(n, CW)


def _columns(*names):
    at, out = 0, {}
    for n, w in names:
        out[n] = (at, w)
        at += w
    return out, at


SA, SA_W = _columns(("g1", KT), ("g2", KT), ("conv", FT * 4), ("pos", CBLK), ("w2k", P), ("w2v", HD), ("ada_b", 72))


GDN_H, MOBA_H, ML_H = 6, 4, 6
TAPS = 4
F_GQ, F_GK, F_GV, F_LQ, F_LK, F_MQ, F_MK, F_N = 0, 3, 6, 9, 12, 15, 17, 19
F_CONV = list(range(F_MQ))
ZC, VB, VC, OC, GT = 0, 384, 640, 1024, 1408
TMW = GT + 24
B_WIN = ([((f, f + 1), 0, 0) for f in (0, 2, 4, 6, 8, 10, 12, 15, 17)] + [((14,), 0, P), ((), GT, 24), ((), P, GW), ((), VB, GW),
         ((), VC, GW), ((), VC + GW, GW), ((), OC + P, P), ((), OC + GW, P)])
B_WOUT = 4
B_S0 = {"ffn0": 0, "win": FFN_N, "wout": FFN_N + len(B_WIN)}
B_S0["ffn1"] = B_S0["wout"] + B_WOUT
B_N = B_S0["ffn1"] + FFN_N
assert B_N % RING == 0 and B_S0["ffn1"] % RING == 0
SB, SB_W = _columns(("conv", 15 * TAPS), ("gate_bias", 24), ("a_log", GDN_H), ("gdn_norm", HD), ("ml_norm", ML_H * HD))


def b_width(n):
    if B_S0["win"] <= n < B_S0["wout"]:
        f, _, w = B_WIN[n - B_S0["win"]]
        return KT * (P * len(f) + w)
    return CW


def build(nc, t, only_first=False):
    with ExitStack() as ctx:
        def sb(name, shape, dt=F32):
            return ctx.enter_context(nc.sbuf_tensor(name, shape, dt))

        def sem(name):
            return ctx.enter_context(nc.semaphore(name))

        raw = sb("raw", [P, RING, CW])
        w_hi = sb("w_hi", [P, RING, CW], F32R)
        w_lo = sb("w_lo", [P, RING, CW], F32R)
        x = sb("x", [P, TT, DM])
        hT_hi = sb("hT_hi", [P, KT, SEQ], F32R)
        hT_lo = sb("hT_lo", [P, KT, SEQ], F32R)
        hid_hi = sb("hid_hi", [P, 4, SEQ], F32R)
        hid_lo = sb("hid_lo", [P, 4, SEQ], F32R)
        cst = sb("cst", [P, CONST.shape[1]])
        spa = sb("spa", [P, max(SA_W, SB_W)])
        cvec = sb("cvec", [P, 2, KT])
        mod = sb("mod", [P, DEPTH, 72])
        modl = sb("modl", [P, 72])
        gateb = sb("gateb", [P, DM])
        lnw = sb("lnw", [P, 2, DM])
        st = sb("st", [P, 32])
        SCR = 18000
        scratch = sb("scratch", [P, SCR])

        def carver():
            at = 0

            def carve(*dims):
                nonlocal at
                n = int(np.prod(dims))
                v = scratch[:, at:at + n]
                at += n
                assert at <= SCR, at
                if len(dims) == 1:
                    return v
                names = "abcd"[:len(dims)]
                return v.rearrange(f"p ({' '.join(names)}) -> p {' '.join(names)}", **dict(zip(names, dims)))
            return carve

        carve = carver()
        xn, junk = carve(TT, DM), carve(TT, DM)
        carve = carver()
        cv, sg, h32 = carve(2, SEQ), carve(2, SEQ), carve(2, SEQ)
        carve = carver()
        pj, tb = carve(TT, PJW), carve(len(TB), SEQ)
        lg, pr, pt = carve(2, CAUS), carve(2, CAUS), carve(2, CAUS)
        mix = carve(TT, DM)
        relu, isc, dmask = carve(2, CAUS), carve(CAUS), carve(CAUS)
        iws, ags, fac = carve(TT, IDX_H), carve(TT, 15), carve(2, TT)
        den, nmax, rden = carve(21, TT), carve(21, TT), carve(2, TT)
        m8, dmin, dexp, dfac = carve(2, 8), carve(2, TT), carve(6, TT), carve(6, TT)
        lc, mc, dc, pc = carve(TT, NSA_H, 16), carve(TT, NSA_H), carve(TT, NSA_H), carve(TT, NSA_H, 32)
        vr, vc4, kcm, hb = carve(4, 32), carve(HD), carve(16), carve(4, 2, 16)
        flat = lambda v: v.rearrange("p a b -> p (a b)")
        rw = flat(lg)[:, 0:CBLK * NCMP].rearrange("p (j n) -> p j n", n=NCMP)
        dup = scratch[:, TT * PJW + len(TB) * SEQ + 2 * CAUS:TT * PJW + len(TB) * SEQ + 2 * CAUS + TT * 4 * P].rearrange("p (t k n) -> p t k n", t=TT, k=4)
        DUP = [k for k, b in enumerate(TB) if b[3] > 1]
        rot = [flat(mix)[:, 512 * k:512 * k + 400] for k in range(4)]
        pcT = flat(pt)[:, 0:SEQ].rearrange("p (t n) -> p t n", t=TT)
        pcT4 = flat(pt)[:, SEQ:2 * SEQ].rearrange("p (t n) -> p t n", t=TT)

        carve = carver()
        gdiag, hx, part = carve(KT, P), carve(2, SEQ), carve(2, 512)
        bst, bag = carve(TT, 2, 6), carve(TT, 2)
        carve = carver()
        fm, tm = carve(F_N, SEQ), carve(TT, TMW)
        mixb = carve(TT, DM)
        lgb, prb, ptb = carve(2, CAUS), carve(2, CAUS), carve(2, CAUS)
        kbT, vb = carve(3, SEQ), carve(TT, GDN_H, HD)
        grow = carve(SEQ)
        xx = carve(2 * GDN_H, 2, P)
        gt, ga, gl1, gl = carve(TT, 24), carve(TT, 12), carve(TT, 12), carve(TT, 12)
        cg, ngr, beta, sig = carve(TT, 12), carve(TT, 12), carve(TT, 6), carve(TT, 6)
        bm, em, ealog, negG = carve(TT, 6), carve(TT, 6), carve(6), carve(TT, 6)
        denb, nmaxb, rdenb = carve(10, TT), carve(10, TT), carve(2, TT)
        hst, hst2, hst3 = carve(TT, 6), carve(TT, 6), carve(TT, 6)
        cvb = xx.rearrange("p a b c -> p (a b c)")[:, 0:1024].rearrange("p (a k n) -> p a k n", a=2, k=2)
        row_b, row_f, row_i, row_m = (flat(mixb)[:, 256 * k:256 * k + 256] for k in range(4))
        norm_r = flat(mixb)[:, 1024:1280]
        sq = scratch[:, F_N * SEQ + TT * TMW + TT * DM:F_N * SEQ + TT * TMW + TT * DM + 6 * SEQ].rearrange("p (f n) -> p f n", f=6)
        attnT = fm.rearrange("p f n -> p (f n)")[:, F_LQ * SEQ:F_LQ * SEQ + GDN_H * CAUS].rearrange("p (h n) -> p h n", h=GDN_H)
        sysT = scratch[:, F_N * SEQ + TT * TMW + TT * DM:F_N * SEQ + TT * TMW + TT * DM + GDN_H * CAUS].rearrange(
            "p (h n) -> p h n", h=GDN_H)
        dec = [tm[:, i, VB:VB + CAUS] for i in range(2)]
        atm = tm[:, 0, VB:VB + 512].rearrange("p (k n) -> p k n", k=4)
        ym = tm[:, 1, VB:VB + 512].rearrange("p (k n) -> p k n", k=4)
        uu = kbT.rearrange("p a b -> p (a b)").rearrange("p (t n) -> p t n", t=TT)
        sq2 = xx.rearrange("p a b c -> p (a b c)")[:, 0:768].rearrange("p (t n) -> p t n", t=TT)
        sq3 = xx.rearrange("p a b c -> p (a b c)")[:, 768:1536].rearrange("p (t n) -> p t n", t=TT)

        ps = [ctx.enter_context(nc.psum_tensor(f"bank{i}", [P, 512], F32)) for i in range(8)]
        S, PT, O, G = ps[0:2], ps[2:4], ps[4:6], ps[6:8]
        ADA, UP, TP, ACC, CO = ps[7], ps[0:2], ps[2:4], ps[4:8], [ps[4], ps[5], ps[0], ps[1]]

        def const(name, parts=P):
            a, w = CST[name]
            return cst[0:parts, a:a + w]

        ident = const("ident")

        def sa(name, i=None):
            a, w = SA[name]
            return spa[:, a:a + w] if i is None else spa[:, a + i:a + i + 1]

        def conv_tap(f, i):
            return spa[:, bass.ds(f * 4 + (SA["conv"][0] + i), 1)]

        def sbp(name, i=None):
            a, w = SB[name]
            return spa[:, a:a + w] if i is None else spa[:, a + i:a + i + 1]

        def modc(sub, which):
            return modl[:, (sub * 3 + which) * KT:(sub * 3 + which + 1) * KT]

        raw_in = [sem(f"raw_in{i}") for i in range(RING)]
        hi_done, lo_done = sem("hi_done"), sem("lo_done")
        chunk_mm = sem("chunk_mm")
        direct_mm = sem("direct_mm")
        NEW = RING
        start_in, small_in, out_st = sem("start_in"), sem("small_in"), sem("out_st")
        ln_in = sem("ln_in")
        layer_done, layer_go = sem("layer_done"), sem("layer_go")
        pre = sem("pre")
        FIN = {n: sem("fin_" + n) for n in ("ss", "std", "rstd", "x")}
        A = {n: sem("a_" + n) for n in (
            "ss", "std", "rstd", "xn", "tp", "tp_hi", "tp_lo", "pj", "blk", "blk_ev", "rope_i", "rope_h", "dup",
            "ix", "ix_relu", "ix_acc", "dmask", "gate", "gate_e", "rw", "cg", "cg_e", "cgel", "ckv", "ckv_ev", "cs", "cnm",
            "cexp", "cp", "cpt", "cpt_ev", "co", "co_ev", "s", "nm", "e", "pt", "pt_ev", "o", "o_ev",
            "dila", "dila_e", "mix", "ada_ev", "dve", "x", "c1", "cv1", "cv2", "sg", "h", "hid_hi", "hid_lo")}

        B = {n: sem("b_" + n) for n in (
            "modl", "gdiag", "gateb", "gateb_ev", "tp", "tp_mod", "tp_hi", "tp_lo", "tap", "conv", "fm", "tm",
            "gt", "ge", "gln", "gl", "cum", "cg", "rows", "rows_ev", "scan", "mback", "bm", "em",
            "sq", "ss", "ssr", "rn", "rnb", "rnb_ev", "bb", "kb", "vt", "vb",
            "s", "s_free", "nm", "e", "p", "pt", "pt_ev", "o", "o_ev",
            "ds", "dl", "dec", "dmul", "xinit", "atm", "y", "y_ev", "z", "xx",
            "u", "u_ev", "w1", "go", "gsq", "gms", "grs", "gout", "lden", "lvar", "lrs", "mix",
            "dve", "act", "std", "ln", "sg", "h", "hid_hi", "hid_lo")}
        B_UNITS = [("moba", h) for h in range(MOBA_H)] + [("mlstm", h) for h in range(ML_H)]
        NUB = len(B_UNITS)
        B_LAGP, B_LAGT, B_LAGO, B_LAGV = 1, 3, 4, 5
        N_A, S_A = DEPTH * A_N // RING, DEPTH * A_S

        def arrivals_b(l, n):
            return l * (16 * B_N // RING) + 16 * (N_A + n // RING + 1)

        UNITS = ([("slc", h) for h in range(NSA_H)] + [("win", h) for h in range(NSA_H)]
                 + [("dil", h) for h in range(DIL_H)] + [("dsa", h) for h in range(DSA_H)])
        NU, U_DIL, U_DSA = len(UNITS), 2 * NSA_H, 2 * NSA_H + DIL_H
        LAG_T, LAG_O, LAG_V = 2, 3, 4

        def unit(u):
            kind, h = UNITS[u]
            if kind == "dil":
                return T_CQ + h // 2, T_CK + h // 2, 64 * (h % 2), COL["cv"] + HD * h, const(f"dil{h // 2}"), 640 + HD * h
            q, k, v, m, o = {"slc": (T_AQ, T_KS, "vs", const("causal"), 0), "win": (T_AQ, T_KW, "vw", const("causal"), 0),
                             "dsa": (T_BQ, T_BK, "bv", dmask, 320)}[kind]
            return q + h // 2, k, 64 * (h % 2), COL[v], m, o + HD * h

        def ada_chunks(step):
            per = -(-A_ADA // (NU + LAG_O))
            return range(min(A_ADA, step * per), min(A_ADA, (step + 1) * per))

        def arrivals(l, n):
            return l * (16 * A_N // RING) + 16 * (n // RING + 1)

        def bank_count(c):
            conv = B_WIN[c][0][0] in F_CONV
            if conv:
                return len([1 for b in B_WIN[:c + 1] if b[0] and b[0][0] in F_CONV])
            return len([1 for b in B_WIN[:c + 1] if b[0]])

        def tap(f, i):
            return sbp("conv", F_CONV.index(f) * TAPS + i)

        def mod_count(v, k):
            return (v if v < 2 else v - 1) * KT + k

        block = ctx.enter_context(nc.Block())

        def load_b(sp, l, j, n0):
            for r in range(RING):
                n = n0 + r
                sp.wait_ge(lo_done, l * B_N + j * RING + (S_A + n - RING + 1 + NEW))
                sp.dma_start(raw[:, n % RING, :],
                             t["wb"][bass.ds(l, 1), bass.ds(j * RING + n, 1), :, :].rearrange("o c p n -> (o c p) n")
                             ).then_inc(raw_in[n % RING], 16)

        @block.sync
        def _(sp):
            sp.dma_start(cst[:, :], t["const"]).then_inc(start_in, 16)
            sp.dma_start(x[:, :, :], t["x"].rearrange("o (t p) d -> p (o t) d", p=P)).then_inc(start_in, 16)
            sp.dma_start(cvec[:, 0, :], t["c"]).then_inc(start_in, 16)
            sp.dma_start(lnw[:, 0, :], t["final_g"].partition_broadcast(P)).then_inc(start_in, 16)
            with sp.Fori(0, DEPTH) as l:
                for n in range(A_N0["ffn"]):
                    kind, i = a_chunk(n - RING)
                    if kind == "split":
                        sp.wait_ge(lo_done, l * A_S + (i + 1 + NEW))
                    else:
                        sp.wait_ge(direct_mm, l * A_D + (i + 1))
                    w = a_width(n)
                    sp.dma_start(raw[:, n % RING, 0:w],
                                 t["wa"][bass.ds(l, 1), n, :, 0:w].rearrange("o p n -> (o p) n")).then_inc(raw_in[n % RING], 16)
                with sp.Fori(0, FFN_N // RING) as j:
                    for r in range(RING):
                        sp.wait_ge(lo_done, l * A_S + j * RING + (A_WIN + A_WOUT + r - RING + 1 + NEW))
                        sp.dma_start(raw[:, r, :],
                                     t["wa"][bass.ds(l, 1), bass.ds(j * RING + (A_N0["ffn"] + r), 1), :, :]
                                     .rearrange("o c p n -> (o c p) n")).then_inc(raw_in[r], 16)
            with sp.Fori(0, DEPTH) as l:
                with sp.Fori(0, FFN_N // RING) as j:
                    load_b(sp, l, j, 0)
                for n in range(B_S0["win"], B_S0["ffn1"]):
                    sp.wait_ge(lo_done, l * B_N + (S_A + n - RING + 1 + NEW))
                    w = b_width(n)
                    sp.dma_start(raw[:, n % RING, 0:w],
                                 t["wb"][bass.ds(l, 1), n, :, 0:w].rearrange("o p n -> (o p) n")).then_inc(raw_in[n % RING], 16)
                with sp.Fori(0, FFN_N // RING) as j:
                    load_b(sp, l, j, B_S0["ffn1"])
            sp.wait_ge(layer_go, 2 * DEPTH)
            sp.dma_start(t["out"].rearrange("o (t p) d -> p (o t) d", p=P), x[:, :, :]).then_inc(out_st, 16)
            sp.wait_ge(out_st, 16)

        def pool_levels(pool):
            for lev in range(7):
                for u in range(2 * GDN_H):
                    n = lev * 2 * GDN_H + u
                    if n == 0:
                        pool.wait_ge(B["dmul"], GDN_H)
                    if n >= 4:
                        pool.wait_ge(B["y"], n - 3)
                    at = 0 if u % 2 == 0 else SEQ
                    nc.gpsimd.tensor_tensor(atm[:, n % 4, :], sysT[:, u // 2, at:at + P], const(f"lev{lev}"),
                                            ALU.mult).then_inc(B["atm"], 1)

        @block.gpsimd
        def _(pool):
            with pool.Fori(0, DEPTH) as l:
                pool.dma_start(spa[:, 0:SA_W], t["sa"][bass.ds(l, 1), :, :].rearrange("o p n -> (o p) n")).then_inc(small_in, 16)
                pool.wait_ge(layer_done, 3)
                pool.sem_clear(layer_done)
                for s_ in A.values():
                    pool.sem_clear(s_)
                pool.sem_inc(layer_go, 1)
            with pool.Fori(0, DEPTH) as l:
                pool.dma_start(spa[:, 0:SB_W], t["sb"][bass.ds(l, 1), :, :].rearrange("o p n -> (o p) n")).then_inc(small_in, 16)
                for sub in range(3):
                    if sub == 0:
                        pool.wait_ge(FIN["x"], TT)
                    else:
                        pool.wait_ge(B["ln"], sub)
                    for k, name in enumerate(("ln_g", "ln_b")):
                        pool.dma_start(lnw[:, k, :], t[name][bass.ds(l, 1), sub, :].rearrange("o n -> (o n)").partition_broadcast(P)
                                       ).then_inc(ln_in, 16)
                    if sub == 1:
                        pool_levels(pool)
                pool.wait_ge(layer_done, 3)
                pool.sem_clear(layer_done)
                for s_ in B.values():
                    pool.sem_clear(s_)
                pool.sem_inc(layer_go, 1)

        @block.tensor
        def _(pe):
            pe.sem_inc(chunk_mm, NEW)
            pe.wait_ge(start_in, 64)
            pe.wait_ge(pre, 1)

            def products(out, pairs):
                n = len(pairs)
                for i, ((ah, al), (bh, bl)) in enumerate(pairs):
                    nc.tensor.matmul(out, ah, bh, start=(i == 0), stop=False)
                    nc.tensor.matmul(out, ah, bl, start=False, stop=False)
                    last = nc.tensor.matmul(out, al, bh, start=False, stop=(i == n - 1))
                return last

            def to_features(N, v, src):
                for k in range(KT):
                    if k >= 2:
                        pe.wait_ge(N["tp_lo"], v * KT + k - 1)
                    for i in range(TT):
                        last = nc.tensor.transpose(TP[k % 2][:, i * P:(i + 1) * P], src[:, i, k * P:(k + 1) * P], ident)
                    last.then_inc(N["tp"], 1)
                pe.wait_ge(N["tp_lo"], v * KT + KT)

            def token_chunk(out, slot, width, first=0):
                stride = first + width
                for i in range(TT):
                    rows = slice(i * P, (i + 1) * P)
                    last = products(out[:, i * width:(i + 1) * width],
                                    [((hT_hi[:, k, rows], hT_lo[:, k, rows]),
                                      (w_hi[:, slot, k * stride + first:(k + 1) * stride],
                                       w_lo[:, slot, k * stride + first:(k + 1) * stride]))
                                     for k in range(KT)])
                return last

            def feature_tile(out, slot, half, stride=2 * P):
                cols = lambda k: slice(k * stride + half * P, k * stride + half * P + P)
                return products(out, [((w_hi[:, slot, cols(k)], w_lo[:, slot, cols(k)]), (hT_hi[:, k, :], hT_lo[:, k, :]))
                                      for k in range(KT)])

            def ffn(N, split, h0):
                def up(f, f2, pos, slot, wait_bank=True):
                    pe.wait_ge(lo_done, pos + (1 + NEW) + split)
                    if wait_bank:
                        pe.wait_ge(N["h"], f + (h0 - 1))
                    feature_tile(UP[f2][:, 0:SEQ], slot, 0)
                    feature_tile(UP[f2][:, SEQ:2 * SEQ], slot, 1).then_inc(chunk_mm, 1)

                def down(f, f4, pos, slot, first=False, last_one=False):
                    pe.wait_ge(lo_done, pos + (1 + NEW) + split)
                    for k2 in range(2):
                        pe.wait_ge(N["hid_lo"], f + (h0 + k2 + 1))
                        for i in range(TT):
                            rows = slice(i * P, (i + 1) * P)
                            for half in range(2):
                                cols = slice(k2 * DM + half * 512, k2 * DM + half * 512 + 512)
                                out = ACC[2 * i + half][:, :]
                                ah, al = hid_hi[:, f4 + k2, rows], hid_lo[:, f4 + k2, rows]
                                bh, bl = w_hi[:, slot, cols], w_lo[:, slot, cols]
                                nc.tensor.matmul(out, ah, bh, start=first and k2 == 0, stop=False, skip_group_check=True)
                                nc.tensor.matmul(out, ah, bl, start=False, stop=False, skip_group_check=True)
                                last = nc.tensor.matmul(out, al, bh, start=False, stop=last_one and k2 == 1,
                                                        skip_group_check=True)
                    last.then_inc(chunk_mm, 1)

                def turn(j, first=False):
                    for r in range(2):
                        f, pos = j * 4 + 2 * r, j * 6 + (1 + 3 * r)
                        up(f + 1, 1, pos, 1, wait_bank=not (first and r == 0))
                        up(f + 2, 0, pos + 1, 2)
                        down(f, 2 * r, pos + 2, 0, first=first and r == 0)

                up(0, 0, 0, 0, wait_bank=False)
                turn(0, first=True)
                with pe.Fori(1, (FT - 2) // 4) as j:
                    turn(j)
                up(FT - 1, 1, FFN_N - 2, (FFN_N - 2) % RING)
                down(FT - 2, 0, FFN_N - 1, (FFN_N - 1) % RING, last_one=True)

            with pe.Fori(0, DEPTH) as l:
                split = l * A_S
                pe.wait_ge(A["xn"], TT)
                to_features(A, 0, xn)
                for c, width in enumerate(WIN_A):
                    pe.wait_ge(lo_done, split + (c + 1 + NEW))
                    if c >= 2:
                        pe.wait_ge(A["pj"], c - 1)
                    token_chunk(G[c % 2], c % RING, width).then_inc(chunk_mm, 1)

                pe.wait_ge(A["pj"], A_WIN)
                for b in range(len(TB) // 2):
                    if b == 2:
                        pe.wait_ge(A["rope_i"], 1)
                    if b == 3:
                        pe.wait_ge(A["dup"], len(DUP))
                    if b >= 2:
                        pe.wait_ge(A["blk_ev"], b - 1)
                    for k in range(2):
                        name, first, width, copies = TB[2 * b + k]
                        for i in range(TT):
                            src = pj[:, i, COL[name] + first:COL[name] + first + width]
                            if copies > 1:
                                src = dup[:, i, DUP.index(2 * b + k), :]
                            last = nc.tensor.transpose(G[b % 2][:, k * SEQ + i * P:k * SEQ + (i + 1) * P], src, ident)
                    last.then_inc(A["blk"], 1)

                pe.wait_ge(A["blk_ev"], T_IK // 2 + 1)
                for h in range(IDX_H):
                    if h >= 2:
                        pe.wait_ge(A["ix_relu"], h - 1)
                    q, rows = T_IQ + h // 4, slice(32 * (h % 4), 32 * (h % 4) + 32)
                    nc.tensor.matmul(S[h % 2][:, 0:P], tb[rows, q, 0:P], tb[rows, T_IK, 0:P], start=True, stop=True)
                    nc.tensor.matmul(S[h % 2][:, P:CAUS], tb[rows, q, P:SEQ], tb[rows, T_IK, :],
                                     start=True, stop=True).then_inc(A["ix"], 1)

                pe.wait_ge(A["rw"], 2)
                pe.wait_ge(A["blk_ev"], len(TB) // 2)
                j = 0
                for d in range(A_CMP):
                    n = A_N0["cmp"] + d
                    pe.wait_ge(raw_in[n % RING], arrivals(l, n))
                    for jj in range(a_width(n) // P):
                        for kv in range(2):
                            rows = slice(64 * kv, 64 * kv + 64)
                            last = nc.tensor.matmul(G[kv][:, 0:NCMP], raw[rows, n % RING, jj * P:(jj + 1) * P],
                                                    rw[rows, j, :], start=(j == 0), stop=(j == CBLK - 1))
                        j += 1
                    last.then_inc(direct_mm, 1)
                pe.wait_ge(A["cgel"], 1)
                nc.tensor.matmul(G[0][:, 32:32 + NCMP], sa("w2k"), hb[:, 3, 0, 0:NCMP], start=True, stop=True)
                nc.tensor.matmul(G[0][:, 64:64 + HD], flat(vr), sa("w2v"), start=True, stop=True).then_inc(A["ckv"], 1)
                pe.wait_ge(A["ckv_ev"], 2)
                pe.wait_ge(A["ix_relu"], IDX_H)
                for odd in range(2):
                    for i in range(TT):
                        for h in range(odd, NSA_H, 2):
                            rows, at = slice(64 * odd, 64 * odd + 64), (i * 3 + h // 2) * 16
                            last = nc.tensor.matmul(S[odd][:, at:at + NCMP], tb[rows, T_AQR + h // 2, i * P:(i + 1) * P],
                                                    kcm[rows, 0:NCMP], start=True, stop=True)
                    last.then_inc(A["cs"], 1)
                pe.wait_ge(A["cp"], 1)
                for i in range(TT):
                    nc.tensor.transpose(PT[0][:, i * P:(i + 1) * P], pc[:, i, 0:4, :], ident)
                    last = nc.tensor.transpose(PT[0][0:32, SEQ + i * P:SEQ + (i + 1) * P], pc[:, i, 4, :], ident)
                last.then_inc(A["cpt"], 1)
                pe.wait_ge(A["cpt_ev"], 2)
                for h in range(NSA_H):
                    for i in range(TT):
                        r, at = 32 * (h % 4), (h // 4 * TT + i) * HD
                        src = pcT[r:r + NCMP, i, :] if h < 4 else pcT4[0:NCMP, i, :]
                        last = nc.tensor.matmul(CO[h % 4][:, at:at + HD], src, vc4[r:r + NCMP, :], start=True, stop=True)
                    last.then_inc(A["co"], 1)

                def scores(u):
                    q, k, r, _, _, _ = unit(u)
                    if u >= 2:
                        pe.wait_ge(A["nm"], u - 1)
                    rows = slice(r, r + HD)
                    nc.tensor.matmul(S[u % 2][:, 0:P], tb[rows, q, 0:P], tb[rows, k, 0:P], start=True, stop=True)
                    nc.tensor.matmul(S[u % 2][:, P:CAUS], tb[rows, q, P:SEQ], tb[rows, k, :],
                                     start=True, stop=True).then_inc(A["s"], 1)

                def turn_weights(u):
                    pe.wait_ge(A["e"], u + 1)
                    if u >= 2:
                        pe.wait_ge(A["pt_ev"], u - 1)
                    for cols in (slice(0, P), slice(P, SEQ), slice(SEQ, CAUS)):
                        last = nc.tensor.transpose(PT[u % 2][:, cols], pr[:, u % 2, cols], ident)
                    last.then_inc(A["pt"], 1)

                def values(u):
                    _, _, _, v, _, _ = unit(u)
                    pe.wait_ge(A["pt_ev"], u + 1)
                    if u >= 2:
                        pe.wait_ge(A["o_ev"], u - 1)
                    out, w = O[u % 2], pt[:, u % 2, :]
                    nc.tensor.matmul(out[:, 0:HD], w[:, 0:P], pj[:, 0, v:v + HD], start=True, stop=True)
                    nc.tensor.matmul(out[:, HD:2 * HD], w[:, P:SEQ], pj[:, 0, v:v + HD], start=True, stop=False)
                    nc.tensor.matmul(out[:, HD:2 * HD], w[:, SEQ:CAUS], pj[:, 1, v:v + HD],
                                     start=False, stop=True).then_inc(A["o"], 1)

                def modulation(d):
                    n = A_N0["ada"] + d
                    pe.wait_ge(raw_in[n % RING], arrivals(l, n))
                    for half in range(2):
                        for k in range(KT):
                            at = (half * KT + k) * P
                            last = nc.tensor.matmul(ADA[:, 2 * d + half:2 * d + half + 1], raw[:, n % RING, at:at + P],
                                                    cvec[:, 1, k:k + 1], start=(k == 0), stop=(k == KT - 1))
                    last.then_inc(direct_mm, 1)

                pe.wait_ge(A["co_ev"], NSA_H)
                for step in range(NU + LAG_O):
                    if step < NU:
                        if step == U_DSA:
                            pe.wait_ge(A["dmask"], 1)
                        scores(step)
                    if LAG_T <= step < NU + LAG_T:
                        turn_weights(step - LAG_T)
                    if step >= LAG_O:
                        values(step - LAG_O)
                    for d in ada_chunks(step):
                        modulation(d)

                pe.wait_ge(A["mix"], 1)
                to_features(A, 1, mix)
                pe.wait_ge(A["ada_ev"], 1)
                for c in range(A_WOUT):
                    pe.wait_ge(lo_done, split + (A_WIN + c + 1 + NEW))
                    if c >= 2:
                        pe.wait_ge(A["x"], c - 1)
                    token_chunk(G[c % 2], (A_WIN + c) % RING, GW).then_inc(chunk_mm, 1)
                pe.wait_ge(A["xn"], 2 * TT)
                to_features(A, 2, xn)
                ffn(A, split + (A_WIN + A_WOUT), 0)
                pe.drain().then_inc(layer_done, 1)
                pe.wait_ge(layer_go, l + 1)

            def gate_on_all(sub):
                pe.wait_ge(B["gdiag"], sub + 1)
                for half in range(2):
                    nc.tensor.matmul(G[half][:, :], const("ones"), gdiag[:, 4 * half:4 * half + 4, :].rearrange("p k n -> p (k n)"),
                                     start=True, stop=True).then_inc(B["gateb"], 1)

            pe.wait_ge(FIN["x"], TT)
            with pe.Fori(0, DEPTH) as l:
                split = l * B_N + S_A
                gate_on_all(0)
                to_features(B, 0, x)
                pe.wait_ge(B["gateb_ev"], 2)
                ffn(B, split, 0)
                pe.wait_ge(B["ln"], 1)
                gate_on_all(1)
                to_features(B, 1, x)
                pe.wait_ge(B["gateb_ev"], 4)
                nf = ntm = 0
                for c, (ftiles, _, width) in enumerate(B_WIN):
                    s_ = B_S0["win"] + c
                    pe.wait_ge(lo_done, split + (s_ + 1 + NEW))
                    if c >= 2:
                        ftiles_b, _, width_b = B_WIN[c - 2]
                        if width_b:
                            pe.wait_ge(B["tm"], len([1 for b in B_WIN[:c - 1] if b[2]]))
                        if ftiles_b:
                            pe.wait_ge(B["conv"] if ftiles_b[0] in F_CONV else B["fm"], bank_count(c - 2))
                    for k in range(len(ftiles)):
                        last = feature_tile(G[c % 2][:, k * SEQ:(k + 1) * SEQ], s_ % RING, k, P * len(ftiles) + width)
                    if width:
                        last = token_chunk(G[c % 2][:, SEQ * len(ftiles):], s_ % RING, width, P * len(ftiles))
                    last.then_inc(chunk_mm, 1)

                pe.wait_ge(B["gl"], 1)
                pe.wait_ge(B["tm"], 8)
                nc.tensor.matmul(S[0][:, 0:12], const("upto"), gl[:, 0, :], start=True, stop=True)
                nc.tensor.matmul(S[0][:, 12:24], const("ones"), gl[:, 0, :], start=True, stop=False)
                nc.tensor.matmul(S[0][:, 12:24], const("upto"), gl[:, 1, :], start=False, stop=True).then_inc(B["cum"], 1)
                pe.wait_ge(B["cg"], 1)
                for i in range(TT):
                    cols = slice(i * P, (i + 1) * P)
                    cols2 = slice(SEQ + i * P, SEQ + (i + 1) * P)
                    nc.tensor.transpose(PT[0][0:12, cols], ngr[:, i, :], ident)
                    nc.tensor.transpose(PT[0][0:6, cols2], beta[:, i, :], ident)
                    nc.tensor.transpose(PT[1][0:6, cols], gl[:, i, 6:12], ident)
                    last = nc.tensor.transpose(PT[1][0:6, cols2], gt[:, i, 18:24], ident)
                last.then_inc(B["rows"], 1)
                pe.wait_ge(B["sq"], 1)
                half = const("half").rearrange("p (f n) -> p f n", f=6)
                for f in range(6):
                    last = nc.tensor.matmul(O[0][0:12, 0:SEQ], half[:, f, :], sq[:, f, :], start=(f == 0), stop=(f == 5))
                last.then_inc(B["ss"], 1)
                pe.wait_ge(B["scan"], 1)
                for i in range(TT):
                    last = nc.tensor.transpose(S[1][:, i * 6:i * 6 + 6], row_m[0:6, i * P:(i + 1) * P], ident[0:6, 0:6])
                last.then_inc(B["mback"], 1)
                pe.wait_ge(B["rn"], 1)
                pair12 = const("pair12", 12).rearrange("p (f n) -> p f n", f=6)
                for f in range(6):
                    if f >= 4:
                        pe.wait_ge(B["rnb_ev"], f // 2 - 1)
                    last = nc.tensor.matmul(G[f // 2 % 2][:, f % 2 * SEQ:(f % 2 + 1) * SEQ], pair12[:, f, :], norm_r[0:12, :],
                                            start=True, stop=True)
                    if f % 2:
                        last.then_inc(B["rnb"], 1)
                pair = const("pair", 6).rearrange("p (f n) -> p f n", f=3)
                for f in range(3):
                    bank, at = (O[1], f * SEQ) if f < 2 else (O[0], 0)
                    if f == 2:
                        pe.wait_ge(B["ssr"], 1)
                    last = nc.tensor.matmul(bank[:, at:at + SEQ], pair[:, f, :], row_b[0:6, :], start=True, stop=True)
                last.then_inc(B["bb"], 1)
                pe.wait_ge(B["rows_ev"], 4)
                for i in range(TT):
                    for f in range(3):
                        last = nc.tensor.transpose(PT[i][:, f * P:(f + 1) * P], fm[:, F_GV + f, i * P:(i + 1) * P], ident)
                    last.then_inc(B["vt"], 1)

                def spread_row(out, r):
                    return nc.tensor.matmul(out, ident[0:12, r:r + 1].to_broadcast([12, P]), grow[0:12, :], start=True, stop=True)

                def scores_b(u):
                    kind, h = B_UNITS[u]
                    if 2 <= u < MOBA_H + 2:
                        pe.wait_ge(B["s_free"], u - 1)
                    elif u >= 2:
                        pe.wait_ge(B["p"], u - 1 - MOBA_H)
                    q, k = (F_MQ, F_MK) if kind == "moba" else (F_LQ, F_LK)
                    rows = slice(64 * (h % 2), 64 * (h % 2) + 64)
                    if kind == "mlstm":
                        spread_row(G[u % 2][:, 0:SEQ], 6 + h)
                    nc.tensor.matmul(S[u % 2][:, 0:P], fm[rows, q + h // 2, 0:P], fm[rows, k + h // 2, 0:P], start=True, stop=True)
                    nc.tensor.matmul(S[u % 2][:, P:CAUS], fm[rows, q + h // 2, P:SEQ], fm[rows, k + h // 2, :],
                                     start=True, stop=True).then_inc(B["s"], 1)

                def turn_b(u):
                    if B_UNITS[u][0] == "moba":
                        pe.wait_ge(B["e"], u + 1)
                    else:
                        pe.wait_ge(B["p"], u - MOBA_H + 1)
                    if u >= 2:
                        pe.wait_ge(B["pt_ev"], u - 1)
                    for cols in (slice(0, P), slice(P, SEQ), slice(SEQ, CAUS)):
                        last = nc.tensor.transpose(PT[u % 2][:, cols], prb[:, u % 2, cols], ident)
                    last.then_inc(B["pt"], 1)

                def values_b(u):
                    kind, h = B_UNITS[u]
                    v = (VB if kind == "moba" else VC) + h * HD
                    pe.wait_ge(B["pt_ev"], u + 1)
                    if u >= 2:
                        pe.wait_ge(B["o_ev"], u - 1)
                    out, w = O[u % 2], ptb[:, u % 2, :]
                    nc.tensor.matmul(out[:, 0:HD], w[:, 0:P], tm[:, 0, v:v + HD], start=True, stop=True)
                    nc.tensor.matmul(out[:, HD:2 * HD], w[:, P:SEQ], tm[:, 0, v:v + HD], start=True, stop=False)
                    nc.tensor.matmul(out[:, HD:2 * HD], w[:, SEQ:CAUS], tm[:, 1, v:v + HD], start=False, stop=True).then_inc(B["o"], 1)

                pe.wait_ge(B["vb"], TT)
                pe.wait_ge(B["kb"], 3)
                pe.wait_ge(B["em"], 1)
                for step in range(NUB + B_LAGO):
                    if step < NUB:
                        scores_b(step)
                    if B_LAGT <= step < NUB + B_LAGT:
                        turn_b(step - B_LAGT)
                    if step >= B_LAGO:
                        values_b(step - B_LAGO)

                pe.wait_ge(B["o_ev"], NUB)
                for h in range(GDN_H):
                    if h >= 2:
                        pe.wait_ge(B["dmul"], h - 1)
                    rows = slice(64 * (h % 2), 64 * (h % 2) + 64)
                    spread_row(G[h % 2][:, 0:SEQ], h)
                    kT = fm[rows, F_GK + h // 2, :]
                    for bank, other in ((S[h % 2], fm[rows, F_GQ + h // 2, :]), (PT[h % 2], kbT[rows, h // 2, :])):
                        nc.tensor.matmul(bank[:, 0:SEQ], kT[:, 0:P], other[:, 0:SEQ], start=True, stop=True)
                        last = nc.tensor.matmul(bank[:, SEQ:CAUS], kT[:, P:SEQ], other[:, P:SEQ], start=True, stop=True)
                    last.then_inc(B["ds"], 1)
                pe.wait_ge(B["dmul"], GDN_H)
                pe.wait_ge(B["xinit"], 1)
                NI = 2 * GDN_H

                def inv_y(n):
                    lev, u = n // NI, n % NI
                    pe.wait_ge(B["atm"], n + 1)
                    if lev:
                        pe.wait_ge(B["xx"], n - NI + 1)
                    if n >= 4:
                        pe.wait_ge(B["y_ev"], n - 3)
                    nc.tensor.matmul(ps[n % 4][:, 0:P], atm[:, n % 4, :], xx[:, u, 0, :], start=True, stop=True).then_inc(B["y"], 1)

                def inv_z(n):
                    u = n % NI
                    pe.wait_ge(B["y_ev"], n + 1)
                    if n >= 4:
                        pe.wait_ge(B["xx"], n - 3)
                    nc.tensor.matmul(ps[4 + n % 4][:, 0:P], xx[:, u, 1, :], ym[:, n % 4, :], start=True, stop=True)
                    nc.tensor.matmul(ps[4 + n % 4][:, P:SEQ], ym[:, n % 4, :], xx[:, u, 1, :], start=True, stop=True).then_inc(B["z"], 1)

                for n in range(7 * NI + 2):
                    if n < 7 * NI:
                        inv_y(n)
                    if n >= 2:
                        inv_z(n - 2)
                pe.wait_ge(B["xx"], 7 * NI)
                pe.wait_ge(B["y_ev"], 7 * NI)
                hd = lambda h: slice(h * HD, (h + 1) * HD)
                for h in range(GDN_H):
                    last = nc.tensor.matmul(ps[0][:, hd(h)], xx[:, 2 * h, 1, :], vb[:, 0, h, :], start=True, stop=True)
                last.then_inc(B["u"], 1)
                pe.wait_ge(B["u_ev"], 1)
                for h in range(GDN_H):
                    last = nc.tensor.matmul(ps[1][:, hd(h)], sysT[:, h, P:SEQ], uu[:, 0, hd(h)], start=True, stop=True)
                last.then_inc(B["u"], 1)
                for h in range(GDN_H):
                    last = nc.tensor.matmul(ps[3][:, hd(h)], attnT[:, h, 0:P], uu[:, 0, hd(h)], start=True, stop=True)
                last.then_inc(B["go"], 1)
                pe.wait_ge(B["w1"], 1)
                for h in range(GDN_H):
                    last = nc.tensor.matmul(ps[2][:, hd(h)], xx[:, 2 * h + 1, 1, :], vb[:, 1, h, :], start=True, stop=True)
                last.then_inc(B["u"], 1)
                pe.wait_ge(B["u_ev"], 2)
                for h in range(GDN_H):
                    nc.tensor.matmul(ps[4][:, hd(h)], attnT[:, h, P:SEQ], uu[:, 0, hd(h)], start=True, stop=False)
                    last = nc.tensor.matmul(ps[4][:, hd(h)], attnT[:, h, SEQ:CAUS], uu[:, 1, hd(h)], start=False, stop=True)
                last.then_inc(B["go"], 1)

                pe.wait_ge(B["mix"], 1)
                to_features(B, 2, mixb)
                for c in range(B_WOUT):
                    s_ = B_S0["wout"] + c
                    pe.wait_ge(lo_done, split + (s_ + 1 + NEW))
                    token_chunk(ACC[c][:, :], s_ % RING, GW).then_inc(chunk_mm, 1)
                pe.wait_ge(B["ln"], 2)
                gate_on_all(2)
                to_features(B, 3, x)
                pe.wait_ge(B["gateb_ev"], 6)
                ffn(B, split + B_S0["ffn1"], FT)
                pe.drain().then_inc(layer_done, 1)
                pe.wait_ge(layer_go, l + (DEPTH + 1))

        @block.scalar
        def _(act):
            act.wait_ge(start_in, 64)
            nc.scalar.activation(cvec[:, 1, :], cvec[:, 0, :], ACT.Silu).then_inc(pre, 1)

            def hi(s, slot, raw_slot, raw_wait, width=CW):
                act.wait_ge(raw_in[raw_slot], raw_wait)
                act.wait_ge(chunk_mm, s + 1)
                nc.scalar.activation(w_hi[:, slot, 0:width], raw[:, raw_slot, 0:width], ACT.Copy).then_inc(hi_done, 1)

            def root_mean_square(N, v):
                for i in range(TT):
                    nc.scalar.activation(junk[:, i, :], x[:, i, :], ACT.Square, accum_out=st[:, i:i + 1]).then_inc(N["ss"], 1)
                act.wait_ge(N["ss"], v * TT + TT)
                nc.scalar.activation(st[:, 2:4], st[:, 0:2], ACT.Sqrt, scale=1.0 / DM, bias=NORM_EPS).then_inc(N["std"], 1)

            def hi_features(N, v, gain):
                for k in range(KT):
                    act.wait_ge(N["tp"], v * KT + k + 1)
                    nc.scalar.activation(hT_hi[:, k, :], TP[k % 2][:, 0:SEQ], ACT.Copy,
                                         scale=sa(gain, k) if gain else 1.0).then_inc(N["tp_hi"], 1)

            def ffn(N, split, raw0, h0, conv, more):
                def hi_at(pos, slot):
                    hi(pos + split, slot, slot, raw0 + after(pos))

                def after(pos):
                    return 16 * (pos // RING + 1)

                def post(f, f2, f4, pos, ahead):
                    act.wait_ge(chunk_mm, pos + (1 + NEW) + split)
                    if conv:
                        nc.scalar.activation(cv[:, f2, :], UP[f2][:, 0:SEQ], ACT.Identity, scale=conv_tap(f, 2),
                                             bias=conv_tap(f, 3)).then_inc(N["c1"], 1)
                    else:
                        nc.scalar.activation(sg[:, f2, :], UP[f2][:, 0:SEQ], ACT.Silu).then_inc(N["sg"], 1)
                    ahead()
                    if conv:
                        act.wait_ge(N["cv2"], f + (h0 + 1))
                        nc.scalar.activation(sg[:, f2, :], cv[:, f2, :], ACT.Silu).then_inc(N["sg"], 1)
                    act.wait_ge(N["h"], f + (h0 + 1))
                    nc.scalar.activation(hid_hi[:, f4, :], h32[:, f2, :], ACT.Copy).then_inc(N["hid_hi"], 1)

                def turn(j, stop=FFN_N + 2):
                    for q in range(6):
                        def ahead():
                            pos = q + 4
                            if isinstance(j, int):
                                if j * 6 + pos < stop:
                                    hi(split + (j * 6 + pos), pos % RING, pos % RING, raw0 + 16 * ((j * 6 + pos) // RING + 1))
                            else:
                                hi(j * 6 + pos + split, pos % RING, pos % RING, j * 32 + 16 * (pos // RING + 1) + raw0)
                        if q % 3 == 2:
                            ahead()
                        else:
                            f = j * 4 + (1 + q - q // 3)
                            f4 = (1 + q - q // 3) % 4
                            post(f, f4 % 2, f4, j * 6 + (1 + q), ahead)

                hi(split + 2, 2, 2, raw0 + 16)
                post(0, 0, 0, 0, lambda: hi(split + 3, 0, 0, raw0 + 32))
                turns = (FT - 2) // 4
                with act.Fori(0, turns - 1) as j:
                    turn(j)
                turn(turns - 1, FFN_N + more)
                post(FT - 1, 1, 1, FFN_N - 2,
                     (lambda: hi(split + 34, 34 % RING, 34 % RING, raw0 + 16 * 12)) if more else (lambda: None))

            with act.Fori(0, DEPTH) as l:
                split = l * A_S

                def hi_a(s):
                    n = s if s < A_WIN else s + A_D
                    hi(split + s, s % RING, n % RING, arrivals(l, n), a_width(n))

                hi_a(0)
                hi_a(1)
                root_mean_square(A, 0)
                act.wait_ge(small_in, l * 16 + 16)
                hi_features(A, 0, "g1")
                for c, width in enumerate(WIN_A):
                    if c + 2 < A_WIN:
                        hi_a(c + 2)
                    act.wait_ge(chunk_mm, split + (c + 1 + NEW))
                    nc.scalar.activation(pj[:, :, c * GW:c * GW + width],
                                         G[c % 2][:, 0:TT * width].rearrange("p (t n) -> p t n", t=TT),
                                         ACT.Copy).then_inc(A["pj"], 1)
                for b in range(len(TB) // 2):
                    if b == 2:
                        act.wait_ge(A["rope_h"], 1)
                        for k, block_ in enumerate(DUP):
                            name, first, width, copies = TB[block_]
                            nc.scalar.activation(dup[:, :, k, :].rearrange("p t (c n) -> p t c n", c=copies),
                                                 pj[:, :, COL[name]:COL[name] + width].unsqueeze(2)
                                                 .to_broadcast([P, TT, copies, width]), ACT.Copy).then_inc(A["dup"], 1)
                    act.wait_ge(A["blk"], b + 1)
                    nc.scalar.activation(tb[:, 2 * b:2 * b + 2, :], G[b % 2][:, :].rearrange("p (k n) -> p k n", k=2),
                                         ACT.Copy).then_inc(A["blk_ev"], 1)
                for h in range(IDX_H):
                    act.wait_ge(A["ix"], h + 1)
                    if h >= 2:
                        act.wait_ge(A["ix_acc"], h - 1)
                    nc.scalar.activation(relu[:, h % 2, :], S[h % 2][:, 0:CAUS], ACT.Relu,
                                         scale=IDX_D ** -0.5).then_inc(A["ix_relu"], 1)
                act.wait_ge(A["gate"], 1)
                nc.scalar.activation(ags, ags, ACT.Exp, scale=-1.0).then_inc(A["gate_e"], 1)
                act.wait_ge(A["cg"], 1)
                nc.scalar.activation(hb[:, 2, :, 0:NCMP], hb[:, 1, :, 0:NCMP], ACT.Exp,
                                     scale=-2.0 * (2.0 / np.pi) ** 0.5).then_inc(A["cg_e"], 1)
                act.wait_ge(A["ckv"], 1)
                nc.scalar.activation(kcm[:, 0:NCMP], G[0][:, 32:32 + NCMP], ACT.Copy).then_inc(A["ckv_ev"], 1)
                nc.scalar.activation(vc4, G[0][:, 64:64 + HD], ACT.Copy).then_inc(A["ckv_ev"], 1)
                act.wait_ge(A["cnm"], 1)
                nc.scalar.activation(lc[:, :, :, 0:NCMP], lc[:, :, :, 0:NCMP], ACT.Exp).then_inc(A["cexp"], 1)
                act.wait_ge(A["cpt"], 1)
                nc.scalar.activation(pcT, PT[0][:, 0:SEQ].rearrange("p (t n) -> p t n", t=TT), ACT.Copy).then_inc(A["cpt_ev"], 1)
                nc.scalar.activation(pcT4[0:32], PT[0][0:32, SEQ:2 * SEQ].rearrange("p (t n) -> p t n", t=TT),
                                     ACT.Copy).then_inc(A["cpt_ev"], 1)

                def exponentials(u):
                    act.wait_ge(A["nm"], u + 1)
                    if u >= 2:
                        act.wait_ge(A["pt"], u - 1)
                    nc.scalar.activation(pr[:, u % 2, 0:P], lg[:, u % 2, 0:P], ACT.Exp, bias=nmax[:, u, 0:1],
                                         accum_out=den[:, u, 0:1])
                    nc.scalar.activation(pr[:, u % 2, P:CAUS], lg[:, u % 2, P:CAUS], ACT.Exp, bias=nmax[:, u, 1:2],
                                         accum_out=den[:, u, 1:2]).then_inc(A["e"], 1)

                def copy_weights(u):
                    act.wait_ge(A["pt"], u + 1)
                    if u >= 2:
                        act.wait_ge(A["o"], u - 1)
                    nc.scalar.activation(pt[:, u % 2, :], PT[u % 2][:, 0:CAUS], ACT.Copy).then_inc(A["pt_ev"], 1)

                act.wait_ge(A["co"], NSA_H)
                for step in range(NU + LAG_T):
                    if step < NU:
                        exponentials(step)
                    if step >= LAG_T:
                        copy_weights(step - LAG_T)
                act.wait_ge(A["dila"], 1)
                nc.scalar.activation(dexp, dexp, ACT.Exp).then_inc(A["dila_e"], 1)
                hi_a(A_WIN)
                hi_a(A_WIN + 1)
                hi_features(A, 1, None)
                for c in range(A_WOUT):
                    hi_a(A_WIN + c + 2)
                act.wait_ge(A["x"], A_WOUT)
                root_mean_square(A, 1)
                hi_features(A, 2, "g2")
                ffn(A, split + (A_WIN + A_WOUT), l * (16 * A_N // RING) + 16 * (A_N0["ffn"] // RING), 0, True, 0)
                act.drain().then_inc(layer_done, 1)
                act.wait_ge(layer_go, l + 1)
            root_mean_square(FIN, 0)

            def gate_copy(sub):
                for half in range(2):
                    act.wait_ge(B["gateb"], sub * 2 + half + 1)
                    nc.scalar.activation(gateb[:, half * 512:half * 512 + 512], G[half][:, :], ACT.Copy).then_inc(B["gateb_ev"], 1)

            def hi_mod(v):
                for k in range(KT):
                    act.wait_ge(B["tp_mod"], mod_count(v, k) + 1)
                    nc.scalar.activation(hT_hi[:, k, :], hx[:, k % 2, :], ACT.Copy).then_inc(B["tp_hi"], 1)

            def root(sub):
                act.wait_ge(B["std"], 2 * sub + 1)
                nc.scalar.activation(st[:, 8:10], bag[:, :, 1], ACT.Sqrt, bias=LN_EPS).then_inc(B["std"], 1)

            act.wait_ge(FIN["x"], TT)
            with act.Fori(0, DEPTH) as l:
                split = l * B_N + S_A

                def hi_b(s):
                    hi(split + s, s % RING, s % RING, arrivals_b(l, s), b_width(s))

                hi_b(0)
                hi_b(1)
                gate_copy(0)
                hi_mod(0)
                ffn(B, split, l * (16 * B_N // RING) + 16 * N_A, 0, False, 2)
                root(0)
                gate_copy(1)
                hi_mod(1)
                act.wait_ge(small_in, l * 16 + (DEPTH * 16 + 16))
                silus = []

                def silu(c):
                    ftiles = B_WIN[c][0]
                    act.wait_ge(B["conv"], bank_count(c))
                    nc.scalar.activation(fm[:, ftiles[0]:ftiles[0] + len(ftiles), :], cvb[:, c % 2, 0:len(ftiles), :],
                                         ACT.Silu).then_inc(B["fm"], 1)

                for c, (ftiles, at, width) in enumerate(B_WIN):
                    s_ = B_S0["win"] + c
                    hi_b(s_ + 2)
                    if silus and c - silus[0] >= 1:
                        silu(silus.pop(0))
                    act.wait_ge(chunk_mm, split + (s_ + 1 + NEW))
                    bank = G[c % 2]
                    if ftiles and ftiles[0] in F_CONV:
                        for k, f in enumerate(ftiles):
                            if f in F_CONV:
                                nc.scalar.activation(cvb[:, c % 2, k, :], bank[:, k * SEQ:(k + 1) * SEQ], ACT.Copy,
                                                     scale=tap(f, 3)).then_inc(B["tap"], 1)
                        silus.append(c)
                    elif ftiles:
                        nc.scalar.activation(fm[:, ftiles[0]:ftiles[0] + 2, :], bank[:, :].rearrange("p (k n) -> p k n", k=2),
                                             ACT.Copy).then_inc(B["fm"], 1)
                    if width:
                        first = SEQ * len(ftiles)
                        nc.scalar.activation(tm[:, :, at:at + width],
                                             bank[:, first:first + TT * width].rearrange("p (t n) -> p t n", t=TT),
                                             ACT.Copy).then_inc(B["tm"], 1)
                for c in silus:
                    silu(c)
                act.wait_ge(B["tm"], 8)
                nc.scalar.activation(tm[:, :, ZC:ZC + 384], tm[:, :, ZC:ZC + 384], ACT.Silu).then_inc(B["act"], 1)
                nc.scalar.activation(tm[:, :, OC:OC + 384], tm[:, :, OC:OC + 384], ACT.Sigmoid).then_inc(B["act"], 1)
                act.wait_ge(B["fm"], len([1 for b in B_WIN if b[0]]))
                nc.scalar.activation(sq, fm[:, F_GQ:F_GQ + 6, :], ACT.Square).then_inc(B["sq"], 1)
                act.wait_ge(B["gt"], 1)
                nc.scalar.activation(ga, ga, ACT.Exp, scale=-1.0).then_inc(B["ge"], 1)
                nc.scalar.activation(beta, sig, ACT.Exp, scale=-1.0).then_inc(B["ge"], 1)
                nc.scalar.activation(ealog, sbp("a_log"), ACT.Exp).then_inc(B["ge"], 1)
                act.wait_ge(B["ge"], 3)
                nc.scalar.activation(gl1, ga, ACT.Ln, bias=1.0).then_inc(B["gln"], 1)
                act.wait_ge(B["rows"], 1)
                nc.scalar.activation(grow[0:12, :], PT[0][0:12, 0:SEQ], ACT.Copy).then_inc(B["rows_ev"], 1)
                nc.scalar.activation(row_b[0:6, :], PT[0][0:6, SEQ:2 * SEQ], ACT.Copy).then_inc(B["rows_ev"], 1)
                nc.scalar.activation(row_f[0:6, :], PT[1][0:6, 0:SEQ], ACT.Copy).then_inc(B["rows_ev"], 1)
                nc.scalar.activation(row_i[0:6, :], PT[1][0:6, SEQ:2 * SEQ], ACT.Copy).then_inc(B["rows_ev"], 1)
                act.wait_ge(B["ss"], 1)
                nc.scalar.activation(norm_r[0:12, :], O[0][0:12, 0:SEQ], ACT.Sqrt, bias=NORM_EPS).then_inc(B["ssr"], 1)
                act.wait_ge(B["bm"], 1)
                nc.scalar.activation(em, S[1][:, 0:12].rearrange("p (t h) -> p t h", t=TT), ACT.Exp, scale=-1.0).then_inc(B["em"], 1)

                def exp_b(u):
                    kind, h = B_UNITS[u]
                    act.wait_ge(B["nm"], u + 1)
                    if u >= 2:
                        act.wait_ge(B["pt"], u - 1)
                    for i, cols in enumerate((slice(0, P), slice(P, CAUS))):
                        if kind == "moba":
                            last = nc.scalar.activation(prb[:, u % 2, cols], lgb[:, u % 2, cols], ACT.Exp, bias=nmaxb[:, u, i:i + 1],
                                                        accum_out=denb[:, u, i:i + 1])
                        else:
                            last = nc.scalar.activation(prb[:, u % 2, cols], lgb[:, u % 2, cols], ACT.Exp, bias=bm[:, i, h:h + 1])
                    last.then_inc(B["e"], 1)

                def copy_b(u):
                    act.wait_ge(B["pt"], u + 1)
                    if u >= 2:
                        act.wait_ge(B["o"], u - 1)
                    nc.scalar.activation(ptb[:, u % 2, :], PT[u % 2][:, 0:CAUS], ACT.Copy).then_inc(B["pt_ev"], 1)

                for step in range(NUB + B_LAGT):
                    if step < NUB:
                        exp_b(step)
                    if step >= B_LAGT:
                        copy_b(step - B_LAGT)
                for h in range(GDN_H):
                    act.wait_ge(B["dl"], h + 1)
                    nc.scalar.activation(dec[h % 2][:, 0:SEQ], dec[h % 2][:, 0:SEQ], ACT.Exp, bias=negG[:, 0, h:h + 1])
                    nc.scalar.activation(dec[h % 2][:, SEQ:CAUS], dec[h % 2][:, SEQ:CAUS], ACT.Exp, bias=negG[:, 1, h:h + 1]
                                         ).then_inc(B["dec"], 1)
                for n in range(7 * 2 * GDN_H):
                    act.wait_ge(B["y"], n + 1)
                    if n >= 4:
                        act.wait_ge(B["z"], n - 3)
                    nc.scalar.activation(ym[:, n % 4, :], ps[n % 4][:, 0:P], ACT.Copy).then_inc(B["y_ev"], 1)
                act.wait_ge(B["u"], 1)
                nc.scalar.activation(uu[:, 0, :], ps[0][:, 0:384], ACT.Copy).then_inc(B["u_ev"], 1)
                act.wait_ge(B["u"], 3)
                nc.scalar.activation(uu[:, 1, :], ps[2][:, 0:384], ACT.Copy).then_inc(B["u_ev"], 1)
                act.wait_ge(B["go"], 2)
                nc.scalar.activation(sq2[:, 0, :], ps[3][:, 0:384], ACT.Square).then_inc(B["gsq"], 1)
                nc.scalar.activation(sq2[:, 1, :], ps[4][:, 0:384], ACT.Square).then_inc(B["gsq"], 1)
                act.wait_ge(B["gms"], 1)
                nc.scalar.activation(hst, hst, ACT.Sqrt, scale=1.0 / HD, bias=NORM_EPS).then_inc(B["grs"], 1)
                act.wait_ge(B["lvar"], 1)
                nc.scalar.activation(hst3, hst3, ACT.Sqrt, scale=1.0 / HD, bias=NORM_EPS).then_inc(B["lrs"], 1)
                hi_features(B, 2, None)
                for c in range(B_WOUT):
                    hi_b(B_S0["wout"] + c + 2)
                root(1)
                gate_copy(2)
                hi_mod(3)
                ffn(B, split + B_S0["ffn1"], l * (16 * B_N // RING) + 16 * (N_A + B_S0["ffn1"] // RING), FT, False, 0)
                root(2)
                act.drain().then_inc(layer_done, 1)
                act.wait_ge(layer_go, l + (DEPTH + 1))

        @block.vector
        def _(dve):
            dve.sem_inc(lo_done, NEW)
            dve.wait_ge(start_in, 64)

            def lo(s, slot, raw_slot, width=CW):
                dve.wait_ge(hi_done, s + 1)
                nc.vector.tensor_tensor(w_lo[:, slot, 0:width], raw[:, raw_slot, 0:width],
                                        w_hi[:, slot, 0:width].bitcast(F32), ALU.subtract).then_inc(lo_done, 1)

            def normed(N, v):
                dve.wait_ge(N["std"], v + 1)
                nc.vector.reciprocal(st[:, 4:6], st[:, 2:4]).then_inc(N["rstd"], 1)
                dve.wait_ge(N["rstd"], v + 1)

            def rms_norm(N, v):
                normed(N, v)
                for i in range(TT):
                    nc.vector.tensor_scalar(xn[:, i, :], x[:, i, :], st[:, 4 + i:5 + i], None, ALU.mult).then_inc(N["xn"], 1)

            def lo_features(N, v, gain):
                for k in range(KT):
                    dve.wait_ge(N["tp_hi"], v * KT + k + 1)
                    nc.vector.scalar_tensor_tensor(out=hT_lo[:, k, :], in0=TP[k % 2][:, 0:SEQ],
                                                   scalar=sa(gain, k) if gain else 1.0, in1=hT_hi[:, k, :].bitcast(F32),
                                                   op0=ALU.mult, op1=ALU.subtract).then_inc(N["tp_lo"], 1)

            def ffn(N, split, h0, conv, more):
                def post(f, f2, f4, ahead):
                    if conv:
                        dve.wait_ge(N["c1"], f + (h0 + 1))
                        nc.vector.scalar_tensor_tensor(out=cv[:, f2, 1:SEQ], in0=UP[f2][:, 0:SEQ - 1], scalar=conv_tap(f, 1),
                                                       in1=cv[:, f2, 1:SEQ], op0=ALU.mult, op1=ALU.add).then_inc(N["cv1"], 1)
                        dve.wait_ge(N["cv1"], f + (h0 + 1))
                        nc.vector.scalar_tensor_tensor(out=cv[:, f2, 2:SEQ], in0=UP[f2][:, 0:SEQ - 2], scalar=conv_tap(f, 0),
                                                       in1=cv[:, f2, 2:SEQ], op0=ALU.mult, op1=ALU.add).then_inc(N["cv2"], 1)
                    ahead()
                    dve.wait_ge(N["sg"], f + (h0 + 1))
                    nc.vector.tensor_tensor(h32[:, f2, :], sg[:, f2, :], UP[f2][:, SEQ:2 * SEQ], ALU.mult).then_inc(N["h"], 1)
                    dve.wait_ge(N["hid_hi"], f + (h0 + 1))
                    nc.vector.tensor_tensor(hid_lo[:, f4, :], h32[:, f2, :], hid_hi[:, f4, :].bitcast(F32),
                                            ALU.subtract).then_inc(N["hid_lo"], 1)

                def turn(j):
                    for q in range(6):
                        ahead = lambda: lo(j * 6 + (q + 3) + split, q % RING, q % RING)
                        if q % 3 == 2:
                            ahead()
                        else:
                            f4 = (1 + q - q // 3) % 4
                            post(j * 4 + (1 + q - q // 3), f4 % 2, f4, ahead)

                lo(split + 1, 1, 1)
                post(0, 0, 0, lambda: lo(split + 2, 2, 2))
                with dve.Fori(0, (FT - 2) // 4) as j:
                    turn(j)
                post(FT - 1, 1, 1, (lambda: lo(split + FFN_N, 0, 0)) if more else (lambda: None))

            with dve.Fori(0, DEPTH) as l:
                split = l * A_S
                steps = 0

                def link(ins):
                    nonlocal steps
                    steps += 1
                    ins.then_inc(A["dve"], 1)
                    dve.wait_ge(A["dve"], steps)

                def lo_a(s):
                    n = s if s < A_WIN else s + A_D
                    lo(split + s, s % RING, n % RING, a_width(n))

                lo_a(0)
                rms_norm(A, 0)
                dve.wait_ge(small_in, l * 16 + 16)
                lo_features(A, 0, "g1")
                for c in range(1, A_WIN):
                    lo_a(c)

                def rotate(first, heads, width, table, done):
                    r = CST["cos" + table][1] // TT
                    v = pj[:, :, first:first + heads * width].rearrange("p t (h d) -> p t h d", d=width)
                    x1, x2 = v[:, :, :, 0:r], v[:, :, :, r:2 * r]
                    cos, sin = (const(f + table).rearrange("p (t r) -> p t r", t=TT).unsqueeze(2)
                                .to_broadcast([P, TT, heads, r]) for f in ("cos", "sin"))
                    tmp = [b[:, 0:TT * heads * r].rearrange("p (t h r) -> p t h r", t=TT, h=heads) for b in rot]
                    for out, a, b in zip(tmp, (x1, x2, x2, x1), (cos, sin, cos, sin)):
                        last = nc.vector.tensor_tensor(out, a, b, ALU.mult)
                    link(last)
                    nc.vector.tensor_tensor(x1, tmp[0], tmp[1], ALU.subtract)
                    nc.vector.tensor_tensor(x2, tmp[2], tmp[3], ALU.add).then_inc(done, 1)
                    dve.wait_ge(done, 1)

                dve.wait_ge(A["pj"], A_WIN)
                rotate(COL["iq"], ROT_I, IDX_D, "i", A["rope_i"])
                dve.wait_ge(A["blk"], 2)
                rotate(COL["aq"], ROT_H, HD, "h", A["rope_h"])
                nc.vector.tensor_scalar(ags, pj[:, :, COL["ag"]:COL["ag"] + 15], -80.0, None, ALU.max).then_inc(A["gate"], 1)
                nc.vector.tensor_scalar(iws, pj[:, :, COL["iw"]:COL["iw"] + IDX_H], IDX_H ** -0.5, None, ALU.mult)
                dve.wait_ge(A["blk_ev"], T_KCVC // 2 + 1)
                kcvc = tb[:, T_KCVC, :].rearrange("p (m j) -> p m j", j=CSTR)
                for half in range(CBLK // CSTR):
                    js = slice(half * CSTR, (half + 1) * CSTR)
                    nc.vector.tensor_tensor(rw[:, js, :], kcvc[:, half:half + NCMP, :].rearrange("p m j -> p j m"),
                                            sa("pos")[:, js].unsqueeze(2).to_broadcast([P, CSTR, NCMP]),
                                            ALU.add).then_inc(A["rw"], 1)
                link(nc.vector.memset(vr, 0.0))
                link(nc.vector.memset(pc, 0.0))
                for h in range(IDX_H):
                    dve.wait_ge(A["ix_relu"], h + 1)
                    if h:
                        dve.wait_ge(A["ix_acc"], h)
                    for i, cols in enumerate((slice(0, P), slice(P, CAUS))):
                        if h == 0:
                            last = nc.vector.tensor_scalar(isc[:, cols], relu[:, 0, cols], iws[:, i, 0:1], None, ALU.mult)
                        else:
                            last = nc.vector.scalar_tensor_tensor(out=isc[:, cols], in0=relu[:, h % 2, cols],
                                                                  scalar=iws[:, i, h:h + 1], in1=isc[:, cols],
                                                                  op0=ALU.mult, op1=ALU.add)
                    last.then_inc(A["ix_acc"], 1)
                dve.wait_ge(A["gate_e"], 1)
                link(nc.vector.tensor_scalar(ags, ags, 1.0, None, ALU.add))
                link(nc.vector.reciprocal(ags, ags))
                dve.wait_ge(direct_mm, l * A_D + A_CMP)
                nc.vector.tensor_copy(hb[:, 0, 0, 0:NCMP], G[0][:, 0:NCMP])
                link(nc.vector.tensor_copy(hb[:, 0, 1, 0:NCMP], G[1][:, 0:NCMP]))
                hv = [hb[:, k, :, 0:NCMP] for k in range(4)]
                link(nc.vector.tensor_tensor(hv[1], hv[0], hv[0], ALU.mult))
                link(nc.vector.tensor_scalar(hv[1], hv[1], 0.044715, 1.0, ALU.mult, ALU.add))
                link(nc.vector.tensor_tensor(hv[1], hv[1], hv[0], ALU.mult))
                nc.vector.tensor_scalar(hv[1], hv[1], -50.0, None, ALU.max).then_inc(A["cg"], 1)
                dve.wait_ge(A["cg_e"], 1)
                link(nc.vector.tensor_scalar(hv[2], hv[2], 1.0, None, ALU.add))
                link(nc.vector.reciprocal(hv[2], hv[2]))
                link(nc.vector.tensor_tensor(hv[3], hv[0], hv[2], ALU.mult))
                nc.vector.tensor_copy(vr[:, :, 0:NCMP], hb[:, 3, 1, 0:NCMP].unsqueeze(1).to_broadcast([P, 4, NCMP])
                                      ).then_inc(A["cgel"], 1)
                per_head = lambda name: (const(name).rearrange("p (t n) -> p t n", t=TT).unsqueeze(2)
                                         .to_broadcast([P, TT, NSA_H, NCMP]))
                lcv = lc[:, :, :, 0:NCMP]
                dve.wait_ge(A["cs"], 2)
                for odd in range(2):
                    sc = S[odd][:, 0:TT * 3 * 16].rearrange("p (t h n) -> p t h n", t=TT, h=3)[:, :, 0:3 - odd, 0:NCMP]
                    for i in range(TT):
                        last = nc.vector.scalar_tensor_tensor(out=lcv[:, i, odd::2], in0=sc[:, i], scalar=SCALE,
                                                              in1=per_head("cmp_add")[:, i, odd::2], op0=ALU.mult, op1=ALU.add)
                link(last)
                link(nc.vector.tensor_reduce(mc, lcv, AX.X, ALU.max))
                nc.vector.tensor_tensor(lcv, lcv, mc.unsqueeze(3).to_broadcast([P, TT, NSA_H, NCMP]),
                                        ALU.subtract).then_inc(A["cnm"], 1)
                dve.wait_ge(A["cexp"], 1)
                nc.vector.tensor_tensor(pc[:, :, :, 0:NCMP], lcv, per_head("cmp_keep"), ALU.mult).then_inc(A["cp"], 1)
                dve.wait_ge(A["cp"], 1)
                link(nc.vector.tensor_reduce(dc, pc[:, :, :, 0:NCMP], AX.X, ALU.add))
                link(nc.vector.tensor_scalar(dc, dc, 1e-30, None, ALU.max))
                link(nc.vector.reciprocal(dc, dc))
                gates = ags.rearrange("p t (h g) -> p t h g", g=3)
                link(nc.vector.tensor_tensor(dc, dc, gates[:, :, :, 0], ALU.mult))
                for h in range(NSA_H):
                    dve.wait_ge(A["co"], NSA_H)
                    at = h // 4 * TT * HD
                    nc.vector.tensor_tensor(mix[:, :, h * HD:(h + 1) * HD],
                                            CO[h % 4][:, at:at + TT * HD].rearrange("p (t d) -> p t d", t=TT),
                                            dc[:, :, h].unsqueeze(2).to_broadcast([P, TT, HD]), ALU.mult).then_inc(A["co_ev"], 1)

                def select_keys():
                    TAKEN = -3e38
                    link(nc.vector.tensor_tensor(isc, isc, const("causal"), ALU.add))
                    for _ in range(TOPK // 8):
                        nc.vector.max(m8[:, 0, :], isc[:, 0:P])
                        link(nc.vector.max(m8[:, 1, :], isc[:, P:CAUS]))
                        nc.vector.match_replace(isc[:, 0:P], m8[:, 0, :], isc[:, 0:P], TAKEN)
                        link(nc.vector.match_replace(isc[:, P:CAUS], m8[:, 1, :], isc[:, P:CAUS], TAKEN))
                    link(nc.vector.tensor_scalar(dmask, isc, 0.5 * TAKEN, NEG, ALU.is_gt, ALU.mult))
                    nc.vector.tensor_tensor(dmask, dmask, const("causal"), ALU.add).then_inc(A["dmask"], 1)
                    dve.wait_ge(A["dmask"], 1)

                def logits(u):
                    dve.wait_ge(A["s"], u + 1)
                    if u >= 2:
                        dve.wait_ge(A["e"], u - 1)
                    link(nc.vector.scalar_tensor_tensor(out=lg[:, u % 2, :], in0=S[u % 2][:, 0:CAUS], scalar=SCALE,
                                                        in1=unit(u)[4], op0=ALU.mult, op1=ALU.add))
                    nc.vector.tensor_reduce(nmax[:, u, 0:1], lg[:, u % 2, 0:P], AX.X, ALU.max, negate=True)
                    nc.vector.tensor_reduce(nmax[:, u, 1:2], lg[:, u % 2, P:CAUS], AX.X, ALU.max, negate=True).then_inc(A["nm"], 1)

                def outputs(u):
                    kind, h = UNITS[u]
                    at = unit(u)[5]
                    dve.wait_ge(A["o"], u + 1)
                    if kind == "dil":
                        nc.vector.tensor_copy(mix[:, :, at:at + HD], O[u % 2][:, 0:TT * HD].rearrange("p (t d) -> p t d", t=TT)
                                              ).then_inc(A["o_ev"], 1)
                        return
                    link(nc.vector.reciprocal(rden[:, u % 2, :], den[:, u, :]))
                    f = rden[:, u % 2, :]
                    if kind != "dsa":
                        f = fac[:, u % 2, :]
                        link(nc.vector.tensor_tensor(f, rden[:, u % 2, :], gates[:, :, h, 1 if kind == "slc" else 2], ALU.mult))
                    for i in range(TT):
                        out, o = mix[:, i, at:at + HD], O[u % 2][:, i * HD:(i + 1) * HD]
                        if kind == "dsa":
                            last = nc.vector.tensor_scalar(out, o, f[:, i:i + 1], None, ALU.mult)
                        else:
                            last = nc.vector.scalar_tensor_tensor(out=out, in0=o, scalar=f[:, i:i + 1], in1=out,
                                                                  op0=ALU.mult, op1=ALU.add)
                    last.then_inc(A["o_ev"], 1)

                dve.wait_ge(A["co_ev"], NSA_H)
                for step in range(NU + LAG_V):
                    if step == 4:
                        select_keys()
                    if step < NU:
                        logits(step)
                    if step >= LAG_V:
                        outputs(step - LAG_V)
                dve.wait_ge(A["o_ev"], NU)
                nm = nmax[:, U_DIL:U_DSA, :].rearrange("p (g h) t -> p g (h t)", g=3)
                dn = den[:, U_DIL:U_DSA, :].rearrange("p (g h) t -> p g (h t)", g=3)
                ex, fc = (v.rearrange("p (g h) t -> p g (h t)", g=3) for v in (dexp, dfac))
                low = dmin.rearrange("p h t -> p (h t)")
                link(nc.vector.tensor_tensor(low, nm[:, 0, :], nm[:, 1, :], ALU.min))
                link(nc.vector.tensor_tensor(low, low, nm[:, 2, :], ALU.min))
                spread = low.unsqueeze(1).to_broadcast([P, 3, 2 * TT])
                nc.vector.tensor_tensor(ex, spread, nm, ALU.subtract).then_inc(A["dila"], 1)
                dve.wait_ge(direct_mm, l * A_D + A_D)
                nc.vector.tensor_tensor(mod[:, bass.ds(l, 1), :].rearrange("p o n -> p (o n)"), ADA[:, 0:72], sa("ada_b"),
                                        ALU.add).then_inc(A["ada_ev"], 1)
                dve.wait_ge(A["dila_e"], 1)
                link(nc.vector.tensor_tensor(fc, ex, dn, ALU.mult))
                link(nc.vector.tensor_tensor(low, fc[:, 0, :], fc[:, 1, :], ALU.add))
                link(nc.vector.tensor_tensor(low, low, fc[:, 2, :], ALU.add))
                link(nc.vector.reciprocal(low, low))
                link(nc.vector.tensor_tensor(fc, ex, spread, ALU.mult))
                for i in range(TT):
                    o = mix[:, i, 640:DM].rearrange("p (h d) -> p h d", d=HD)
                    last = nc.vector.tensor_tensor(o, o, dfac[:, :, i].unsqueeze(2).to_broadcast([P, DIL_H, HD]), ALU.mult)
                last.then_inc(A["mix"], 1)
                lo_a(A_WIN)
                lo_features(A, 1, None)
                for c in range(A_WOUT):
                    lo_a(A_WIN + c + 1)
                    dve.wait_ge(chunk_mm, split + (A_WIN + c + 1 + NEW))
                    cols = slice(c * GW, (c + 1) * GW)
                    nc.vector.tensor_tensor(x[:, :, cols], x[:, :, cols], G[c % 2][:, :].rearrange("p (t n) -> p t n", t=TT),
                                            ALU.add).then_inc(A["x"], 1)
                rms_norm(A, 1)
                lo_features(A, 2, "g2")
                ffn(A, split + (A_WIN + A_WOUT), 0, True, 0)
                dve.wait_ge(chunk_mm, split + (A_S + NEW))
                for i in range(TT):
                    for half in range(2):
                        cols = slice(half * 512, half * 512 + 512)
                        last = nc.vector.tensor_tensor(x[:, i, cols], x[:, i, cols], ACC[2 * i + half][:, :], ALU.add)
                dve.drain().then_inc(layer_done, 1)
                dve.wait_ge(layer_go, l + 1)
            normed(FIN, 0)
            for i in range(TT):
                nc.vector.scalar_tensor_tensor(out=x[:, i, :], in0=x[:, i, :], scalar=st[:, 4 + i:5 + i], in1=lnw[:, 0, :],
                                               op0=ALU.mult, op1=ALU.mult).then_inc(FIN["x"], 1)

            def gate_diagonal(sub):
                nc.vector.tensor_tensor(gdiag, ident.unsqueeze(1).to_broadcast([P, KT, P]),
                                        modc(sub, 2).unsqueeze(2).to_broadcast([P, KT, P]), ALU.mult).then_inc(B["gdiag"], 1)

            def modulate(v, sub):
                def low(k):
                    dve.wait_ge(B["tp_hi"], v * KT + k + 1)
                    nc.vector.tensor_tensor(hT_lo[:, k, :], hx[:, k % 2, :], hT_hi[:, k, :].bitcast(F32),
                                            ALU.subtract).then_inc(B["tp_lo"], 1)

                for k in range(KT):
                    dve.wait_ge(B["tp"], v * KT + k + 1)
                    nc.vector.tensor_scalar(hx[:, k % 2, :], TP[k % 2][:, 0:SEQ], modc(sub, 1)[:, k:k + 1],
                                            modc(sub, 0)[:, k:k + 1], ALU.mult, ALU.add).then_inc(B["tp_mod"], 1)
                    if k:
                        low(k - 1)
                low(KT - 1)

            dve.wait_ge(FIN["x"], TT)
            with dve.Fori(0, DEPTH) as l:
                split = l * B_N + S_A
                steps = 0

                def link(ins):
                    nonlocal steps
                    steps += 1
                    ins.then_inc(B["dve"], 1)
                    dve.wait_ge(B["dve"], steps)

                def lo_b(s):
                    lo(split + s, s % RING, s % RING, b_width(s))

                def layer_norm(sub, read):
                    for i in range(TT):
                        for half in range(2):
                            cols = slice(half * 512, half * 512 + 512)
                            for k, (xc, y) in enumerate(read(i, half)):
                                n = xc.stop - xc.start
                                pc_ = part[:, half, k * n:(k + 1) * n]
                                link(nc.vector.tensor_tensor(pc_, y, gateb[:, xc], ALU.mult))
                            link(nc.vector.scalar_tensor_tensor(out=x[:, i, cols], in0=x[:, i, cols], scalar=ALPHA,
                                                                in1=part[:, half, :], op0=ALU.mult, op1=ALU.add))
                            link(nc.vector.bn_stats(bst[:, i, half, :], x[:, i, cols]))
                        last = nc.vector.bn_aggr(bag[:, i, :], bst[:, i, :, :].rearrange("p a b -> p (a b)"))
                    last.then_inc(B["std"], 1)
                    dve.wait_ge(B["std"], 2 * sub + 2)
                    link(nc.vector.reciprocal(st[:, 10:12], st[:, 8:10]))
                    dve.wait_ge(ln_in, l * 96 + 32 * (sub + 1))
                    for i in range(TT):
                        link(nc.vector.tensor_scalar(x[:, i, :], x[:, i, :], bag[:, i, 0:1], st[:, 10 + i:11 + i],
                                                     ALU.subtract, ALU.mult))
                        link(nc.vector.tensor_tensor(x[:, i, :], x[:, i, :], lnw[:, 0, :], ALU.mult))
                        last = nc.vector.tensor_tensor(x[:, i, :], x[:, i, :], lnw[:, 1, :], ALU.add)
                        if i == 0:
                            link(last)
                    last.then_inc(B["ln"], 1)
                    dve.wait_ge(B["ln"], sub + 1)

                def from_down(i, half):
                    yield slice(half * 512, half * 512 + 512), ACC[2 * i + half][:, :]

                def from_wout(i, half):
                    for c in range(2):
                        yield (slice(half * 512 + c * GW, half * 512 + (c + 1) * GW),
                               ACC[2 * half + c][:, i * GW:(i + 1) * GW])

                lo_b(0)
                link(nc.vector.tensor_copy(modl[:, :], mod[:, bass.ds(l, 1), :].rearrange("p o n -> p (o n)")))
                by_kind = modl[:, :].rearrange("p (s w n) -> p s w n", s=3, w=3)
                link(nc.vector.tensor_scalar(by_kind[:, :, 1:3, :], by_kind[:, :, 1:3, :], 1.0, None, ALU.add))
                link(nc.vector.tensor_scalar(by_kind[:, 0:3:2, 2, :], by_kind[:, 0:3:2, 2, :], 0.5, None, ALU.mult))
                gate_diagonal(0)
                modulate(0, 0)
                ffn(B, split, 0, False, 2)
                dve.wait_ge(chunk_mm, split + (FFN_N + NEW))
                layer_norm(0, from_down)
                gate_diagonal(1)
                modulate(1, 1)

                dve.wait_ge(small_in, l * 16 + (DEPTH * 16 + 16))
                ntap = 0
                for c, (ftiles, _, _) in enumerate(B_WIN):
                    lo_b(B_S0["win"] + c + 1)
                    if not ftiles or ftiles[0] not in F_CONV:
                        continue
                    ntap += len(ftiles)
                    dve.wait_ge(B["tap"], ntap)
                    if c and B_WIN[c][2]:
                        dve.wait_ge(B["tm"], 1)
                    for d in range(1, TAPS):
                        for k, f in enumerate(ftiles):
                            last = nc.vector.scalar_tensor_tensor(
                                out=cvb[:, c % 2, k, d:SEQ], in0=G[c % 2][:, k * SEQ:(k + 1) * SEQ - d], scalar=tap(f, TAPS - 1 - d),
                                in1=cvb[:, c % 2, k, d:SEQ], op0=ALU.mult, op1=ALU.add)
                        if d < TAPS - 1:
                            link(last)
                    last.then_inc(B["conv"], 1)
                dve.wait_ge(B["tm"], 8)
                link(nc.vector.tensor_tensor(gt, tm[:, :, GT:GT + 24], sbp("gate_bias").unsqueeze(1).to_broadcast([P, TT, 24]), ALU.add))
                nc.vector.tensor_scalar(sig, gt[:, :, 12:18], -80.0, None, ALU.max)
                nc.vector.scalar_tensor_tensor(out=ga, in0=gt[:, :, 0:12], scalar=-1.0, in1=gt[:, :, 0:12], op0=ALU.mult,
                                               op1=ALU.max).then_inc(B["gt"], 1)
                dve.wait_ge(B["gln"], 1)
                link(nc.vector.scalar_tensor_tensor(out=gl[:, :, 0:6], in0=gt[:, :, 0:6], scalar=0.0, in1=gl1[:, :, 0:6],
                                                    op0=ALU.max, op1=ALU.add))
                link(nc.vector.scalar_tensor_tensor(out=gl[:, :, 0:6], in0=gl[:, :, 0:6], scalar=-1.0,
                                                    in1=ealog.unsqueeze(1).to_broadcast([P, TT, 6]), op0=ALU.mult, op1=ALU.mult))
                nc.vector.scalar_tensor_tensor(out=gl[:, :, 6:12], in0=gt[:, :, 6:12], scalar=0.0, in1=gl1[:, :, 6:12],
                                               op0=ALU.min, op1=ALU.subtract).then_inc(B["gl"], 1)
                link(nc.vector.tensor_scalar(beta, beta, 1.0, None, ALU.add))
                link(nc.vector.reciprocal(beta, beta))
                dve.wait_ge(B["cum"], 1)
                link(nc.vector.tensor_copy(cg, S[0][:, 0:24].rearrange("p (t n) -> p t n", t=TT)))
                nc.vector.tensor_copy(ngr[:, :, 0:6], cg[:, :, 0:6])
                nc.vector.tensor_scalar(negG, cg[:, :, 0:6], -1.0, None, ALU.mult)
                nc.vector.tensor_tensor(ngr[:, :, 6:12], gt[:, :, 18:24], cg[:, :, 6:12], ALU.subtract).then_inc(B["cg"], 1)
                dve.wait_ge(B["rows_ev"], 4)
                nc.vector.tensor_tensor_scan(row_m[0:6, :], row_f[0:6, :], row_i[0:6, :], 0.0, ALU.add, ALU.max).then_inc(B["scan"], 1)
                dve.wait_ge(B["ssr"], 1)
                nc.vector.reciprocal(norm_r[0:12, :], norm_r[0:12, :]).then_inc(B["rn"], 1)
                dve.wait_ge(B["mback"], 1)
                nc.vector.tensor_tensor(bm, cg[:, :, 6:12], S[1][:, 0:12].rearrange("p (t h) -> p t h", t=TT),
                                        ALU.subtract).then_inc(B["bm"], 1)
                for f in range(3):
                    dve.wait_ge(B["rnb"], f + 1)
                    qk = fm[:, 2 * f:2 * f + 2, :]
                    nc.vector.tensor_tensor(qk, qk, G[f % 2][:, :].rearrange("p (k n) -> p k n", k=2), ALU.mult).then_inc(B["rnb_ev"], 1)
                dve.wait_ge(B["rnb_ev"], 3)
                dve.wait_ge(B["bb"], 1)
                for f in range(3):
                    bank, at = (O[1], f * SEQ) if f < 2 else (O[0], 0)
                    nc.vector.tensor_tensor(kbT[:, f, :], fm[:, F_GK + f, :], bank[:, at:at + SEQ], ALU.mult).then_inc(B["kb"], 1)
                for i in range(TT):
                    dve.wait_ge(B["vt"], i + 1)
                    nc.vector.tensor_tensor(vb[:, i, :, :], PT[i][:, 0:384].rearrange("p (h d) -> p h d", d=HD),
                                            beta[:, i, :].unsqueeze(2).to_broadcast([P, GDN_H, HD]), ALU.mult).then_inc(B["vb"], 1)

                def logits_b(u):
                    kind, h = B_UNITS[u]
                    dve.wait_ge(B["s"], u + 1)
                    if u >= 2:
                        dve.wait_ge(B["e"], u - 1)
                    if kind == "moba":
                        ins = nc.vector.scalar_tensor_tensor(out=lgb[:, u % 2, :], in0=S[u % 2][:, 0:CAUS], scalar=SCALE,
                                                             in1=const("causal"), op0=ALU.mult, op1=ALU.add)
                        ins.then_inc(B["s_free"], 1)
                        dve.wait_ge(B["s_free"], u + 1)
                        nc.vector.tensor_reduce(nmaxb[:, u, 0:1], lgb[:, u % 2, 0:P], AX.X, ALU.max, negate=True)
                        nc.vector.tensor_reduce(nmaxb[:, u, 1:2], lgb[:, u % 2, P:CAUS], AX.X, ALU.max, negate=True).then_inc(B["nm"], 1)
                    else:
                        nc.vector.tensor_tensor(lgb[:, u % 2, 0:P], G[u % 2][:, 0:P], const("causal")[:, 0:P], ALU.add)
                        nc.vector.tensor_tensor(lgb[:, u % 2, P:CAUS], G[u % 2][:, 0:SEQ], const("causal")[:, P:CAUS],
                                                ALU.add).then_inc(B["nm"], 1)

                def weigh(u):
                    if not 0 <= u < NUB or B_UNITS[u][0] != "mlstm":
                        return
                    dve.wait_ge(B["e"], u + 1)
                    for i, cols in enumerate((slice(0, P), slice(P, CAUS))):
                        last = nc.vector.scalar_tensor_tensor(out=prb[:, u % 2, cols], in0=S[u % 2][:, cols], scalar=SCALE,
                                                              in1=prb[:, u % 2, cols], op0=ALU.mult, op1=ALU.mult,
                                                              accum_out=denb[:, u, i:i + 1])
                    last.then_inc(B["p"], 1)

                def outputs_b(u):
                    kind, h = B_UNITS[u]
                    dve.wait_ge(B["o"], u + 1)
                    o = O[u % 2][:, 0:TT * HD].rearrange("p (t d) -> p t d", t=TT)
                    if kind == "moba":
                        link(nc.vector.reciprocal(rdenb[:, u % 2, :], denb[:, u, :]))
                        nc.vector.tensor_tensor(mixb[:, :, 384 + h * HD:384 + (h + 1) * HD], o,
                                                rdenb[:, u % 2, :].unsqueeze(2).to_broadcast([P, TT, HD]), ALU.mult).then_inc(B["o_ev"], 1)
                    else:
                        nc.vector.tensor_copy(mixb[:, :, 640 + h * HD:640 + (h + 1) * HD], o).then_inc(B["o_ev"], 1)

                dve.wait_ge(B["rows_ev"], 4)
                for step in range(NUB + B_LAGV):
                    if step < NUB:
                        logits_b(step)
                    weigh(step - B_LAGP)
                    if step >= B_LAGV:
                        outputs_b(step - B_LAGV)

                def delta_products(h):
                    dve.wait_ge(B["dec"], h + 1)
                    nc.vector.scalar_tensor_tensor(out=attnT[:, h, :], in0=S[h % 2][:, 0:CAUS], scalar=SCALE, in1=dec[h % 2],
                                                   op0=ALU.mult, op1=ALU.mult)
                    nc.vector.tensor_tensor(sysT[:, h, :], PT[h % 2][:, 0:CAUS], dec[h % 2], ALU.mult).then_inc(B["dmul"], 1)

                for k in range(2):
                    last = nc.vector.tensor_copy(xx[:, :, k, :], ident.unsqueeze(1).to_broadcast([P, 2 * GDN_H, P]))
                last.then_inc(B["xinit"], 1)
                for h in range(GDN_H):
                    dve.wait_ge(B["ds"], h + 1)
                    if h >= 2:
                        dve.wait_ge(B["dmul"], h - 1)
                    nc.vector.tensor_tensor(dec[h % 2][:, 0:SEQ], G[h % 2][:, 0:SEQ], const("causalT")[:, 0:SEQ], ALU.add)
                    nc.vector.tensor_tensor(dec[h % 2][:, SEQ:CAUS], G[h % 2][:, P:SEQ], const("causalT")[:, SEQ:CAUS],
                                            ALU.add).then_inc(B["dl"], 1)
                    if h:
                        delta_products(h - 1)
                delta_products(GDN_H - 1)
                dve.wait_ge(B["xinit"], 1)
                for n in range(7 * 2 * GDN_H):
                    dve.wait_ge(B["z"], n + 1)
                    v = xx[:, n % (2 * GDN_H), :, :]
                    nc.vector.tensor_tensor(v, v, ps[4 + n % 4][:, 0:SEQ].rearrange("p (k n) -> p k n", k=2),
                                            ALU.subtract).then_inc(B["xx"], 1)
                dve.wait_ge(B["u"], 2)
                vb1 = vb[:, 1, :, :].rearrange("p h d -> p (h d)")
                nc.vector.tensor_tensor(vb1, vb1, ps[1][:, 0:384], ALU.subtract).then_inc(B["w1"], 1)

                heads = lambda v: v.rearrange("p t (h d) -> p t h d", d=HD)
                wide = lambda v: v.unsqueeze(3).to_broadcast([P, TT, 6, HD])
                hc = heads(mixb[:, :, 640:DM])
                dn = denb[:, MOBA_H:NUB, :].rearrange("p h t -> p t h")
                link(nc.vector.scalar_tensor_tensor(out=hst2, in0=dn, scalar=-1.0, in1=dn, op0=ALU.mult, op1=ALU.max))
                link(nc.vector.tensor_tensor(hst2, hst2, em, ALU.max))
                link(nc.vector.reciprocal(hst2, hst2))
                link(nc.vector.tensor_tensor(hc, hc, wide(hst2), ALU.mult))
                dve.wait_ge(B["act"], 2)
                link(nc.vector.tensor_tensor(hc, hc, heads(tm[:, :, OC:OC + 384]), ALU.mult))
                link(nc.vector.tensor_reduce(hst2, hc, AX.X, ALU.add))
                link(nc.vector.tensor_scalar(hst2, hst2, 1.0 / HD, None, ALU.mult))
                link(nc.vector.tensor_tensor(hc, hc, wide(hst2), ALU.subtract))
                dve.wait_ge(B["u"], 3)
                link(nc.vector.tensor_tensor(heads(sq3), hc, hc, ALU.mult))
                nc.vector.tensor_reduce(hst3, heads(sq3), AX.X, ALU.add).then_inc(B["lvar"], 1)
                dve.wait_ge(B["gsq"], 2)
                nc.vector.tensor_reduce(hst, heads(sq2), AX.X, ALU.add).then_inc(B["gms"], 1)
                dve.wait_ge(B["grs"], 1)
                link(nc.vector.reciprocal(hst, hst))
                oa = heads(mixb[:, :, 0:384])
                for i in range(TT):
                    last = nc.vector.tensor_tensor(oa[:, i], ps[3 + i][:, 0:384].rearrange("p (h d) -> p h d", d=HD),
                                                   hst[:, i, :].unsqueeze(2).to_broadcast([P, 6, HD]), ALU.mult)
                link(last)
                link(nc.vector.tensor_tensor(oa, oa, sbp("gdn_norm").unsqueeze(1).unsqueeze(1).to_broadcast([P, TT, 6, HD]), ALU.mult))
                nc.vector.tensor_tensor(mixb[:, :, 0:384], mixb[:, :, 0:384], tm[:, :, ZC:ZC + 384], ALU.mult)
                dve.wait_ge(B["lrs"], 1)
                link(nc.vector.reciprocal(hst3, hst3))
                link(nc.vector.tensor_tensor(hc, hc, wide(hst3), ALU.mult))
                nc.vector.tensor_tensor(mixb[:, :, 640:DM], mixb[:, :, 640:DM],
                                        sbp("ml_norm").unsqueeze(1).to_broadcast([P, TT, 384]), ALU.mult).then_inc(B["mix"], 1)
                lo_features(B, 2, None)
                for c in range(B_WOUT):
                    lo_b(B_S0["wout"] + c + 1)
                dve.wait_ge(chunk_mm, split + (B_S0["ffn1"] + NEW))
                layer_norm(1, from_wout)
                gate_diagonal(2)
                modulate(3, 2)
                ffn(B, split + B_S0["ffn1"], FT, False, 0)
                dve.wait_ge(chunk_mm, split + (B_N + NEW))
                layer_norm(2, from_down)
                dve.drain().then_inc(layer_done, 1)
                dve.wait_ge(layer_go, l + (DEPTH + 1))
    return nc


def pack_first(inputs):
    f = lambda n: np.asarray(inputs[n], np.float32)
    wa = np.zeros((DEPTH, A_N, P, CW), np.float32)
    w_in, w1, ada, w_out, w_up, w_down = f("w_in"), f("cmp_w1"), f("ada_w_2"), f("w_out"), f("w_up"), f("w_down")
    tiles = lambda a: a.reshape(KT, P, -1).transpose(1, 0, 2)
    order = np.concatenate([np.arange(SRC[n][0], SRC[n][0] + SRC[n][1]) for n in COL])
    for l in range(DEPTH):
        w = np.zeros((DM, PJW), np.float32)
        w[:, :D_IN] = w_in[l][:, order]
        for c, width in enumerate(WIN_A):
            wa[l, c, :, :KT * width] = tiles(w[:, c * GW:c * GW + width]).reshape(P, -1)
        cmp1 = w1[l].reshape(2, CBLK, HD, P).transpose(0, 2, 1, 3).reshape(P, CBLK * P)
        at = 0
        for n in range(A_N0["cmp"], A_N0["ada"]):
            wa[l, n, :, :a_width(n)] = cmp1[:, at:at + a_width(n)]
            at += a_width(n)
        for d in range(A_ADA):
            a = tiles(ada[l][:, d * 256:(d + 1) * 256]).reshape(P, KT, 2, P).transpose(0, 2, 1, 3)
            wa[l, A_N0["ada"] + d] = a.reshape(P, CW)
        for c in range(A_WOUT):
            wa[l, A_N0["wout"] + c] = tiles(w_out[l][:, c * GW:(c + 1) * GW]).reshape(P, CW)
        wa[l, A_N0["ffn"]:] = pack_ffn(w_up[l], w_down[l])
    sa = np.zeros((DEPTH, P, SA_W), np.float32)
    col = lambda v: v.reshape(-1, P).T
    for l in range(DEPTH):
        def put(name, a):
            at, w = SA[name]
            sa[l, :, at:at + w] = a.reshape(P, w)
        put("g1", col(f("norm1_g")[l]))
        put("g2", col(f("norm2_g")[l]))
        taps = np.concatenate([f("conv_w")[l], f("conv_b")[l][None]], 0)
        put("conv", taps.reshape(4, FT, P).transpose(2, 1, 0))
        put("pos", f("cmp_pos")[l].transpose(0, 2, 1).reshape(P, CBLK))
        w2 = f("cmp_w2")[l]
        put("w2k", np.concatenate([w2[0], w2[0]], 1))
        put("w2v", w2[1])
        put("ada_b", col(f("ada_b_2")[l]))
    return {"wa": wa, "sa": sa, "const": CONST, "x": f("x"), "c": np.ascontiguousarray(col(f("c_2")[0])),
            "final_g": f("final_g")}


def pack_second(inputs):
    f = lambda n: np.asarray(inputs[n + "_2"], np.float32)
    w13, w2, w_in, w_out = f("ffn_w13"), f("ffn_w2"), f("w_in"), f("w_out")
    tiles = lambda a: a.reshape(KT, P, -1).transpose(1, 0, 2)
    r = np.arange
    feat = np.concatenate([r(0, 1152), r(2316, 3084), r(1548, 2060)])
    tok = np.concatenate([r(1164, 1548), r(2060, 2316), r(3084, 3468), r(3480, 3864),
                          r(1152, 1158), r(3474, 3480), r(1158, 1164), r(3468, 3474)])
    wb = np.zeros((DEPTH, B_N, P, CW), np.float32)
    sb = np.zeros((DEPTH, P, SB_W), np.float32)
    for l in range(DEPTH):
        wb[l, :FFN_N] = pack_ffn(w13[l, 0], w2[l, 0])
        wb[l, B_S0["ffn1"]:] = pack_ffn(w13[l, 1], w2[l, 1])
        for c, (ftiles, at, width) in enumerate(B_WIN):
            cols = np.concatenate([feat[P * k:P * (k + 1)] for k in ftiles] + [tok[at:at + width]]).astype(int)
            wb[l, B_S0["win"] + c, :, :KT * len(cols)] = tiles(w_in[l][:, cols]).reshape(P, -1)
        for c in range(B_WOUT):
            wb[l, B_S0["wout"] + c] = tiles(w_out[l][:, c * GW:(c + 1) * GW]).reshape(P, CW)

        def put(name, a):
            at, w = SB[name]
            sb[l, :, at:at + w] = a.reshape(-1, w) if a.ndim == 1 else a.reshape(P, w)
        taps = np.concatenate([f("gdn_conv")[l], f("mlstm_conv")[l]], 1)
        put("conv", taps.reshape(TAPS, 15, P).transpose(2, 1, 0))
        put("gate_bias", np.concatenate([f("gdn_dt_bias")[l], f("mlstm_f_bias")[l], np.zeros(6, np.float32), f("mlstm_i_bias")[l]]))
        put("a_log", f("gdn_a_log")[l])
        put("gdn_norm", f("gdn_norm")[l])
        put("ml_norm", f("mlstm_norm")[l])
    return {"wb": wb, "sb": sb, "ln_g": f("ln_g"), "ln_b": f("ln_b")}


def pack_ffn(up, down):
    out = np.zeros((FFN_N, P, CW), np.float32)
    u = up.reshape(KT, P, 2, FT, P)
    for f in range(FT):
        pos = 0 if f == 0 else 1 + 3 * ((f - 1) // 2) + (f - 1) % 2
        out[pos] = u[:, :, :, f, :].transpose(1, 0, 2, 3).reshape(P, CW)
    d = down.reshape(FT // 2, 2, P, DM)
    for i in range(FT // 2):
        pos = 3 + 3 * i if i < FT // 2 - 1 else FFN_N - 1
        out[pos] = d[i].transpose(1, 0, 2).reshape(P, CW)
    return out


def kernel(**inputs):
    import concourse.bacc as bacc
    from concourse.bass_utils import run_bass_kernel_spmd

    nc = bacc.Bacc("TRN2", target_bir_lowering=False, num_devices=1)
    arrays, tensors = {}, {}
    for name, a in {**pack_first(inputs), **pack_second(inputs)}.items():
        arrays["in_" + name] = np.ascontiguousarray(a)
        tensors[name] = nc.dram_tensor("in_" + name, a.shape, F32, kind="ExternalInput").ap()
    tensors["out"] = nc.dram_tensor("out", (1, SEQ, DM), F32, kind="ExternalOutput").ap()
    build(nc, tensors)
    return run_bass_kernel_spmd(nc, [arrays], core_ids=[0]).results[0]["out"]
```

```python
from contextlib import ExitStack

import numpy as np

import concourse.bass as bass
from concourse import mybir

F32 = mybir.dt.float32
F32R = mybir.dt.float32r
ACT = mybir.ActivationFunctionType
ALU = mybir.AluOpType
AX = mybir.AxisListType

P = 128
SEQ, DM, DEPTH = 256, 1024, 2
TT = SEQ // P
KT = DM // P
HD = 64
SCALE = HD ** -0.5
NEG = -1e30
DFF = 2816
FT = DFF // P
NORM_EPS, LN_EPS = 1e-6, 1e-5
ALPHA = (2 * DEPTH) ** 0.25
CW = 2048
RING = 3
CAUS = P + SEQ

NSA_H, DSA_H, DIL_H, IDX_H, IDX_D = 5, 5, 6, 8, 32
SRC = {}
_o = 0
for _n, _w in (("aq", 320), ("kc", 64), ("vc", 64), ("ks", 64), ("vs", 64), ("kw", 64), ("vw", 64), ("ag", 15),
               ("bq", 320), ("bk", 64), ("bv", 64), ("iq", 256), ("ik", 32), ("iw", 8),
               ("cq", 384), ("ck", 384), ("cv", 384)):
    SRC[_n] = (_o, _w)
    _o += _w
D_IN = _o
COL = {}
_o = 0
for _n in ("aq", "ks", "kw", "bq", "bk", "cq", "ck", "iq", "ik", "kc", "vc", "vs", "vw", "bv", "cv", "ag", "iw"):
    COL[_n] = _o
    _o += SRC[_n][1]
ROT_H = 25
ROT_I = IDX_H + 1
GW = 256
PJW = D_IN + D_IN % 2
WIN_A = [min(GW, PJW - c) for c in range(0, PJW, GW)]
NCMP, CBLK, CSTR = 15, 32, 16
TOPK = SEQ // 4

A_WIN, A_CMP, A_WOUT, FFN_N = len(WIN_A), 3, 4, 33
MOD = 9 * KT
MOD2 = MOD // 2
ADA_N = MOD2 // 2
ADA_T = ADA_N // RING
A_N0 = {"win": 0, "cmp": A_WIN, "wout": A_WIN + A_CMP}
A_N0["ffn"] = A_N0["wout"] + A_WOUT
A_N = A_N0["ffn"] + FFN_N
A_S = A_WIN + A_WOUT + FFN_N
A_D = A_CMP
assert A_N % RING == 0 and A_S % RING == 0 and A_N0["ffn"] % RING == 0 and (A_WIN + A_WOUT) % RING == 0

TB = [("aq", 0, 128, 1), ("aq", 128, 128, 1), ("aq", 256, 128, 1), ("kc", 0, 128, 1),
      ("iq", 0, 128, 1), ("iq", 128, 128, 1), ("ik", 0, 32, 4), ("bk", 0, 64, 2),
      ("bq", 0, 128, 1), ("bq", 128, 128, 1), ("bq", 256, 128, 1), ("ks", 0, 64, 2), ("kw", 0, 64, 2),
      ("aq", 0, 128, 1), ("aq", 128, 128, 1), ("aq", 256, 128, 1),
      ("cq", 0, 128, 1), ("cq", 128, 128, 1), ("cq", 256, 128, 1),
      ("ck", 0, 128, 1), ("ck", 128, 128, 1), ("ck", 256, 128, 1)]
T_AQR, T_KCVC, T_IQ, T_IK, T_BK, T_BQ, T_KS, T_KW, T_AQ, T_CQ, T_CK = 0, 3, 4, 6, 7, 8, 11, 12, 13, 16, 19

CST = {}


def _constants():
    parts, at = [], 0

    def put(name, a):
        nonlocal at
        a = np.asarray(a, np.float32).reshape(a.shape[0], -1)
        if a.shape[0] < P:
            a = np.concatenate([a, np.zeros((P - a.shape[0], a.shape[1]), np.float32)])
        CST[name] = (at, a.shape[1])
        parts.append(a)
        at += a.shape[1]

    i, j = np.arange(P)[:, None], np.arange(P)[None, :]
    put("ident", np.eye(P))
    put("ones", np.ones((P, P)))
    put("upto", (i <= j).astype(np.float32))
    add = lambda ok: np.where(ok, 0.0, NEG)
    full = np.ones((P, P), bool)
    put("causal", np.concatenate([add(j <= i), add(full), add(j <= i)], 1))
    put("causalT", np.concatenate([add(i <= j), add(full), add(i <= j)], 1))
    put("dil0", np.concatenate([add(j <= i), add(j >= i), add(j <= i)], 1))
    for g, r in ((1, 4), (2, 16)):
        step = (i - j) % r == 0
        put(f"dil{g}", np.concatenate([add((j <= i) & step), add(step), add((j <= i) & step)], 1))
    t = np.arange(SEQ).reshape(TT, P).T[:, :, None]
    ok = (np.arange(NCMP) * CSTR + CBLK - 1)[None, None, :] <= t
    put("cmp_add", add(ok))
    put("cmp_keep", ok.astype(np.float32))
    for name, rot in (("h", 16), ("i", 8)):
        inv = 1.0 / (500000.0 ** (np.arange(0, rot, 2, dtype=np.float32) / np.float32(rot)))
        ang = np.arange(SEQ, dtype=np.float32)[:, None] * inv[None, :].astype(np.float32)
        for f, fn in (("cos", np.cos), ("sin", np.sin)):
            put(f + name, fn(ang).astype(np.float32).reshape(TT, P, rot // 2).transpose(1, 0, 2))
    for b in range(7):
        s = 1 << b
        put(f"lev{b}", ((i // (2 * s) == j // (2 * s)) & (j % (2 * s) >= s) & (i % (2 * s) < s)).astype(np.float32))
    put("pair_of", (i // 64 == np.arange(2)[None, :]).astype(np.float32))
    put("quad_of", (i // 32 == np.arange(4)[None, :]).astype(np.float32))
    pair = np.zeros((6, 3, P), np.float32)
    for h in range(6):
        pair[h, h // 2, 64 * (h % 2):64 * (h % 2) + 64] = 1
    put("pair", pair)
    pair12 = np.zeros((12, 6, P), np.float32)
    for h in range(12):
        pair12[h, h // 2, 64 * (h % 2):64 * (h % 2) + 64] = 1
    put("pair12", pair12)
    half = np.zeros((P, 6, 12), np.float32)
    for f in range(6):
        half[:64, f, 2 * f] = 1
        half[64:, f, 2 * f + 1] = 1
    put("half", half)
    return np.ascontiguousarray(np.concatenate(parts, 1))


CONST = _constants()


def a_chunk(n):
    if n < A_N0["cmp"]:
        return "split", n
    if n < A_N0["wout"]:
        return "direct", n - A_N0["cmp"]
    return "split", n - A_D


def a_width(n):
    if n < A_WIN:
        return KT * WIN_A[n]
    return {A_N0["cmp"] + 1: CW // 2, A_N0["cmp"] + 2: CW // 2}.get(n, CW)


def _columns(*names):
    at, out = 0, {}
    for n, w in names:
        out[n] = (at, w)
        at += w
    return out, at


SA, SA_W = _columns(("g1", KT), ("g2", KT), ("conv", FT * 4), ("pos", CBLK), ("w2k", P), ("w2v", HD), ("ada_b", MOD2))


GDN_H, MOBA_H, ML_H = 6, 4, 6
TAPS = 4
F_GQ, F_GK, F_GV, F_LQ, F_LK, F_MQ, F_MK, F_N = 0, 3, 6, 9, 12, 15, 17, 19
F_CONV = list(range(F_MQ))
ZC, VB, VC, OC, TMW = 0, 384, 640, 1024, 1408
GATES = 24
B_WIN = ([((), 0, 0)] + [((f, f + 1), 0, 0) for f in range(0, 14, 2)] + [((14,), 0, 0), ((15, 16), 0, 0), ((17, 18), 0, 0)]
         + [((), 0, P)] + [((), c, GW) for c in range(P, TMW, GW)])
N_FEAT, N_TOK = len([b for b in B_WIN if b[0]]), len([b for b in B_WIN if b[2]])
B_WOUT = 4
B_S0 = {"ffn0": 0, "win": FFN_N, "wout": FFN_N + len(B_WIN)}
B_S0["ffn1"] = B_S0["wout"] + B_WOUT
B_N = B_S0["ffn1"] + FFN_N
assert B_N % RING == 0 and B_S0["ffn1"] % RING == 0
SB, SB_W = _columns(("conv", 15 * TAPS), ("gate_bias", 24), ("a_log", GDN_H), ("gdn_norm", HD), ("ml_norm", ML_H * HD),
                      ("ada_b", MOD2), ("ln_g", 2 * KT), ("ln_b", 2 * KT))


def b_width(n):
    if B_S0["win"] <= n < B_S0["wout"]:
        f, _, w = B_WIN[n - B_S0["win"]]
        return KT * (P * len(f) + w or GATES)
    return CW


def build(nc, t, only_first=False):
    with ExitStack() as ctx:
        def sb(name, shape, dt=F32):
            return ctx.enter_context(nc.sbuf_tensor(name, shape, dt))

        def sem(name):
            return ctx.enter_context(nc.semaphore(name))

        raw = sb("raw", [P, RING, CW])
        w_hi = sb("w_hi", [P, RING, CW], F32R)
        w_lo = sb("w_lo", [P, RING, CW], F32R)
        x = sb("x", [P, TT, DM])
        hT_hi = sb("hT_hi", [P, KT, SEQ], F32R)
        hT_lo = sb("hT_lo", [P, KT, SEQ], F32R)
        hid_hi = sb("hid_hi", [P, 4, SEQ], F32R)
        hid_lo = sb("hid_lo", [P, 4, SEQ], F32R)
        cst = sb("cst", [P, CONST.shape[1]])
        spa = sb("spa", [P, max(SA_W, SB_W)])
        moda = sb("moda", [P, MOD2])
        mod = sb("mod", [P, DEPTH, MOD2])
        modl = sb("modl", [P, MOD])
        gateb = sb("gateb", [P, DM])
        lnw = sb("lnw", [P, 2, DM])
        st = sb("st", [P, 32])
        SCR = 18000
        scratch = sb("scratch", [P, SCR])

        def carver():
            at = 0

            def carve(*dims):
                nonlocal at
                n = int(np.prod(dims))
                v = scratch[:, at:at + n]
                at += n
                assert at <= SCR, at
                if len(dims) == 1:
                    return v
                names = "abcd"[:len(dims)]
                return v.rearrange(f"p ({' '.join(names)}) -> p {' '.join(names)}", **dict(zip(names, dims)))
            return carve

        carve = carver()
        xn, junk = carve(TT, DM), carve(TT, DM)
        carve = carver()
        cv, sg, h32 = carve(2, SEQ), carve(2, SEQ), carve(2, SEQ)
        ada_raw = scratch[:, SCR - RING * CW:SCR].rearrange("p (r n) -> p r n", r=RING)
        cb = scratch[:, SCR - RING * CW - DM:SCR - RING * CW]
        carve = carver()
        pj, tb = carve(TT, PJW), carve(len(TB), SEQ)
        lg, pr, pt = carve(2, CAUS), carve(2, CAUS), carve(2, CAUS)
        mix = carve(TT, DM)
        relu, isc, dmask = carve(2, CAUS), carve(CAUS), carve(CAUS)
        iws, ags, fac = carve(TT, IDX_H), carve(TT, 15), carve(2, TT)
        den, nmax, rden = carve(21, TT), carve(21, TT), carve(2, TT)
        m8, dmin, dexp, dfac = carve(2, 8), carve(2, TT), carve(6, TT), carve(6, TT)
        lc, mc, dc, pc = carve(TT, NSA_H, 16), carve(TT, NSA_H), carve(TT, NSA_H), carve(TT, NSA_H, 32)
        vr, hb = carve(4, 32), carve(4, 2 * NCMP)
        flat = lambda v: v.rearrange("p a b -> p (a b)")
        lent = [gateb[:, :], lnw[:, 1, :]]
        rw = lent[0][:, 0:CBLK * 2 * NCMP].rearrange("p (j n) -> p j n", n=2 * NCMP)
        pcT, pcT4 = (lent[1][:, SEQ * k:SEQ * (k + 1)].rearrange("p (t n) -> p t n", t=TT) for k in range(2))
        vbd = lent[1][:, 2 * SEQ:3 * SEQ].rearrange("p (h d) -> p h d", d=HD)
        kbd = lent[1][:, 3 * SEQ:3 * SEQ + 32].rearrange("p (h n) -> p h n", h=2)
        dup = scratch[:, TT * PJW + len(TB) * SEQ + 2 * CAUS:TT * PJW + len(TB) * SEQ + 2 * CAUS + TT * 4 * P].rearrange("p (t k n) -> p t k n", t=TT, k=4)
        DUP = [k for k, b in enumerate(TB) if b[3] > 1]
        rot = [flat(mix)[:, 512 * k:512 * k + 400] for k in range(4)]

        carve = carver()
        carve(6 * SEQ)
        gdiag, hx, part = carve(KT, P), carve(4, SEQ), carve(2, 512)
        bst, bag, bshift = carve(TT, 2, 6), carve(TT, 2), carve(2, KT)
        carve = carver()
        fm, tm = carve(F_N, SEQ), carve(TT, TMW)
        mixb = carve(TT, DM)
        lgb, prb, ptb = carve(2, CAUS), carve(2, CAUS), carve(2, CAUS)
        kbT, vb = carve(3, SEQ), carve(TT, GDN_H, HD)
        grow = carve(SEQ)
        xx = carve(2 * GDN_H, 2, P)
        gt, ga, gl1, gl = carve(TT, 24), carve(TT, 12), carve(TT, 12), carve(TT, 12)
        cg, ngr, beta, sig = carve(TT, 12), carve(TT, 12), carve(TT, 6), carve(TT, 6)
        bm, em, ealog, negG = carve(TT, 6), carve(TT, 6), carve(6), carve(TT, 6)
        denb, nmaxb, rdenb = carve(10, TT), carve(10, TT), carve(2, TT)
        hst, hst2, hst3 = carve(TT, 6), carve(TT, 6), carve(TT, 6)
        cvb = xx.rearrange("p a b c -> p (a b c)")[:, 0:1024].rearrange("p (a k n) -> p a k n", a=2, k=2)
        row_b, row_f, row_i, row_m = (flat(mixb)[:, 256 * k:256 * k + 256] for k in range(4))
        norm_r, row_g = flat(mixb)[:, 1024:1280], flat(mixb)[:, 1280:1536]
        sq = scratch[:, F_N * SEQ + TT * TMW + TT * DM:F_N * SEQ + TT * TMW + TT * DM + 6 * SEQ].rearrange("p (f n) -> p f n", f=6)
        attnT = fm.rearrange("p f n -> p (f n)")[:, F_LQ * SEQ:F_LQ * SEQ + GDN_H * CAUS].rearrange("p (h n) -> p h n", h=GDN_H)
        sysT = scratch[:, F_N * SEQ + TT * TMW + TT * DM:F_N * SEQ + TT * TMW + TT * DM + GDN_H * CAUS].rearrange(
            "p (h n) -> p h n", h=GDN_H)
        dec = [tm[:, i, VB:VB + CAUS] for i in range(2)]
        atm = tm[:, 0, VB:VB + 512].rearrange("p (k n) -> p k n", k=4)
        ym = tm[:, 1, VB:VB + 512].rearrange("p (k n) -> p k n", k=4)
        uu = kbT.rearrange("p a b -> p (a b)").rearrange("p (t n) -> p t n", t=TT)
        sq2 = xx.rearrange("p a b c -> p (a b c)")[:, 0:768].rearrange("p (t n) -> p t n", t=TT)

        ps = [ctx.enter_context(nc.psum_tensor(f"bank{i}", [P, 512], F32)) for i in range(8)]
        S, PT, O, G = ps[0:2], ps[2:4], ps[4:6], ps[6:8]
        RN = [ps[0], ps[5], ps[4]]
        UP, TP, ACC = ps[0:2], ps[2:6], ps[4:8]

        def const(name, parts=P):
            a, w = CST[name]
            return cst[0:parts, a:a + w]

        ident = const("ident")

        def sa(name, i=None):
            a, w = SA[name]
            return spa[:, a:a + w] if i is None else spa[:, a + i:a + i + 1]

        def conv_tap(f, i):
            return spa[:, bass.ds(f * 4 + (SA["conv"][0] + i), 1)]

        def sbp(name, i=None):
            a, w = SB[name]
            return spa[:, a:a + w] if i is None else spa[:, a + i:a + i + 1]

        def modc(sub, which):
            return modl[:, (sub * 3 + which) * KT:(sub * 3 + which + 1) * KT]

        raw_in = [sem(f"raw_in{i}") for i in range(RING)]
        hi_done, lo_done = sem("hi_done"), sem("lo_done")
        chunk_mm = sem("chunk_mm")
        direct_mm = sem("direct_mm")
        NEW = RING
        ada_in = [sem(f"ada_in{i}") for i in range(RING)]
        ada_used = sem("ada_used")
        c_in, c_silu = sem("c_in"), sem("c_silu")
        x_in = sem("x_in")
        start_in, small_in, out_st = sem("start_in"), sem("small_in"), sem("out_st")
        ln_in = sem("ln_in")
        layer_done, layer_go = sem("layer_done"), sem("layer_go")
        FIN = {n: sem("fin_" + n) for n in ("rstd", "x")}
        NEXT = {n: sem("next_" + n) for n in ("ss", "std")}
        A = {n: sem("a_" + n) for n in (
            "ss", "std", "rstd", "xn", "tp", "tp_hi", "tp_lo", "pj", "blk", "blk_ev", "rope_i", "rope_h", "dup",
            "ix", "ix_relu", "ix_acc", "gate", "gate_e", "rw", "cg", "cg_e", "cgel", "ckv", "ckv_ev", "cs", "cnm",
            "cexp", "cp", "cpt", "cpt_ev", "co", "zero", "s", "nm", "e", "pt", "pt_ev", "o", "o_ev",
            "dila", "dila_e", "dve", "x", "c1", "cv1", "cv2", "y0", "sg", "h", "hid_hi", "hid_lo")}

        B = {n: sem("b_" + n) for n in (
            "modl", "gdiag", "gateb", "gateb_ev", "tp", "tp_mod", "tp_hi", "tp_lo", "tap", "conv", "fm", "tm",
            "gcopy", "gtok", "gt", "ge", "gln", "gl", "cum", "cg", "rows", "rows_ev", "scan", "mback", "bm", "em",
            "sq", "ss", "ssr", "rn", "rnb", "rnb_ev", "bb", "kb", "vt", "vb",
            "s", "s_free", "nm", "e", "p", "pt", "pt_ev", "o", "o_ev",
            "ds", "dl", "dec", "dmul", "xinit", "xt", "xt_ev", "atm", "y", "y_ev", "z", "xx",
            "u", "u_ev", "w1", "go", "gsq", "gms", "grs", "gout", "lden", "lvar", "lrs", "mix",
            "dve", "act", "std", "nx", "xg", "y0", "sg", "h", "hid_hi", "hid_lo")}
        B_UNITS = [("moba", h) for h in range(MOBA_H)] + [("mlstm", h) for h in range(ML_H)]
        NUB = len(B_UNITS)
        LATE = [3, 4, 5, 6, 7, 0, 1, 2]
        LEVELS = P.bit_length() - 1
        B_LAGP, B_LAGT, B_LAGO, B_LAGV = 1, 2, 3, 4
        N_A, S_A = DEPTH * A_N // RING, DEPTH * A_S

        def arrivals_b(l, n):
            return l * (16 * B_N // RING) + 16 * (N_A + n // RING + 1)

        UNITS = ([("dil", h) for h in range(DIL_H)] + [("slc", h) for h in range(NSA_H)]
                 + [("win", h) for h in range(NSA_H)] + [("dsa", h) for h in range(DSA_H)])
        NU = len(UNITS)
        LAG_T, LAG_O, LAG_V = 2, 3, 4
        HIDDEN_AT, GELU_AT, GELU_E_AT, GELU2_AT, CKV_AT, CKV_EV_AT = 0, 5, 6, 7, 9, 10
        CS_AT, CSM_AT, CEXP_AT, CP_AT, CPT_AT, CPT_EV_AT, CO_AT = 12, 13, 14, 15, 17, 18, 20
        JOIN_AT, SELECT_AT, DIL_AT, DIL_E_AT = 22, 2, 11, 12

        def unit(u):
            kind, h = UNITS[u]
            if kind == "dil":
                return T_CQ + h // 2, T_CK + h // 2, 64 * (h % 2), COL["cv"] + HD * h, const(f"dil{h // 2}"), 640 + HD * h
            q, k, v, m, o = {"slc": (T_AQ, T_KS, "vs", const("causal"), 0), "win": (T_AQ, T_KW, "vw", const("causal"), 0),
                             "dsa": (T_BQ, T_BK, "bv", dmask, 320)}[kind]
            return q + h // 2, k, 64 * (h % 2), COL[v], m, o + HD * h

        def arrivals(l, n):
            return l * (16 * A_N // RING) + 16 * (n // RING + 1)

        def tap(f, i):
            return sbp("conv", F_CONV.index(f) * TAPS + i)

        def mod_count(v, k):
            return (v if v < 2 else v - 1) * KT + k

        block = ctx.enter_context(nc.Block())

        def load_b(sp, l, j, n0, r):
            n = n0 + r
            sp.wait_ge(lo_done, l * B_N + j * RING + (S_A + n - RING + 1 + NEW))
            sp.dma_start(raw[:, n % RING, :], t["wb"][bass.ds(l, 1), bass.ds(j * RING + n, 1), :, :]
                         .rearrange("o c p n -> (o c p) n")).then_inc(raw_in[n % RING], 16)

        @block.sync
        def _(sp):
            def load_ada(l, part, j, r):
                sp.dma_start(ada_raw[:, r, :], t["wm"][bass.ds(l, 1), bass.ds(j * RING + (part * ADA_N + r), 1), :, :]
                             .rearrange("o c p n -> (o c p) n")).then_inc(ada_in[r], 16)

            def load_ffn(l, part, load):
                for r in range(RING):
                    load(0, r)
                if part == 0:
                    sp.wait_ge(A["x"], A_WOUT)
                else:
                    sp.wait_ge(layer_go, l + DEPTH)
                sp.dma_start(cb, t["c"].partition_broadcast(P)).then_inc(c_in, 16)
                for r in range(RING):
                    load_ada(l, part, 0, r)
                with sp.Fori(0, FFN_N // RING // 2) as j:
                    for i in range(2):
                        for r in range(RING):
                            load(j * 2 + (i + 1), r)
                            if i == 0:
                                sp.wait_ge(ada_used, (l + part * DEPTH) * ADA_N + j * RING + (r + 1))
                                load_ada(l, part, j + 1, r)

            sp.dma_start(x[:, :, :], t["x"].rearrange("o (t p) d -> p (o t) d", p=P)).then_inc(x_in, 16)
            sp.dma_start(cst[:, 0:P], t["const"][:, 0:P]).then_inc(x_in, 16)
            with sp.Fori(0, DEPTH) as l:
                for n in range(A_N0["ffn"]):
                    kind, i = a_chunk(n - RING)
                    if kind == "split":
                        sp.wait_ge(lo_done, l * A_S + (i + 1 + NEW))
                    else:
                        sp.wait_ge(direct_mm, l * A_D + (i + 1))
                    w = a_width(n)
                    sp.dma_start(raw[:, n % RING, 0:w],
                                 t["wa"][bass.ds(l, 1), n, :, 0:w].rearrange("o p n -> (o p) n")).then_inc(raw_in[n % RING], 16)
                def load(j, r):
                    sp.wait_ge(lo_done, l * A_S + j * RING + (A_WIN + A_WOUT + r - RING + 1 + NEW))
                    sp.dma_start(raw[:, r, :], t["wa"][bass.ds(l, 1), bass.ds(j * RING + (A_N0["ffn"] + r), 1), :, :]
                                 .rearrange("o c p n -> (o c p) n")).then_inc(raw_in[r], 16)

                load_ffn(l, 0, load)
            with sp.Fori(0, DEPTH) as l:
                load_ffn(l, 1, lambda j, r: load_b(sp, l, j, 0, r))
                for n in range(B_S0["win"], B_S0["ffn1"]):
                    sp.wait_ge(lo_done, l * B_N + (S_A + n - RING + 1 + NEW))
                    w = b_width(n)
                    sp.dma_start(raw[:, n % RING, 0:w],
                                 t["wb"][bass.ds(l, 1), n, :, 0:w].rearrange("o p n -> (o p) n")).then_inc(raw_in[n % RING], 16)
                with sp.Fori(0, FFN_N // RING) as j:
                    for r in range(RING):
                        load_b(sp, l, j, B_S0["ffn1"], r)
            sp.wait_ge(layer_go, 2 * DEPTH)
            sp.dma_start(t["out"].rearrange("o (t p) d -> p (o t) d", p=P), x[:, :, :]).then_inc(out_st, 16)
            sp.wait_ge(out_st, 16)

        def pool_levels(pool):
            for lev in range(1, LEVELS):
                for u in range(2 * GDN_H):
                    n = (lev - 1) * 2 * GDN_H + u
                    if n == 0:
                        pool.wait_ge(B["dmul"], GDN_H)
                    if n >= 4:
                        pool.wait_ge(B["y"], n - 3)
                    at = 0 if u % 2 == 0 else SEQ
                    nc.gpsimd.tensor_tensor(atm[:, n % 4, :], sysT[:, u // 2, at:at + P], const(f"lev{lev}"),
                                            ALU.mult).then_inc(B["atm"], 1)

        def numbers(steps):
            n = [s_.num for s_ in steps.values()]
            assert n == list(range(n[0], n[0] + len(n)))
            return range(n[0], n[0] + len(n))

        @block.gpsimd
        def _(pool):
            pool.wait_ge(raw_in[1], 16)
            pool.dma_start(cst[:, P:], t["const"][:, P:]).then_inc(start_in, 16)
            pool.dma_start(lnw[:, 0, :], t["final_g"].partition_broadcast(P)).then_inc(start_in, 16)
            with pool.Fori(0, DEPTH) as l:
                for v in (rw, kbd, vr, pc):
                    last = nc.gpsimd.memset(v, 0.0)
                last.then_inc(A["zero"], 1)
                pool.wait_ge(layer_done, 3)
                pool.sem_clear(layer_done)
                pool.sem_clear(numbers(A))
                pool.sem_inc(layer_go, 1)
            with pool.Fori(0, DEPTH) as l:
                for sub in range(3):
                    if sub == 0:
                        pool.wait_ge(FIN["x"], TT)
                    else:
                        pool.wait_ge(B["xg"], 2 * sub)
                    for k, name in enumerate(("ln_g", "ln_b")):
                        pool.dma_start(lnw[:, k, :], t[name][bass.ds(l, 1), sub, :].rearrange("o n -> (o n)").partition_broadcast(P)
                                       ).then_inc(ln_in, 16)
                    if sub < 2:
                        pool.wait_ge(ln_in, l * 96 + 32 * (sub + 1))
                        pool.wait_ge(B["tp"], (1 + 2 * sub) * KT + KT)
                        for k, op in enumerate((ALU.mult, ALU.add)):
                            if k:
                                pool.wait_ge(B["xg"], 2 * sub + 1)
                            nc.gpsimd.tensor_tensor(x[:, :, :], x[:, :, :], lnw[:, k, :].unsqueeze(1).to_broadcast([P, TT, DM]), op
                                                    ).then_inc(B["xg"], 1)
                    if sub == 0:
                        pool_levels(pool)
                pool.wait_ge(layer_done, 3)
                pool.sem_clear(layer_done)
                pool.sem_clear(numbers(B))
                pool.sem_inc(layer_go, 1)

        @block.tensor
        def _(pe):
            pe.sem_inc(chunk_mm, NEW)
            pe.wait_ge(x_in, 32)

            def products(out, pairs):
                n = len(pairs)
                for i, ((ah, al), (bh, bl)) in enumerate(pairs):
                    nc.tensor.matmul(out, ah, bh, start=(i == 0), stop=False)
                    nc.tensor.matmul(out, ah, bl, start=False, stop=False)
                    last = nc.tensor.matmul(out, al, bh, start=False, stop=(i == n - 1))
                return last

            def to_features(N, v, src, between=None, order=range(KT)):
                for n, k in enumerate(order):
                    if n == len(TP) and between:
                        between()
                    if n >= len(TP):
                        if between:
                            pe.wait_ge(N["tp_mod"], mod_count(v, n) - len(TP) + 1)
                        else:
                            pe.wait_ge(N["tp_lo"], v * KT + n - len(TP) + 1)
                    if k == 0 and n:
                        pe.wait_ge(N["mix"], 2)
                    for i in range(TT):
                        last = nc.tensor.transpose(TP[n % len(TP)][:, i * P:(i + 1) * P], src[:, i, k * P:(k + 1) * P], ident)
                    last.then_inc(N["tp"], 1)
                pe.wait_ge(N["tp_lo"], v * KT + KT)

            def token_chunk(out, slot, width):
                for i in range(TT):
                    rows = slice(i * P, (i + 1) * P)
                    last = products(out[:, i * width:(i + 1) * width],
                                    [((hT_hi[:, k, rows], hT_lo[:, k, rows]),
                                      (w_hi[:, slot, k * width:(k + 1) * width], w_lo[:, slot, k * width:(k + 1) * width]))
                                     for k in range(KT)])
                return last

            def feature_tile(out, slot, half, stride=2 * P):
                cols = lambda k: slice(k * stride + half * P, k * stride + half * P + P)
                return products(out, [((w_hi[:, slot, cols(k)], w_lo[:, slot, cols(k)]), (hT_hi[:, k, :], hT_lo[:, k, :]))
                                      for k in range(KT)])

            def ffn(N, split, h0):
                def up(f, f2, pos, slot, wait_bank=True):
                    pe.wait_ge(lo_done, pos + (1 + NEW) + split)
                    if wait_bank:
                        pe.wait_ge(N["h"], f + (h0 - 1))
                    feature_tile(UP[f2][:, 0:SEQ], slot, 0)
                    feature_tile(UP[f2][:, SEQ:2 * SEQ], slot, 1).then_inc(chunk_mm, 1)

                def down(f, f4, pos, slot, first=False, last_one=False):
                    pe.wait_ge(lo_done, pos + (1 + NEW) + split)
                    for k2, i in ((0, 0), (1, 0), (0, 1), (1, 1)) if last_one else ((0, 0), (0, 1), (1, 0), (1, 1)):
                        pe.wait_ge(N["hid_lo"], f + (h0 + k2 + 1))
                        rows = slice(i * P, (i + 1) * P)
                        for half in range(2):
                            cols = slice(k2 * DM + half * 512, k2 * DM + half * 512 + 512)
                            out = ACC[2 * i + half][:, :]
                            ah, al = hid_hi[:, f4 + k2, rows], hid_lo[:, f4 + k2, rows]
                            bh, bl = w_hi[:, slot, cols], w_lo[:, slot, cols]
                            nc.tensor.matmul(out, ah, bh, start=first and k2 == 0, stop=False, skip_group_check=True)
                            nc.tensor.matmul(out, ah, bl, start=False, stop=False, skip_group_check=True)
                            last = nc.tensor.matmul(out, al, bh, start=False, stop=last_one and k2 == 1, skip_group_check=True)
                        if last_one and (k2, i) == (1, 0):
                            last.then_inc(N["y0"], 1)
                    last.then_inc(chunk_mm, 1)

                def turn(j, first=False):
                    for r in range(2):
                        f, pos = j * 4 + 2 * r, j * 6 + (1 + 3 * r)
                        up(f + 1, 1, pos, 1, wait_bank=not (first and r == 0))
                        up(f + 2, 0, pos + 1, 2)
                        down(f, 2 * r, pos + 2, 0, first=first and r == 0)

                up(0, 0, 0, 0, wait_bank=False)
                turn(0, first=True)
                with pe.Fori(1, (FT - 2) // 4) as j:
                    turn(j)
                up(FT - 1, 1, FFN_N - 2, (FFN_N - 2) % RING)
                down(FT - 2, 0, FFN_N - 1, (FFN_N - 1) % RING, last_one=True)

            with pe.Fori(0, DEPTH) as l:
                split = l * A_S
                pe.wait_ge(A["xn"], TT)
                to_features(A, 0, xn)
                for c, width in enumerate(WIN_A):
                    pe.wait_ge(lo_done, split + (c + 1 + NEW))
                    if c >= 2:
                        pe.wait_ge(A["pj"], c - 1)
                    token_chunk(G[c % 2], c % RING, width).then_inc(chunk_mm, 1)

                pe.wait_ge(A["pj"], A_WIN)
                for b in range(len(TB) // 2):
                    if b == 2:
                        pe.wait_ge(A["rope_i"], 1)
                    if b == 3:
                        pe.wait_ge(A["dup"], len(DUP))
                    if b >= 2:
                        pe.wait_ge(A["blk_ev"], b - 1)
                    for k in range(2):
                        name, first, width, copies = TB[2 * b + k]
                        for i in range(TT):
                            src = pj[:, i, COL[name] + first:COL[name] + first + width]
                            if copies > 1:
                                src = dup[:, i, DUP.index(2 * b + k), :]
                            last = nc.tensor.transpose(G[b % 2][:, k * SEQ + i * P:k * SEQ + (i + 1) * P], src, ident)
                    last.then_inc(A["blk"], 1)

                pe.wait_ge(A["blk_ev"], T_IK // 2 + 1)
                for h in range(IDX_H):
                    if h >= 2:
                        pe.wait_ge(A["ix_relu"], h - 1)
                    q, rows = T_IQ + h // 4, slice(32 * (h % 4), 32 * (h % 4) + 32)
                    nc.tensor.matmul(S[h % 2][:, 0:P], tb[rows, q, 0:P], tb[rows, T_IK, 0:P], start=True, stop=True)
                    nc.tensor.matmul(S[h % 2][:, P:CAUS], tb[rows, q, P:SEQ], tb[rows, T_IK, :],
                                     start=True, stop=True).then_inc(A["ix"], 1)

                def scores(u):
                    q, k, r, _, _, _ = unit(u)
                    if u >= 2:
                        pe.wait_ge(A["nm"], u - 1)
                    rows = slice(r, r + HD)
                    nc.tensor.matmul(S[u % 2][:, 0:P], tb[rows, q, 0:P], tb[rows, k, 0:P], start=True, stop=True)
                    nc.tensor.matmul(S[u % 2][:, P:CAUS], tb[rows, q, P:SEQ], tb[rows, k, :],
                                     start=True, stop=True).then_inc(A["s"], 1)

                def turn_weights(u):
                    pe.wait_ge(A["e"], u + 1)
                    if u >= 2:
                        pe.wait_ge(A["pt_ev"], u - 1)
                    for cols in (slice(0, P), slice(P, SEQ), slice(SEQ, CAUS)):
                        last = nc.tensor.transpose(PT[u % 2][:, cols], pr[:, u % 2, cols], ident)
                    last.then_inc(A["pt"], 1)

                def values(u):
                    _, _, _, v, _, _ = unit(u)
                    pe.wait_ge(A["pt_ev"], u + 1)
                    if u >= 2:
                        pe.wait_ge(A["o_ev"], u - 1)
                    out, w = O[u % 2], pt[:, u % 2, :]
                    nc.tensor.matmul(out[:, 0:HD], w[:, 0:P], pj[:, 0, v:v + HD], start=True, stop=True)
                    nc.tensor.matmul(out[:, HD:2 * HD], w[:, P:SEQ], pj[:, 0, v:v + HD], start=True, stop=False)
                    nc.tensor.matmul(out[:, HD:2 * HD], w[:, SEQ:CAUS], pj[:, 1, v:v + HD],
                                     start=False, stop=True).then_inc(A["o"], 1)

                def hidden(part):
                    if part == 0:
                        pe.wait_ge(A["rw"], 2)
                    d, first = ((0, 0), (0, 8), (1, 0), (2, 0))[part]
                    n = A_N0["cmp"] + d
                    pe.wait_ge(raw_in[n % RING], arrivals(l, n))
                    for jj in range(8):
                        j = 8 * part + jj
                        last = nc.tensor.matmul(G[0][:, 0:2 * NCMP], raw[:, n % RING, (first + jj) * P:(first + jj + 1) * P],
                                                rw[:, j, :], start=(j == 0), stop=(j == CBLK - 1))
                    if part:
                        last.then_inc(direct_mm, 1)

                def compressed(step):
                    if HIDDEN_AT <= step < HIDDEN_AT + 4:
                        hidden(step - HIDDEN_AT)
                    if step == CKV_AT:
                        pe.wait_ge(A["cgel"], 1)
                        nc.tensor.matmul(G[1][:, 0:NCMP], sa("w2k"), hb[:, 3, 0:NCMP], start=True, stop=True)
                        nc.tensor.matmul(G[1][:, HD:2 * HD], flat(vr), sa("w2v"), start=True, stop=True).then_inc(A["ckv"], 1)
                    if step == CS_AT:
                        pe.wait_ge(A["ckv_ev"], 1)
                        for i in range(TT):
                            for b in range(3):
                                at = 32 + (i * 3 + b) * 32
                                last = nc.tensor.matmul(G[0][:, at:at + 32], tb[:, T_AQR + b, i * P:(i + 1) * P], flat(kbd),
                                                        start=True, stop=True)
                        last.then_inc(A["cs"], 1)
                    if step == CPT_AT:
                        pe.wait_ge(A["cp"], 1)
                        for i in range(TT):
                            nc.tensor.transpose(G[1][:, i * P:(i + 1) * P], pc[:, i, 0:4, :], ident)
                            last = nc.tensor.transpose(G[1][0:32, SEQ + i * P:SEQ + (i + 1) * P], pc[:, i, 4, :], ident)
                        last.then_inc(A["cpt"], 1)
                    if step == CO_AT:
                        pe.wait_ge(A["cpt_ev"], 2)
                        for i in range(TT):
                            nc.tensor.matmul(G[0][:, i * SEQ:(i + 1) * SEQ], pcT[:, i, :], flat(vbd), start=True, stop=True)
                        for i in range(TT):
                            last = nc.tensor.matmul(G[1][:, i * HD:(i + 1) * HD], pcT4[0:32, i, :], vbd[0:32, 0, :],
                                                    start=True, stop=True)
                        last.then_inc(A["co"], 1)

                pe.wait_ge(A["blk_ev"], len(TB) // 2)
                pe.wait_ge(A["ix_relu"], IDX_H)
                for step in range(NU + LAG_O):
                    if step < NU:
                        scores(step)
                    if LAG_T <= step < NU + LAG_T:
                        turn_weights(step - LAG_T)
                    if step >= LAG_O:
                        values(step - LAG_O)
                    compressed(step)

                pe.wait_ge(A["o_ev"], NU)
                to_features(A, 1, mix)
                for c in range(A_WOUT):
                    pe.wait_ge(lo_done, split + (A_WIN + c + 1 + NEW))
                    if c >= 2:
                        pe.wait_ge(A["x"], c - 1)
                    token_chunk(G[c % 2], (A_WIN + c) % RING, GW).then_inc(chunk_mm, 1)
                pe.wait_ge(A["xn"], 2 * TT)
                to_features(A, 2, xn)
                ffn(A, split + (A_WIN + A_WOUT), 0)
                pe.drain().then_inc(layer_done, 1)
                pe.wait_ge(layer_go, l + 1)

            def gate_on_all(sub):
                pe.wait_ge(B["gdiag"], sub + 1)
                for half in range(2):
                    nc.tensor.matmul(G[half][:, :], const("ones"), gdiag[:, 4 * half:4 * half + 4, :].rearrange("p k n -> p (k n)"),
                                     start=True, stop=True).then_inc(B["gateb"], 1)

            pe.wait_ge(start_in, 32)
            pe.wait_ge(FIN["x"], TT)
            with pe.Fori(0, DEPTH) as l:
                split = l * B_N + S_A
                to_features(B, 0, x, lambda: gate_on_all(0))
                pe.wait_ge(B["gateb_ev"], 2)
                ffn(B, split, 0)
                pe.wait_ge(B["nx"], TT)
                to_features(B, 1, x, lambda: gate_on_all(1))
                pe.wait_ge(B["gateb_ev"], 4)
                def prelude(c):
                    if c == 1:
                        pe.wait_ge(B["gcopy"], 1)
                        for i in range(TT):
                            last = nc.tensor.transpose(S[0][:, i * GATES:(i + 1) * GATES], row_g[0:GATES, i * P:(i + 1) * P],
                                                       ident[0:GATES, 0:GATES])
                        last.then_inc(B["gtok"], 1)
                    if c == 5:
                        pe.wait_ge(B["gl"], 1)
                        nc.tensor.matmul(S[1][:, 0:12], const("upto"), gl[:, 0, :], start=True, stop=True)
                        nc.tensor.matmul(S[1][:, 12:24], const("ones"), gl[:, 0, :], start=True, stop=False)
                        nc.tensor.matmul(S[1][:, 12:24], const("upto"), gl[:, 1, :], start=False, stop=True).then_inc(B["cum"], 1)
                    if c == 7:
                        pe.wait_ge(B["cg"], 1)
                        for i in range(TT):
                            cols = slice(i * P, (i + 1) * P)
                            cols2 = slice(SEQ + i * P, SEQ + (i + 1) * P)
                            nc.tensor.transpose(PT[0][0:12, cols], ngr[:, i, :], ident)
                            nc.tensor.transpose(PT[0][0:6, cols2], beta[:, i, :], ident)
                            nc.tensor.transpose(PT[1][0:6, cols], gl[:, i, 6:12], ident)
                            last = nc.tensor.transpose(PT[1][0:6, cols2], gt[:, i, 18:24], ident)
                        last.then_inc(B["rows"], 1)
                    if c == 9:
                        pe.wait_ge(B["sq"], 1)
                        half = const("half").rearrange("p (f n) -> p f n", f=6)
                        for f in range(6):
                            last = nc.tensor.matmul(O[0][0:12, 0:SEQ], half[:, f, :], sq[:, f, :], start=(f == 0), stop=(f == 5))
                        last.then_inc(B["ss"], 1)
                    if c == 10:
                        pe.wait_ge(B["scan"], 1)
                        for i in range(TT):
                            last = nc.tensor.transpose(S[1][:, 32 + i * 6:32 + i * 6 + 6], row_m[0:6, i * P:(i + 1) * P], ident[0:6, 0:6])
                        last.then_inc(B["mback"], 1)
                    if c == 12:
                        pe.wait_ge(B["rn"], 1)
                        pair12 = const("pair12", 12).rearrange("p (f n) -> p f n", f=6)
                        for f in range(6):
                            last = nc.tensor.matmul(RN[f // 2][:, f % 2 * SEQ:(f % 2 + 1) * SEQ], pair12[:, f, :], norm_r[0:12, :],
                                                    start=True, stop=True)
                            if f % 2:
                                last.then_inc(B["rnb"], 1)
                    if c == 13:
                        pe.wait_ge(B["rows_ev"], 4)
                        pair = const("pair", 6).rearrange("p (f n) -> p f n", f=3)
                        for f in range(3):
                            last = nc.tensor.matmul(PT[f // 2][:, f % 2 * SEQ:(f % 2 + 1) * SEQ], pair[:, f, :], row_b[0:6, :],
                                                    start=True, stop=True)
                        last.then_inc(B["bb"], 1)
                    if c == 15:
                        pe.wait_ge(B["rnb_ev"], 2)
                        pe.wait_ge(B["fm"], N_FEAT)
                        for i in range(TT):
                            for f in range(3):
                                last = nc.tensor.transpose(RN[i][:, f * P:(f + 1) * P], fm[:, F_GV + f, i * P:(i + 1) * P], ident)
                            last.then_inc(B["vt"], 1)

                for c, (ftiles, _, width) in enumerate(B_WIN):
                    s_ = B_S0["win"] + c
                    pe.wait_ge(lo_done, split + (s_ + 1 + NEW))
                    if c >= 2:
                        ftiles_b, _, width_b = B_WIN[c - 2]
                        if width_b:
                            pe.wait_ge(B["tm"], len([1 for b in B_WIN[:c - 1] if b[2]]))
                        elif ftiles_b:
                            pe.wait_ge(B["conv"] if ftiles_b[0] in F_CONV else B["fm"], c - 2)
                        else:
                            pe.wait_ge(B["gcopy"], 1)
                    if c == 0:
                        cols = [slice(k * GATES, (k + 1) * GATES) for k in range(KT)]
                        last = products(G[0][0:GATES, 0:SEQ], [((w_hi[:, s_ % RING, cols[k]], w_lo[:, s_ % RING, cols[k]]),
                                                                (hT_hi[:, k, :], hT_lo[:, k, :])) for k in range(KT)])
                    for k in range(len(ftiles)):
                        last = feature_tile(G[c % 2][:, k * SEQ:(k + 1) * SEQ], s_ % RING, k, P * len(ftiles))
                    if width:
                        last = token_chunk(G[c % 2], s_ % RING, width)
                    last.then_inc(chunk_mm, 1)
                    prelude(c)

                def spread_row(out, r):
                    return nc.tensor.matmul(out, ident[0:12, r:r + 1].to_broadcast([12, P]), grow[0:12, :], start=True, stop=True)

                def scores_b(u):
                    kind, h = B_UNITS[u]
                    if 2 <= u < MOBA_H + 2:
                        pe.wait_ge(B["s_free"], u - 1)
                    elif u >= 2:
                        pe.wait_ge(B["p"], u - 1 - MOBA_H)
                    q, k = (F_MQ, F_MK) if kind == "moba" else (F_LQ, F_LK)
                    rows = slice(64 * (h % 2), 64 * (h % 2) + 64)
                    if kind == "mlstm":
                        spread_row(G[u % 2][:, 0:SEQ], 6 + h)
                    nc.tensor.matmul(S[u % 2][:, 0:P], fm[rows, q + h // 2, 0:P], fm[rows, k + h // 2, 0:P], start=True, stop=True)
                    nc.tensor.matmul(S[u % 2][:, P:CAUS], fm[rows, q + h // 2, P:SEQ], fm[rows, k + h // 2, :],
                                     start=True, stop=True).then_inc(B["s"], 1)

                def turn_b(u):
                    if B_UNITS[u][0] == "moba":
                        pe.wait_ge(B["e"], u + 1)
                    else:
                        pe.wait_ge(B["p"], u - MOBA_H + 1)
                    if u >= 2:
                        pe.wait_ge(B["pt_ev"], u - 1)
                    for cols in (slice(0, P), slice(P, SEQ), slice(SEQ, CAUS)):
                        last = nc.tensor.transpose(PT[u % 2][:, cols], prb[:, u % 2, cols], ident)
                    last.then_inc(B["pt"], 1)

                def values_b(u):
                    kind, h = B_UNITS[u]
                    v = (VB if kind == "moba" else VC) + h * HD
                    pe.wait_ge(B["pt_ev"], u + 1)
                    if u >= 2:
                        pe.wait_ge(B["o_ev"], u - 1)
                    out, w = O[u % 2], ptb[:, u % 2, :]
                    nc.tensor.matmul(out[:, 0:HD], w[:, 0:P], tm[:, 0, v:v + HD], start=True, stop=True)
                    nc.tensor.matmul(out[:, HD:2 * HD], w[:, P:SEQ], tm[:, 0, v:v + HD], start=True, stop=False)
                    nc.tensor.matmul(out[:, HD:2 * HD], w[:, SEQ:CAUS], tm[:, 1, v:v + HD], start=False, stop=True).then_inc(B["o"], 1)

                pe.wait_ge(B["fm"], N_FEAT)
                pe.wait_ge(B["tm"], N_TOK)
                pe.wait_ge(B["vb"], TT)
                pe.wait_ge(B["kb"], 3)
                pe.wait_ge(B["em"], 1)
                for step in range(NUB + B_LAGO):
                    if step < NUB:
                        scores_b(step)
                    if B_LAGT <= step < NUB + B_LAGT:
                        turn_b(step - B_LAGT)
                    if step >= B_LAGO:
                        values_b(step - B_LAGO)

                pe.wait_ge(B["o_ev"], NUB)
                for h in range(GDN_H):
                    if h >= 2:
                        pe.wait_ge(B["dmul"], h - 1)
                    rows = slice(64 * (h % 2), 64 * (h % 2) + 64)
                    spread_row(G[h % 2][:, 0:SEQ], h)
                    kT = fm[rows, F_GK + h // 2, :]
                    for bank, other in ((S[h % 2], fm[rows, F_GQ + h // 2, :]), (PT[h % 2], kbT[rows, h // 2, :])):
                        nc.tensor.matmul(bank[:, 0:SEQ], kT[:, 0:P], other[:, 0:SEQ], start=True, stop=True)
                        last = nc.tensor.matmul(bank[:, SEQ:CAUS], kT[:, P:SEQ], other[:, P:SEQ], start=True, stop=True)
                    last.then_inc(B["ds"], 1)
                pe.wait_ge(B["dmul"], GDN_H)
                NI = 2 * GDN_H
                NZ = (LEVELS - 1) * NI
                for u in range(NI):
                    pe.wait_ge(B["xinit"], u // 2 + 1)
                    last = nc.tensor.transpose(ps[4 + u // 4][:, u % 4 * P:(u % 4 + 1) * P], xx[:, u, 1, :], ident)
                    if u % 4 == 3:
                        last.then_inc(B["xt"], 1)
                pe.wait_ge(B["xt_ev"], NI // 4)

                def inv_y(n):
                    u = n % NI
                    pe.wait_ge(B["atm"], n + 1)
                    if n >= NI:
                        pe.wait_ge(B["xx"], n - NI + 1)
                    if n >= 4:
                        pe.wait_ge(B["y_ev"], n - 3)
                    nc.tensor.matmul(ps[n % 4][:, 0:P], atm[:, n % 4, :], xx[:, u, 0, :], start=True, stop=True).then_inc(B["y"], 1)

                def inv_z(n):
                    u = n % NI
                    pe.wait_ge(B["y_ev"], n + 1)
                    if n >= 4:
                        pe.wait_ge(B["xx"], n - 3)
                    if n < NZ - NI:
                        nc.tensor.matmul(ps[4 + n % 4][:, 0:P], xx[:, u, 1, :], ym[:, n % 4, :], start=True, stop=True)
                    nc.tensor.matmul(ps[4 + n % 4][:, P:SEQ], ym[:, n % 4, :], xx[:, u, 1, :], start=True, stop=True).then_inc(B["z"], 1)

                for n in range(NZ + 2):
                    if n < NZ:
                        inv_y(n)
                    if n >= 2:
                        inv_z(n - 2)
                pe.wait_ge(B["xx"], NZ)
                pe.wait_ge(B["y_ev"], NZ)
                hd = lambda h: slice(h * HD, (h + 1) * HD)
                for h in range(GDN_H):
                    last = nc.tensor.matmul(ps[0][:, hd(h)], xx[:, 2 * h, 1, :], vb[:, 0, h, :], start=True, stop=True)
                last.then_inc(B["u"], 1)
                pe.wait_ge(B["u_ev"], 1)
                for h in range(GDN_H):
                    last = nc.tensor.matmul(ps[1][:, hd(h)], sysT[:, h, P:SEQ], uu[:, 0, hd(h)], start=True, stop=True)
                last.then_inc(B["u"], 1)
                for h in range(GDN_H):
                    last = nc.tensor.matmul(ps[6][:, hd(h)], attnT[:, h, 0:P], uu[:, 0, hd(h)], start=True, stop=True)
                last.then_inc(B["go"], 1)
                pe.wait_ge(B["w1"], 1)
                for h in range(GDN_H):
                    last = nc.tensor.matmul(ps[2][:, hd(h)], xx[:, 2 * h + 1, 1, :], vb[:, 1, h, :], start=True, stop=True)
                last.then_inc(B["u"], 1)
                pe.wait_ge(B["u_ev"], 2)
                for h in range(GDN_H):
                    nc.tensor.matmul(ps[7][:, hd(h)], attnT[:, h, P:SEQ], uu[:, 0, hd(h)], start=True, stop=False)
                    last = nc.tensor.matmul(ps[7][:, hd(h)], attnT[:, h, SEQ:CAUS], uu[:, 1, hd(h)], start=False, stop=True)
                last.then_inc(B["go"], 1)

                pe.wait_ge(B["mix"], 1)
                to_features(B, 2, mixb, order=LATE)
                for c in range(B_WOUT):
                    s_ = B_S0["wout"] + c
                    pe.wait_ge(lo_done, split + (s_ + 1 + NEW))
                    token_chunk(ACC[c][:, :], s_ % RING, GW).then_inc(chunk_mm, 1)
                pe.wait_ge(B["nx"], 2 * TT)
                to_features(B, 3, x, lambda: gate_on_all(2))
                pe.wait_ge(B["gateb_ev"], 6)
                ffn(B, split + B_S0["ffn1"], FT)
                pe.drain().then_inc(layer_done, 1)
                pe.wait_ge(layer_go, l + (DEPTH + 1))

        @block.scalar
        def _(act):
            act.wait_ge(x_in, 32)

            def silu_c(uses):
                act.wait_ge(c_in, uses * 16)
                nc.scalar.activation(cb, cb, ACT.Silu).then_inc(c_silu, 1)

            def hi(s, slot, raw_slot, raw_wait, width=CW):
                act.wait_ge(raw_in[raw_slot], raw_wait)
                act.wait_ge(chunk_mm, s + 1)
                nc.scalar.activation(w_hi[:, slot, 0:width], raw[:, raw_slot, 0:width], ACT.Copy).then_inc(hi_done, 1)

            def root_mean_square(N, uses, x_ready=None):
                for i in range(TT):
                    if x_ready:
                        act.wait_ge(A["x"], x_ready + i)
                    nc.scalar.activation(junk[:, i, :], x[:, i, :], ACT.Square, accum_out=st[:, i:i + 1]).then_inc(N["ss"], 1)
                act.wait_ge(N["ss"], uses * TT + TT)
                nc.scalar.activation(st[:, 2:4], st[:, 0:2], ACT.Sqrt, scale=1.0 / DM, bias=NORM_EPS).then_inc(N["std"], 1)

            def hi_features(N, v, gain, order=range(KT)):
                for n, k in enumerate(order):
                    act.wait_ge(N["tp"], v * KT + n + 1)
                    nc.scalar.activation(hT_hi[:, k, :], TP[n % len(TP)][:, 0:SEQ], ACT.Copy,
                                         scale=sa(gain, k) if gain else 1.0).then_inc(N["tp_hi"], 1)

            def ffn(N, split, raw0, h0, conv, more):
                def hi_at(pos, slot):
                    hi(pos + split, slot, slot, raw0 + after(pos))

                def after(pos):
                    return 16 * (pos // RING + 1)

                def post(f, f2, f4, pos, ahead):
                    act.wait_ge(chunk_mm, pos + (1 + NEW) + split)
                    if conv:
                        nc.scalar.activation(cv[:, f2, :], UP[f2][:, 0:SEQ], ACT.Identity, scale=conv_tap(f, 2),
                                             bias=conv_tap(f, 3)).then_inc(N["c1"], 1)
                    else:
                        nc.scalar.activation(sg[:, f2, :], UP[f2][:, 0:SEQ], ACT.Silu).then_inc(N["sg"], 1)
                    ahead()
                    if conv:
                        act.wait_ge(N["cv2"], f + (h0 + 1))
                        nc.scalar.activation(sg[:, f2, :], cv[:, f2, :], ACT.Silu).then_inc(N["sg"], 1)
                    act.wait_ge(N["h"], f + (h0 + 1))
                    nc.scalar.activation(hid_hi[:, f4, :], h32[:, f2, :], ACT.Copy).then_inc(N["hid_hi"], 1)

                def turn(j, stop=FFN_N + 2):
                    for q in range(6):
                        def ahead():
                            pos = q + 4
                            if isinstance(j, int):
                                if j * 6 + pos < stop:
                                    hi(split + (j * 6 + pos), pos % RING, pos % RING, raw0 + 16 * ((j * 6 + pos) // RING + 1))
                            else:
                                hi(j * 6 + pos + split, pos % RING, pos % RING, j * 32 + 16 * (pos // RING + 1) + raw0)
                        if q % 3 == 2:
                            ahead()
                        else:
                            f = j * 4 + (1 + q - q // 3)
                            f4 = (1 + q - q // 3) % 4
                            post(f, f4 % 2, f4, j * 6 + (1 + q), ahead)

                hi(split + 2, 2, 2, raw0 + 16)
                post(0, 0, 0, 0, lambda: hi(split + 3, 0, 0, raw0 + 32))
                turns = (FT - 2) // 4
                with act.Fori(0, turns - 1) as j:
                    turn(j)
                turn(turns - 1, FFN_N + more)
                post(FT - 1, 1, 1, FFN_N - 2,
                     (lambda: hi(split + 34, 34 % RING, 34 % RING, raw0 + 16 * 12)) if more else (lambda: None))

            root_mean_square(NEXT, 0)
            with act.Fori(0, DEPTH) as l:
                split = l * A_S

                def hi_a(s):
                    n = s if s < A_WIN else s + A_D
                    hi(split + s, s % RING, n % RING, arrivals(l, n), a_width(n))

                act.dma_start(spa[:, 0:SA_W], t["sa"][bass.ds(l, 1), :, :].rearrange("o p n -> (o p) n")).then_inc(small_in, 16)
                hi_a(0)
                act.wait_ge(small_in, l * 16 + 16)
                hi_features(A, 0, "g1")
                hi_a(1)
                for c, width in enumerate(WIN_A):
                    if c + 2 < A_WIN:
                        hi_a(c + 2)
                    act.wait_ge(chunk_mm, split + (c + 1 + NEW))
                    nc.scalar.activation(pj[:, :, c * GW:c * GW + width],
                                         G[c % 2][:, 0:TT * width].rearrange("p (t n) -> p t n", t=TT),
                                         ACT.Copy).then_inc(A["pj"], 1)
                for b in range(len(TB) // 2):
                    if b == 2:
                        act.wait_ge(A["rope_h"], 1)
                        for k, block_ in enumerate(DUP):
                            name, first, width, copies = TB[block_]
                            nc.scalar.activation(dup[:, :, k, :].rearrange("p t (c n) -> p t c n", c=copies),
                                                 pj[:, :, COL[name]:COL[name] + width].unsqueeze(2)
                                                 .to_broadcast([P, TT, copies, width]), ACT.Copy).then_inc(A["dup"], 1)
                    act.wait_ge(A["blk"], b + 1)
                    nc.scalar.activation(tb[:, 2 * b:2 * b + 2, :], G[b % 2][:, :].rearrange("p (k n) -> p k n", k=2),
                                         ACT.Copy).then_inc(A["blk_ev"], 1)
                for h in range(IDX_H):
                    act.wait_ge(A["ix"], h + 1)
                    if h >= 2:
                        act.wait_ge(A["ix_acc"], h - 1)
                    nc.scalar.activation(relu[:, h % 2, :], S[h % 2][:, 0:CAUS], ACT.Relu,
                                         scale=IDX_D ** -0.5).then_inc(A["ix_relu"], 1)
                act.wait_ge(A["gate"], 1)
                nc.scalar.activation(ags, ags, ACT.Exp, scale=-1.0).then_inc(A["gate_e"], 1)
                def exponentials(u):
                    act.wait_ge(A["nm"], u + 1)
                    if u >= 2:
                        act.wait_ge(A["pt"], u - 1)
                    nc.scalar.activation(pr[:, u % 2, 0:P], lg[:, u % 2, 0:P], ACT.Exp, bias=nmax[:, u, 0:1],
                                         accum_out=den[:, u, 0:1])
                    nc.scalar.activation(pr[:, u % 2, P:CAUS], lg[:, u % 2, P:CAUS], ACT.Exp, bias=nmax[:, u, 1:2],
                                         accum_out=den[:, u, 1:2]).then_inc(A["e"], 1)

                def copy_weights(u):
                    act.wait_ge(A["pt"], u + 1)
                    if u >= 2:
                        act.wait_ge(A["o"], u - 1)
                    nc.scalar.activation(pt[:, u % 2, :], PT[u % 2][:, 0:CAUS], ACT.Copy).then_inc(A["pt_ev"], 1)

                def compressed(step):
                    if step == GELU_E_AT:
                        act.wait_ge(A["cg"], 1)
                        nc.scalar.activation(hb[:, 2, :], hb[:, 1, :], ACT.Exp, scale=-2.0 * (2.0 / np.pi) ** 0.5).then_inc(A["cg_e"], 1)
                    if step == CEXP_AT:
                        act.wait_ge(A["cnm"], 1)
                        nc.scalar.activation(lc[:, :, :, 0:NCMP], lc[:, :, :, 0:NCMP], ACT.Exp).then_inc(A["cexp"], 1)
                    if step == DIL_E_AT:
                        act.wait_ge(A["dila"], 1)
                        nc.scalar.activation(dexp, dexp, ACT.Exp).then_inc(A["dila_e"], 1)
                    if step == CPT_EV_AT:
                        act.wait_ge(A["cpt"], 1)
                        nc.scalar.activation(pcT, G[1][:, 0:SEQ].rearrange("p (t n) -> p t n", t=TT), ACT.Copy).then_inc(A["cpt_ev"], 1)
                        nc.scalar.activation(pcT4[0:32], G[1][0:32, SEQ:2 * SEQ].rearrange("p (t n) -> p t n", t=TT),
                                             ACT.Copy).then_inc(A["cpt_ev"], 1)

                for step in range(NU + LAG_T):
                    if step < NU:
                        exponentials(step)
                    if step >= LAG_T:
                        copy_weights(step - LAG_T)
                    compressed(step)
                hi_a(A_WIN)
                hi_a(A_WIN + 1)
                hi_features(A, 1, None)
                for c in range(A_WOUT):
                    hi_a(A_WIN + c + 2)
                act.wait_ge(A["x"], A_WOUT)
                root_mean_square(A, 0)
                hi_features(A, 2, "g2")
                silu_c(l + 1)
                ffn(A, split + (A_WIN + A_WOUT), l * (16 * A_N // RING) + 16 * (A_N0["ffn"] // RING), 0, True, 0)
                root_mean_square(NEXT, l + 1, A_WOUT + 1)
                act.drain().then_inc(layer_done, 1)
                act.wait_ge(layer_go, l + 1)

            def hi_mod(v, sub):
                def mod_(k):
                    act.wait_ge(B["tp"], v * KT + k + 1)
                    if k >= 4:
                        act.wait_ge(B["tp_lo"], v * KT + k - 3)
                    nc.scalar.activation(hx[:, k % 4, :], TP[k % len(TP)][:, 0:SEQ], ACT.Identity, scale=modc(sub, 1)[:, k:k + 1],
                                         bias=modc(sub, 0)[:, k:k + 1]).then_inc(B["tp_mod"], 1)

                def hi_(k):
                    act.wait_ge(B["tp_mod"], mod_count(v, k) + 1)
                    nc.scalar.activation(hT_hi[:, k, :], hx[:, k % 4, :], ACT.Copy).then_inc(B["tp_hi"], 1)

                act.wait_ge(B["modl"], min(sub, 1) + 1)
                for k in range(KT):
                    mod_(k)
                    if k:
                        hi_(k - 1)
                    if k == 5:
                        for half in range(2):
                            act.wait_ge(B["gateb"], sub * 2 + half + 1)
                            nc.scalar.activation(gateb[:, half * 512:half * 512 + 512], G[half][:, :], ACT.Copy
                                                 ).then_inc(B["gateb_ev"], 1)
                hi_(KT - 1)

            def root(sub):
                act.wait_ge(B["std"], 2 * sub + 1)
                nc.scalar.activation(st[:, 8:10], bag[:, :, 1], ACT.Sqrt, bias=LN_EPS).then_inc(B["std"], 1)

            act.wait_ge(FIN["x"], TT)
            with act.Fori(0, DEPTH) as l:
                split = l * B_N + S_A

                def hi_b(s):
                    hi(split + s, s % RING, s % RING, arrivals_b(l, s), b_width(s))

                act.dma_start(spa[:, 0:SB_W], t["sb"][bass.ds(l, 1), :, :].rearrange("o p n -> (o p) n")).then_inc(small_in, 16)
                hi_b(0)
                hi_mod(0, 0)
                hi_b(1)
                silu_c(l + (DEPTH + 1))
                ffn(B, split, l * (16 * B_N // RING) + 16 * N_A, 0, False, 2)
                root(0)
                hi_mod(1, 1)
                act.wait_ge(small_in, l * 16 + (DEPTH * 16 + 16))
                silus = []

                def prelude(c):
                    if c == 0:
                        nc.scalar.activation(row_g[0:GATES, :], G[0][0:GATES, 0:SEQ], ACT.Copy).then_inc(B["gcopy"], 1)
                    if c == 3:
                        act.wait_ge(B["gt"], 1)
                        nc.scalar.activation(ga, ga, ACT.Exp, scale=-1.0).then_inc(B["ge"], 1)
                        nc.scalar.activation(beta, sig, ACT.Exp, scale=-1.0).then_inc(B["ge"], 1)
                        nc.scalar.activation(ealog, sbp("a_log"), ACT.Exp).then_inc(B["ge"], 1)
                        act.wait_ge(B["ge"], 3)
                        nc.scalar.activation(gl1, ga, ACT.Ln, bias=1.0).then_inc(B["gln"], 1)
                    if c == 8:
                        act.wait_ge(B["rows"], 1)
                        nc.scalar.activation(grow[0:12, :], PT[0][0:12, 0:SEQ], ACT.Copy).then_inc(B["rows_ev"], 1)
                        nc.scalar.activation(row_b[0:6, :], PT[0][0:6, SEQ:2 * SEQ], ACT.Copy).then_inc(B["rows_ev"], 1)
                        nc.scalar.activation(row_f[0:6, :], PT[1][0:6, 0:SEQ], ACT.Copy).then_inc(B["rows_ev"], 1)
                        nc.scalar.activation(row_i[0:6, :], PT[1][0:6, SEQ:2 * SEQ], ACT.Copy).then_inc(B["rows_ev"], 1)
                        act.wait_ge(B["fm"], 3)
                        nc.scalar.activation(sq, fm[:, F_GQ:F_GQ + 6, :], ACT.Square).then_inc(B["sq"], 1)
                    if c == 10:
                        act.wait_ge(B["ss"], 1)
                        nc.scalar.activation(norm_r[0:12, :], O[0][0:12, 0:SEQ], ACT.Sqrt, bias=NORM_EPS).then_inc(B["ssr"], 1)
                    if c == 12:
                        act.wait_ge(B["bm"], 1)
                        nc.scalar.activation(em, S[1][:, 32:44].rearrange("p (t h) -> p t h", t=TT), ACT.Exp, scale=-1.0
                                             ).then_inc(B["em"], 1)

                def silu(c):
                    ftiles = B_WIN[c][0]
                    act.wait_ge(B["conv"], c)
                    nc.scalar.activation(fm[:, ftiles[0]:ftiles[0] + len(ftiles), :], cvb[:, c % 2, 0:len(ftiles), :],
                                         ACT.Silu).then_inc(B["fm"], 1)

                for c, (ftiles, at, width) in enumerate(B_WIN):
                    s_ = B_S0["win"] + c
                    hi_b(s_ + 2)
                    if silus and c - silus[0] >= 1:
                        silu(silus.pop(0))
                    act.wait_ge(chunk_mm, split + (s_ + 1 + NEW))
                    bank = G[c % 2]
                    if ftiles and ftiles[0] in F_CONV:
                        for k, f in enumerate(ftiles):
                            if f in F_CONV:
                                nc.scalar.activation(cvb[:, c % 2, k, :], bank[:, k * SEQ:(k + 1) * SEQ], ACT.Copy,
                                                     scale=tap(f, 3)).then_inc(B["tap"], 1)
                        silus.append(c)
                    elif ftiles:
                        nc.scalar.activation(fm[:, ftiles[0]:ftiles[0] + 2, :], bank[:, :].rearrange("p (k n) -> p k n", k=2),
                                             ACT.Copy).then_inc(B["fm"], 1)
                    if width:
                        nc.scalar.activation(tm[:, :, at:at + width], bank[:, 0:TT * width].rearrange("p (t n) -> p t n", t=TT),
                                             ACT.Copy).then_inc(B["tm"], 1)
                    prelude(c)
                for c in silus:
                    silu(c)
                def exp_b(u):
                    kind, h = B_UNITS[u]
                    act.wait_ge(B["nm"], u + 1)
                    if u >= 2:
                        act.wait_ge(B["pt"], u - 1)
                    for i, cols in enumerate((slice(0, P), slice(P, CAUS))):
                        if kind == "moba":
                            last = nc.scalar.activation(prb[:, u % 2, cols], lgb[:, u % 2, cols], ACT.Exp, bias=nmaxb[:, u, i:i + 1],
                                                        accum_out=denb[:, u, i:i + 1])
                        else:
                            last = nc.scalar.activation(prb[:, u % 2, cols], lgb[:, u % 2, cols], ACT.Exp, bias=bm[:, i, h:h + 1])
                    last.then_inc(B["e"], 1)

                def copy_b(u):
                    act.wait_ge(B["pt"], u + 1)
                    if u >= 2:
                        act.wait_ge(B["o"], u - 1)
                    nc.scalar.activation(ptb[:, u % 2, :], PT[u % 2][:, 0:CAUS], ACT.Copy).then_inc(B["pt_ev"], 1)

                for step in range(NUB + B_LAGT):
                    if step < NUB:
                        exp_b(step)
                    if step >= B_LAGT:
                        copy_b(step - B_LAGT)
                act.wait_ge(B["tm"], N_TOK)
                nc.scalar.activation(tm[:, :, ZC:ZC + 384], tm[:, :, ZC:ZC + 384], ACT.Silu).then_inc(B["act"], 1)
                nc.scalar.activation(tm[:, :, OC:OC + 384], tm[:, :, OC:OC + 384], ACT.Sigmoid).then_inc(B["act"], 1)
                for h in range(GDN_H):
                    act.wait_ge(B["dl"], h + 1)
                    nc.scalar.activation(dec[h % 2][:, 0:SEQ], dec[h % 2][:, 0:SEQ], ACT.Exp, bias=negG[:, 0, h:h + 1])
                    nc.scalar.activation(dec[h % 2][:, SEQ:CAUS], dec[h % 2][:, SEQ:CAUS], ACT.Exp, bias=negG[:, 1, h:h + 1]
                                         ).then_inc(B["dec"], 1)
                for k in range(2 * GDN_H // 4):
                    act.wait_ge(B["xt"], k + 1)
                    nc.scalar.activation(xx[:, 4 * k:4 * k + 4, 0, :], ps[4 + k][:, :].rearrange("p (u n) -> p u n", u=4), ACT.Copy
                                         ).then_inc(B["xt_ev"], 1)
                for n in range((LEVELS - 1) * 2 * GDN_H):
                    if n == 30:
                        act.wait_ge(B["lvar"], 1)
                        nc.scalar.activation(hst3, hst3, ACT.Sqrt, scale=1.0 / HD, bias=NORM_EPS).then_inc(B["lrs"], 1)
                    act.wait_ge(B["y"], n + 1)
                    if n >= 4:
                        act.wait_ge(B["z"], n - 3)
                    nc.scalar.activation(ym[:, n % 4, :], ps[n % 4][:, 0:P], ACT.Copy).then_inc(B["y_ev"], 1)
                act.wait_ge(B["u"], 1)
                nc.scalar.activation(uu[:, 0, :], ps[0][:, 0:384], ACT.Copy).then_inc(B["u_ev"], 1)
                act.wait_ge(B["u"], 3)
                nc.scalar.activation(uu[:, 1, :], ps[2][:, 0:384], ACT.Copy).then_inc(B["u_ev"], 1)
                act.wait_ge(B["go"], 2)
                nc.scalar.activation(sq2[:, 0, :], ps[6][:, 0:384], ACT.Square).then_inc(B["gsq"], 1)
                nc.scalar.activation(sq2[:, 1, :], ps[7][:, 0:384], ACT.Square).then_inc(B["gsq"], 1)
                act.wait_ge(B["gms"], 1)
                nc.scalar.activation(hst, hst, ACT.Sqrt, scale=1.0 / HD, bias=NORM_EPS).then_inc(B["grs"], 1)
                hi_features(B, 2, None, LATE)
                for c in range(B_WOUT):
                    hi_b(B_S0["wout"] + c + 2)
                root(1)
                hi_mod(3, 2)
                ffn(B, split + B_S0["ffn1"], l * (16 * B_N // RING) + 16 * (N_A + B_S0["ffn1"] // RING), FT, False, 0)
                root(2)
                act.drain().then_inc(layer_done, 1)
                act.wait_ge(layer_go, l + (DEPTH + 1))

        @block.vector
        def _(dve):
            dve.sem_inc(lo_done, NEW)
            dve.wait_ge(x_in, 32)

            def modulation(w, half, column):
                w = w[:, half * DM:(half + 1) * DM]
                return nc.vector.scalar_tensor_tensor(out=w, in0=w, scalar=1.0, in1=cb, op0=ALU.mult, op1=ALU.mult,
                                                      accum_out=column)

            def lo(s, slot, raw_slot, width=CW):
                dve.wait_ge(hi_done, s + 1)
                nc.vector.tensor_tensor(w_lo[:, slot, 0:width], raw[:, raw_slot, 0:width],
                                        w_hi[:, slot, 0:width].bitcast(F32), ALU.subtract).then_inc(lo_done, 1)

            def normed(M, uses, N, v):
                dve.wait_ge(M["std"], uses + 1)
                nc.vector.reciprocal(st[:, 4:6], st[:, 2:4]).then_inc(N["rstd"], 1)
                dve.wait_ge(N["rstd"], v + 1)

            def rms_norm(M, uses, N, v):
                normed(M, uses, N, v)
                for i in range(TT):
                    nc.vector.tensor_scalar(xn[:, i, :], x[:, i, :], st[:, 4 + i:5 + i], None, ALU.mult).then_inc(N["xn"], 1)

            def lo_features(N, v, gain, order=range(KT)):
                for n, k in enumerate(order):
                    dve.wait_ge(N["tp_hi"], v * KT + n + 1)
                    nc.vector.scalar_tensor_tensor(out=hT_lo[:, k, :], in0=TP[n % len(TP)][:, 0:SEQ],
                                                   scalar=sa(gain, k) if gain else 1.0, in1=hT_hi[:, k, :].bitcast(F32),
                                                   op0=ALU.mult, op1=ALU.subtract).then_inc(N["tp_lo"], 1)

            def ffn(N, split, h0, more, conv=False, part=None):

                def post(f, f2, f4, ahead):
                    if conv:
                        dve.wait_ge(N["c1"], f + (h0 + 1))
                        nc.vector.scalar_tensor_tensor(out=cv[:, f2, 1:SEQ], in0=UP[f2][:, 0:SEQ - 1], scalar=conv_tap(f, 1),
                                                       in1=cv[:, f2, 1:SEQ], op0=ALU.mult, op1=ALU.add).then_inc(N["cv1"], 1)
                        dve.wait_ge(N["cv1"], f + (h0 + 1))
                        nc.vector.scalar_tensor_tensor(out=cv[:, f2, 2:SEQ], in0=UP[f2][:, 0:SEQ - 2], scalar=conv_tap(f, 0),
                                                       in1=cv[:, f2, 2:SEQ], op0=ALU.mult, op1=ALU.add).then_inc(N["cv2"], 1)
                    ahead()
                    dve.wait_ge(N["sg"], f + (h0 + 1))
                    nc.vector.tensor_tensor(h32[:, f2, :], sg[:, f2, :], UP[f2][:, SEQ:2 * SEQ], ALU.mult).then_inc(N["h"], 1)
                    dve.wait_ge(N["hid_hi"], f + (h0 + 1))
                    nc.vector.tensor_tensor(hid_lo[:, f4, :], h32[:, f2, :], hid_hi[:, f4, :].bitcast(F32),
                                            ALU.subtract).then_inc(N["hid_lo"], 1)

                def ada(j, k):
                    r, half = k // 2, k % 2
                    if half == 0:
                        dve.wait_ge(ada_in[r], part * (16 * ADA_T) + j * 16 + 16)
                    last = modulation(ada_raw[:, r, :], half, moda[:, bass.ds(j * (2 * RING) + k, 1)])
                    if half:
                        last.then_inc(ada_used, 1)

                def turn(j):
                    for q in range(6):
                        ahead = lambda: lo(j * 6 + (q + 3) + split, q % RING, q % RING)
                        if q % 3 == 2:
                            ahead()
                        else:
                            f4 = (1 + q - q // 3) % 4
                            post(j * 4 + (1 + q - q // 3), f4 % 2, f4, ahead)
                        if part is not None:
                            for k in ((), (0,), (1, 2), (), (3,), (4, 5))[q]:
                                ada(j + 1, k)

                lo(split + 1, 1, 1)
                if part is not None:
                    dve.wait_ge(c_silu, part + 1)
                    for k in range(2 * RING):
                        ada(0, k)
                post(0, 0, 0, lambda: lo(split + 2, 2, 2))
                with dve.Fori(0, (FT - 2) // 4) as j:
                    turn(j)
                post(FT - 1, 1, 1, (lambda: lo(split + FFN_N, 0, 0)) if more else (lambda: None))

            with dve.Fori(0, DEPTH) as l:
                split = l * A_S
                steps = 0

                def link(ins):
                    nonlocal steps
                    steps += 1
                    ins.then_inc(A["dve"], 1)
                    dve.wait_ge(A["dve"], steps)

                def lo_a(s):
                    n = s if s < A_WIN else s + A_D
                    lo(split + s, s % RING, n % RING, a_width(n))

                rms_norm(NEXT, l, A, 0)
                lo_a(0)
                dve.wait_ge(small_in, l * 16 + 16)
                lo_features(A, 0, "g1")
                for c in range(1, A_WIN):
                    lo_a(c)

                def rotate(first, heads, width, table, done):
                    r = CST["cos" + table][1] // TT
                    v = pj[:, :, first:first + heads * width].rearrange("p t (h d) -> p t h d", d=width)
                    x1, x2 = v[:, :, :, 0:r], v[:, :, :, r:2 * r]
                    cos, sin = (const(f + table).rearrange("p (t r) -> p t r", t=TT).unsqueeze(2)
                                .to_broadcast([P, TT, heads, r]) for f in ("cos", "sin"))
                    tmp = [b[:, 0:TT * heads * r].rearrange("p (t h r) -> p t h r", t=TT, h=heads) for b in rot]
                    for out, a, b in zip(tmp, (x1, x2, x2, x1), (cos, sin, cos, sin)):
                        last = nc.vector.tensor_tensor(out, a, b, ALU.mult)
                    link(last)
                    nc.vector.tensor_tensor(x1, tmp[0], tmp[1], ALU.subtract)
                    nc.vector.tensor_tensor(x2, tmp[2], tmp[3], ALU.add).then_inc(done, 1)
                    dve.wait_ge(done, 1)

                dve.wait_ge(start_in, 32)
                dve.wait_ge(A["pj"], A_WIN)
                rotate(COL["iq"], ROT_I, IDX_D, "i", A["rope_i"])
                dve.wait_ge(A["blk"], 2)
                rotate(COL["aq"], ROT_H, HD, "h", A["rope_h"])
                nc.vector.tensor_scalar(ags, pj[:, :, COL["ag"]:COL["ag"] + 15], -80.0, None, ALU.max).then_inc(A["gate"], 1)
                link(nc.vector.tensor_scalar(iws, pj[:, :, COL["iw"]:COL["iw"] + IDX_H], IDX_H ** -0.5, None, ALU.mult))
                dve.wait_ge(A["blk_ev"], T_KCVC // 2 + 1)
                dve.wait_ge(A["zero"], 1)
                kcvc = tb[:, T_KCVC, :].rearrange("p (m j) -> p m j", j=CSTR)
                for half in range(CBLK // CSTR):
                    js = slice(half * CSTR, (half + 1) * CSTR)
                    for kv in range(2):
                        rows, cols = slice(64 * kv, 64 * kv + 64), slice(kv * NCMP, (kv + 1) * NCMP)
                        last = nc.vector.tensor_tensor(rw[rows, js, cols], kcvc[rows, half:half + NCMP, :].rearrange("p m j -> p j m"),
                                                       sa("pos")[rows, js].unsqueeze(2).to_broadcast([64, CSTR, NCMP]), ALU.add)
                    last.then_inc(A["rw"], 1)
                for h in range(IDX_H):
                    dve.wait_ge(A["ix_relu"], h + 1)
                    if h:
                        dve.wait_ge(A["ix_acc"], h)
                    for i, cols in enumerate((slice(0, P), slice(P, CAUS))):
                        if h == 0:
                            last = nc.vector.tensor_scalar(isc[:, cols], relu[:, 0, cols], iws[:, i, 0:1], None, ALU.mult)
                        else:
                            last = nc.vector.scalar_tensor_tensor(out=isc[:, cols], in0=relu[:, h % 2, cols],
                                                                  scalar=iws[:, i, h:h + 1], in1=isc[:, cols],
                                                                  op0=ALU.mult, op1=ALU.add)
                    last.then_inc(A["ix_acc"], 1)
                dve.wait_ge(A["gate_e"], 1)
                link(nc.vector.tensor_scalar(ags, ags, 1.0, None, ALU.add))
                link(nc.vector.reciprocal(ags, ags))
                gates = ags.rearrange("p t (h g) -> p t h g", g=3)
                hv = [hb[:, k, :] for k in range(4)]
                per_head = lambda name: (const(name).rearrange("p (t n) -> p t n", t=TT).unsqueeze(2)
                                         .to_broadcast([P, TT, NSA_H, NCMP]))
                lcv = lc[:, :, :, 0:NCMP]

                def compressed(step):
                    if step == GELU_AT:
                        dve.wait_ge(direct_mm, l * A_D + A_CMP)
                        link(nc.vector.tensor_copy(hv[0], G[0][:, 0:2 * NCMP]))
                        link(nc.vector.tensor_tensor(hv[1], hv[0], hv[0], ALU.mult))
                        link(nc.vector.tensor_scalar(hv[1], hv[1], 0.044715, 1.0, ALU.mult, ALU.add))
                        link(nc.vector.tensor_tensor(hv[1], hv[1], hv[0], ALU.mult))
                        nc.vector.tensor_scalar(hv[1], hv[1], -50.0, None, ALU.max).then_inc(A["cg"], 1)
                    if step == GELU2_AT:
                        dve.wait_ge(A["cg_e"], 1)
                        link(nc.vector.tensor_scalar(hv[2], hv[2], 1.0, None, ALU.add))
                        link(nc.vector.reciprocal(hv[2], hv[2]))
                        link(nc.vector.tensor_tensor(hv[3], hv[0], hv[2], ALU.mult))
                        nc.vector.tensor_copy(vr[:, :, 0:NCMP], hb[:, 3, NCMP:2 * NCMP].unsqueeze(1).to_broadcast([P, 4, NCMP])
                                              ).then_inc(A["cgel"], 1)
                    if step == CKV_EV_AT:
                        dve.wait_ge(A["ckv"], 1)
                        nc.vector.tensor_tensor(kbd[:, :, 0:NCMP], G[1][:, 0:NCMP].unsqueeze(1).to_broadcast([P, 2, NCMP]),
                                                const("pair_of").unsqueeze(2).to_broadcast([P, 2, NCMP]), ALU.mult)
                        nc.vector.tensor_tensor(vbd, G[1][:, HD:2 * HD].unsqueeze(1).to_broadcast([P, 4, HD]),
                                                const("quad_of").unsqueeze(2).to_broadcast([P, 4, HD]), ALU.mult).then_inc(A["ckv_ev"], 1)
                    if step == CSM_AT:
                        dve.wait_ge(A["cs"], 1)
                        sc = G[0][:, 32:32 + TT * 6 * 16].rearrange("p (t h n) -> p t h n", t=TT, h=6)[:, :, 0:NSA_H, 0:NCMP]
                        for i in range(TT):
                            last = nc.vector.scalar_tensor_tensor(out=lcv[:, i], in0=sc[:, i], scalar=SCALE,
                                                                  in1=per_head("cmp_add")[:, i], op0=ALU.mult, op1=ALU.add)
                        link(last)
                        link(nc.vector.tensor_reduce(mc, lcv, AX.X, ALU.max))
                        nc.vector.tensor_tensor(lcv, lcv, mc.unsqueeze(3).to_broadcast([P, TT, NSA_H, NCMP]),
                                                ALU.subtract).then_inc(A["cnm"], 1)
                    if step == CP_AT:
                        dve.wait_ge(A["cexp"], 1)
                        nc.vector.tensor_tensor(pc[:, :, :, 0:NCMP], lcv, per_head("cmp_keep"), ALU.mult).then_inc(A["cp"], 1)
                        dve.wait_ge(A["cp"], 1)
                        link(nc.vector.tensor_reduce(dc, pc[:, :, :, 0:NCMP], AX.X, ALU.add))
                        link(nc.vector.tensor_scalar(dc, dc, 1e-30, None, ALU.max))
                        link(nc.vector.reciprocal(dc, dc))
                        link(nc.vector.tensor_tensor(dc, dc, gates[:, :, :, 0], ALU.mult))

                    if step == JOIN_AT:
                        dve.wait_ge(A["co"], 1)
                        dve.wait_ge(A["o_ev"], DIL_H + 2 * NSA_H)
                        for h in range(NSA_H):
                            for i in range(TT):
                                out, at = mix[:, i, h * HD:(h + 1) * HD], (i * SEQ + h * HD if h < 4 else i * HD)
                                nc.vector.scalar_tensor_tensor(out=out, in0=G[h // 4][:, at:at + HD], scalar=dc[:, i, h:h + 1],
                                                               in1=out, op0=ALU.mult, op1=ALU.add)

                nm = nmax[:, 0:DIL_H, :].rearrange("p (g h) t -> p g (h t)", g=3)
                dn = den[:, 0:DIL_H, :].rearrange("p (g h) t -> p g (h t)", g=3)
                ex, fc = (v.rearrange("p (g h) t -> p g (h t)", g=3) for v in (dexp, dfac))
                low = dmin.rearrange("p h t -> p (h t)")
                spread = low.unsqueeze(1).to_broadcast([P, 3, 2 * TT])

                def dilations(step):
                    if step == DIL_AT:
                        link(nc.vector.tensor_tensor(low, nm[:, 0, :], nm[:, 1, :], ALU.min))
                        link(nc.vector.tensor_tensor(low, low, nm[:, 2, :], ALU.min))
                        nc.vector.tensor_tensor(ex, spread, nm, ALU.subtract).then_inc(A["dila"], 1)
                    if step == DIL_E_AT + 1:
                        dve.wait_ge(A["dila_e"], 1)
                        link(nc.vector.tensor_tensor(fc, ex, dn, ALU.mult))
                        link(nc.vector.tensor_tensor(low, fc[:, 0, :], fc[:, 1, :], ALU.add))
                        link(nc.vector.tensor_tensor(low, low, fc[:, 2, :], ALU.add))
                        link(nc.vector.reciprocal(low, low))
                        link(nc.vector.tensor_tensor(fc, ex, spread, ALU.mult))
                        dve.wait_ge(A["o_ev"], DIL_H)
                        for i in range(TT):
                            o = mix[:, i, 640:DM].rearrange("p (h d) -> p h d", d=HD)
                            nc.vector.tensor_tensor(o, o, dfac[:, :, i].unsqueeze(2).to_broadcast([P, DIL_H, HD]), ALU.mult)

                def select_keys(part):
                    TAKEN = -3e38
                    if part == 0:
                        link(nc.vector.tensor_tensor(isc, isc, const("causal"), ALU.add))
                    if 0 <= part < TOPK // 8:
                        nc.vector.max(m8[:, 0, :], isc[:, 0:P])
                        link(nc.vector.max(m8[:, 1, :], isc[:, P:CAUS]))
                        nc.vector.match_replace(isc[:, 0:P], m8[:, 0, :], isc[:, 0:P], TAKEN)
                        link(nc.vector.match_replace(isc[:, P:CAUS], m8[:, 1, :], isc[:, P:CAUS], TAKEN))
                    if part == TOPK // 8:
                        link(nc.vector.tensor_scalar(dmask, isc, 0.5 * TAKEN, NEG, ALU.is_gt, ALU.mult))
                        link(nc.vector.tensor_tensor(dmask, dmask, const("causal"), ALU.add))

                def logits(u):
                    dve.wait_ge(A["s"], u + 1)
                    if u >= 2:
                        dve.wait_ge(A["e"], u - 1)
                    link(nc.vector.scalar_tensor_tensor(out=lg[:, u % 2, :], in0=S[u % 2][:, 0:CAUS], scalar=SCALE,
                                                        in1=unit(u)[4], op0=ALU.mult, op1=ALU.add))
                    nc.vector.tensor_reduce(nmax[:, u, 0:1], lg[:, u % 2, 0:P], AX.X, ALU.max, negate=True)
                    nc.vector.tensor_reduce(nmax[:, u, 1:2], lg[:, u % 2, P:CAUS], AX.X, ALU.max, negate=True).then_inc(A["nm"], 1)

                def outputs(u):
                    kind, h = UNITS[u]
                    at = unit(u)[5]
                    dve.wait_ge(A["o"], u + 1)
                    if kind == "dil":
                        nc.vector.tensor_copy(mix[:, :, at:at + HD], O[u % 2][:, 0:TT * HD].rearrange("p (t d) -> p t d", t=TT)
                                              ).then_inc(A["o_ev"], 1)
                        return
                    link(nc.vector.reciprocal(rden[:, u % 2, :], den[:, u, :]))
                    f = rden[:, u % 2, :]
                    if kind != "dsa":
                        f = fac[:, u % 2, :]
                        link(nc.vector.tensor_tensor(f, rden[:, u % 2, :], gates[:, :, h, 1 if kind == "slc" else 2], ALU.mult))
                    for i in range(TT):
                        out, o = mix[:, i, at:at + HD], O[u % 2][:, i * HD:(i + 1) * HD]
                        if kind != "win":
                            last = nc.vector.tensor_scalar(out, o, f[:, i:i + 1], None, ALU.mult)
                        else:
                            last = nc.vector.scalar_tensor_tensor(out=out, in0=o, scalar=f[:, i:i + 1], in1=out,
                                                                  op0=ALU.mult, op1=ALU.add)
                    last.then_inc(A["o_ev"], 1)

                for step in range(NU + LAG_V):
                    if step < NU:
                        logits(step)
                    if step >= LAG_V:
                        outputs(step - LAG_V)
                    select_keys(step - SELECT_AT)
                    compressed(step)
                    dilations(step)
                lo_a(A_WIN)
                lo_features(A, 1, None)
                for c in range(A_WOUT):
                    lo_a(A_WIN + c + 1)
                    dve.wait_ge(chunk_mm, split + (A_WIN + c + 1 + NEW))
                    cols = slice(c * GW, (c + 1) * GW)
                    nc.vector.tensor_tensor(x[:, :, cols], x[:, :, cols], G[c % 2][:, :].rearrange("p (t n) -> p t n", t=TT),
                                            ALU.add).then_inc(A["x"], 1)
                rms_norm(A, 0, A, 1)
                lo_features(A, 2, "g2")
                ffn(A, split + (A_WIN + A_WOUT), 0, 0, conv=True, part=l)
                dve.wait_ge(ada_used, l * ADA_N + ADA_N)
                nc.vector.tensor_tensor(mod[:, bass.ds(l, 1), :].rearrange("p o n -> p (o n)"), moda[:, :], sa("ada_b"), ALU.add)
                for i in range(TT):
                    if i == 0:
                        dve.wait_ge(A["y0"], 1)
                    else:
                        dve.wait_ge(chunk_mm, split + (A_S + NEW))
                    for half in range(2):
                        cols = slice(half * 512, half * 512 + 512)
                        last = nc.vector.tensor_tensor(x[:, i, cols], x[:, i, cols], ACC[2 * i + half][:, :], ALU.add)
                    last.then_inc(A["x"], 1)
                dve.drain().then_inc(layer_done, 1)
                dve.wait_ge(layer_go, l + 1)
            normed(NEXT, DEPTH, FIN, 0)
            for i in range(TT):
                nc.vector.scalar_tensor_tensor(out=x[:, i, :], in0=x[:, i, :], scalar=st[:, 4 + i:5 + i], in1=lnw[:, 0, :],
                                               op0=ALU.mult, op1=ALU.mult).then_inc(FIN["x"], 1)

            def gate_diagonal(sub):
                nc.vector.tensor_tensor(gdiag, ident.unsqueeze(1).to_broadcast([P, KT, P]),
                                        modc(sub, 2).unsqueeze(2).to_broadcast([P, KT, P]), ALU.mult).then_inc(B["gdiag"], 1)

            def lo_mod(v):
                for k in range(KT):
                    dve.wait_ge(B["tp_hi"], v * KT + k + 1)
                    nc.vector.tensor_tensor(hT_lo[:, k, :], hx[:, k % 4, :], hT_hi[:, k, :].bitcast(F32),
                                            ALU.subtract).then_inc(B["tp_lo"], 1)

            dve.wait_ge(FIN["x"], TT)
            with dve.Fori(0, DEPTH) as l:
                split = l * B_N + S_A
                steps = 0

                def mark(ins):
                    nonlocal steps
                    steps += 1
                    ins.then_inc(B["dve"], 1)
                    return steps

                def link(ins):
                    nonlocal steps
                    steps += 1
                    ins.then_inc(B["dve"], 1)
                    dve.wait_ge(B["dve"], steps)

                def lo_b(s):
                    lo(split + s, s % RING, s % RING, b_width(s))

                def residual(pieces):
                    done = []
                    for k, (i, half, ys) in enumerate(pieces):
                        for xc, y in ys:
                            at = xc.start - half * 512
                            last = nc.vector.tensor_tensor(part[:, k, at:at + xc.stop - xc.start], y, gateb[:, xc], ALU.mult)
                        done.append(mark(last))
                    for k, (i, half, _) in enumerate(pieces):
                        cols = slice(half * 512, half * 512 + 512)
                        dve.wait_ge(B["dve"], done[k])
                        done.append(mark(nc.vector.scalar_tensor_tensor(out=x[:, i, cols], in0=x[:, i, cols], scalar=ALPHA,
                                                                        in1=part[:, k, :], op0=ALU.mult, op1=ALU.add)))
                    for k, (i, half, _) in enumerate(pieces):
                        dve.wait_ge(B["dve"], done[2 + k])
                        last = nc.vector.bn_stats(bst[:, i, half, :], x[:, i, half * 512:half * 512 + 512])
                    link(last)

                def from_down(i):
                    return [(i, half, [(slice(half * 512, half * 512 + 512), ACC[2 * i + half][:, :])]) for half in range(2)]

                def from_wout(half):
                    cols = lambda c: slice(half * 512 + c * GW, half * 512 + (c + 1) * GW)
                    return [(i, half, [(cols(c), ACC[2 * half + c][:, i * GW:(i + 1) * GW]) for c in range(2)]) for i in range(TT)]

                def residual_down(sub, done):
                    if sub:
                        dve.wait_ge(B["xg"], 2 * sub)
                    dve.wait_ge(B["y0"], sub // 2 + 1)
                    residual(from_down(0))
                    dve.wait_ge(chunk_mm, done)
                    residual(from_down(1))

                def layer_norm(sub):
                    for i in range(TT):
                        last = nc.vector.bn_aggr(bag[:, i, :], bst[:, i, :, :].rearrange("p a b -> p (a b)"))
                    last.then_inc(B["std"], 1)
                    dve.wait_ge(B["std"], 2 * sub + 2)
                    link(nc.vector.reciprocal(st[:, 10:12], st[:, 8:10]))
                    for i in range(TT):
                        nc.vector.tensor_scalar(x[:, i, :], x[:, i, :], bag[:, i, 0:1], st[:, 10 + i:11 + i],
                                                ALU.subtract, ALU.mult).then_inc(B["nx"], 1)
                    if sub == 2:
                        dve.wait_ge(ln_in, l * 96 + 32 * (sub + 1))
                        done = []
                        for i in range(TT):
                            dve.wait_ge(B["nx"], sub * TT + i + 1)
                            done.append(mark(nc.vector.tensor_tensor(x[:, i, :], x[:, i, :], lnw[:, 0, :], ALU.mult)))
                        for i in range(TT):
                            dve.wait_ge(B["dve"], done[i])
                            nc.vector.tensor_tensor(x[:, i, :], x[:, i, :], lnw[:, 1, :], ALU.add)

                link(nc.vector.tensor_copy(modl[:, 0:MOD2], mod[:, bass.ds(l, 1), :].rearrange("p o n -> p (o n)")))
                by_kind = modl[:, :].rearrange("p (s w n) -> p s w n", s=3, w=3)
                link(nc.vector.tensor_scalar(by_kind[:, 0, 1:3, :], by_kind[:, 0, 1:3, :], 1.0, None, ALU.add))
                nc.vector.tensor_scalar(modc(0, 2), modc(0, 2), 0.5, None, ALU.mult).then_inc(B["modl"], 1)
                dve.wait_ge(B["modl"], 1)
                gate_diagonal(0)
                lo_b(0)
                lo_mod(0)
                ffn(B, split, 0, 2, part=l + DEPTH)
                dve.wait_ge(small_in, l * 16 + (DEPTH * 16 + 16))
                dve.wait_ge(ada_used, (l + DEPTH) * ADA_N + ADA_N)
                link(nc.vector.tensor_tensor(modl[:, MOD2:MOD], moda[:, :], sbp("ada_b"), ALU.add))
                link(nc.vector.tensor_scalar(by_kind[:, 1:3, 1:3, :], by_kind[:, 1:3, 1:3, :], 1.0, None, ALU.add))
                link(nc.vector.tensor_scalar(modc(2, 2), modc(2, 2), 0.5, None, ALU.mult))
                scales = by_kind[:, 1:3, 1, :]
                link(nc.vector.tensor_tensor(bshift, sbp("ln_b").rearrange("p (s n) -> p s n", s=2), scales, ALU.mult))
                nc.vector.tensor_tensor(by_kind[:, 1:3, 0, :], by_kind[:, 1:3, 0, :], bshift, ALU.add)
                nc.vector.tensor_tensor(scales, scales, sbp("ln_g").rearrange("p (s n) -> p s n", s=2), ALU.mult
                                        ).then_inc(B["modl"], 1)
                gate_diagonal(1)
                residual_down(0, split + (FFN_N + NEW))
                layer_norm(0)
                lo_mod(1)

                def prelude(c):
                    if c == 2:
                        dve.wait_ge(B["gtok"], 1)
                        link(nc.vector.tensor_tensor(gt, S[0][:, 0:TT * GATES].rearrange("p (t n) -> p t n", t=TT),
                                                     sbp("gate_bias").unsqueeze(1).to_broadcast([P, TT, GATES]), ALU.add))
                        nc.vector.tensor_scalar(sig, gt[:, :, 12:18], -80.0, None, ALU.max)
                        nc.vector.scalar_tensor_tensor(out=ga, in0=gt[:, :, 0:12], scalar=-1.0, in1=gt[:, :, 0:12], op0=ALU.mult,
                                                       op1=ALU.max).then_inc(B["gt"], 1)
                    if c == 4:
                        dve.wait_ge(B["gln"], 1)
                        link(nc.vector.scalar_tensor_tensor(out=gl[:, :, 0:6], in0=gt[:, :, 0:6], scalar=0.0, in1=gl1[:, :, 0:6],
                                                            op0=ALU.max, op1=ALU.add))
                        link(nc.vector.scalar_tensor_tensor(out=gl[:, :, 0:6], in0=gl[:, :, 0:6], scalar=-1.0,
                                                            in1=ealog.unsqueeze(1).to_broadcast([P, TT, 6]), op0=ALU.mult, op1=ALU.mult))
                        nc.vector.scalar_tensor_tensor(out=gl[:, :, 6:12], in0=gt[:, :, 6:12], scalar=0.0, in1=gl1[:, :, 6:12],
                                                       op0=ALU.min, op1=ALU.subtract).then_inc(B["gl"], 1)
                        link(nc.vector.tensor_scalar(beta, beta, 1.0, None, ALU.add))
                        link(nc.vector.reciprocal(beta, beta))
                    if c == 6:
                        dve.wait_ge(B["cum"], 1)
                        link(nc.vector.tensor_copy(cg, S[1][:, 0:24].rearrange("p (t n) -> p t n", t=TT)))
                        nc.vector.tensor_copy(ngr[:, :, 0:6], cg[:, :, 0:6])
                        nc.vector.tensor_scalar(negG, cg[:, :, 0:6], -1.0, None, ALU.mult)
                        nc.vector.tensor_tensor(ngr[:, :, 6:12], gt[:, :, 18:24], cg[:, :, 6:12], ALU.subtract).then_inc(B["cg"], 1)
                    if c == 9:
                        dve.wait_ge(B["rows_ev"], 4)
                        nc.vector.tensor_tensor_scan(row_m[0:6, :], row_f[0:6, :], row_i[0:6, :], 0.0, ALU.add, ALU.max
                                                     ).then_inc(B["scan"], 1)
                    if c == 11:
                        dve.wait_ge(B["ssr"], 1)
                        nc.vector.reciprocal(norm_r[0:12, :], norm_r[0:12, :]).then_inc(B["rn"], 1)
                        dve.wait_ge(B["mback"], 1)
                        nc.vector.tensor_tensor(bm, cg[:, :, 6:12], S[1][:, 32:44].rearrange("p (t h) -> p t h", t=TT),
                                                ALU.subtract).then_inc(B["bm"], 1)
                    if c == 13:
                        for f in range(3):
                            dve.wait_ge(B["rnb"], f + 1)
                            qk = fm[:, 2 * f:2 * f + 2, :]
                            nc.vector.tensor_tensor(qk, qk, RN[f][:, :].rearrange("p (k n) -> p k n", k=2), ALU.mult
                                                    ).then_inc(B["rnb_ev"], 1)
                    if c == 14:
                        dve.wait_ge(B["rnb_ev"], 3)
                        dve.wait_ge(B["bb"], 1)
                        for f in range(3):
                            nc.vector.tensor_tensor(kbT[:, f, :], fm[:, F_GK + f, :], PT[f // 2][:, f % 2 * SEQ:(f % 2 + 1) * SEQ],
                                                    ALU.mult).then_inc(B["kb"], 1)
                    if c == 16:
                        for i in range(TT):
                            dve.wait_ge(B["vt"], i + 1)
                            nc.vector.tensor_tensor(vb[:, i, :, :], RN[i][:, 0:384].rearrange("p (h d) -> p h d", d=HD),
                                                    beta[:, i, :].unsqueeze(2).to_broadcast([P, GDN_H, HD]), ALU.mult).then_inc(B["vb"], 1)

                ntap = 0
                for c, (ftiles, _, _) in enumerate(B_WIN):
                    lo_b(B_S0["win"] + c + 1)
                    if ftiles and ftiles[0] in F_CONV:
                        ntap += len(ftiles)
                        dve.wait_ge(B["tap"], ntap)
                        for d in range(1, TAPS):
                            for k, f in enumerate(ftiles):
                                last = nc.vector.scalar_tensor_tensor(
                                    out=cvb[:, c % 2, k, d:SEQ], in0=G[c % 2][:, k * SEQ:(k + 1) * SEQ - d], scalar=tap(f, TAPS - 1 - d),
                                    in1=cvb[:, c % 2, k, d:SEQ], op0=ALU.mult, op1=ALU.add)
                            if d < TAPS - 1:
                                link(last)
                        last.then_inc(B["conv"], 1)
                    prelude(c)

                def logits_b(u):
                    kind, h = B_UNITS[u]
                    dve.wait_ge(B["s"], u + 1)
                    if u >= 2:
                        dve.wait_ge(B["e"], u - 1)
                    if kind == "moba":
                        ins = nc.vector.scalar_tensor_tensor(out=lgb[:, u % 2, :], in0=S[u % 2][:, 0:CAUS], scalar=SCALE,
                                                             in1=const("causal"), op0=ALU.mult, op1=ALU.add)
                        ins.then_inc(B["s_free"], 1)
                        dve.wait_ge(B["s_free"], u + 1)
                        nc.vector.tensor_reduce(nmaxb[:, u, 0:1], lgb[:, u % 2, 0:P], AX.X, ALU.max, negate=True)
                        nc.vector.tensor_reduce(nmaxb[:, u, 1:2], lgb[:, u % 2, P:CAUS], AX.X, ALU.max, negate=True).then_inc(B["nm"], 1)
                    else:
                        nc.vector.tensor_tensor(lgb[:, u % 2, 0:P], G[u % 2][:, 0:P], const("causal")[:, 0:P], ALU.add)
                        nc.vector.tensor_tensor(lgb[:, u % 2, P:CAUS], G[u % 2][:, 0:SEQ], const("causal")[:, P:CAUS],
                                                ALU.add).then_inc(B["nm"], 1)

                def weigh(u):
                    if not 0 <= u < NUB or B_UNITS[u][0] != "mlstm":
                        return
                    dve.wait_ge(B["e"], u + 1)
                    for i, cols in enumerate((slice(0, P), slice(P, CAUS))):
                        last = nc.vector.scalar_tensor_tensor(out=prb[:, u % 2, cols], in0=S[u % 2][:, cols], scalar=SCALE,
                                                              in1=prb[:, u % 2, cols], op0=ALU.mult, op1=ALU.mult,
                                                              accum_out=denb[:, u, i:i + 1])
                    last.then_inc(B["p"], 1)

                def outputs_b(u):
                    kind, h = B_UNITS[u]
                    dve.wait_ge(B["o"], u + 1)
                    o = O[u % 2][:, 0:TT * HD].rearrange("p (t d) -> p t d", t=TT)
                    if kind == "moba":
                        link(nc.vector.reciprocal(rdenb[:, u % 2, :], denb[:, u, :]))
                        nc.vector.tensor_tensor(mixb[:, :, 384 + h * HD:384 + (h + 1) * HD], o,
                                                rdenb[:, u % 2, :].unsqueeze(2).to_broadcast([P, TT, HD]), ALU.mult).then_inc(B["o_ev"], 1)
                    else:
                        nc.vector.tensor_copy(mixb[:, :, 640 + h * HD:640 + (h + 1) * HD], o).then_inc(B["o_ev"], 1)

                dve.wait_ge(B["rows_ev"], 4)
                for step in range(NUB + B_LAGV):
                    weigh(step - B_LAGP)
                    if step < NUB:
                        logits_b(step)
                    if step >= B_LAGV:
                        outputs_b(step - B_LAGV)

                for h in range(GDN_H):
                    dve.wait_ge(B["ds"], h + 1)
                    nc.vector.tensor_tensor(dec[h % 2][:, 0:SEQ], G[h % 2][:, 0:SEQ], const("causalT")[:, 0:SEQ], ALU.add)
                    nc.vector.tensor_tensor(dec[h % 2][:, SEQ:CAUS], G[h % 2][:, P:SEQ], const("causalT")[:, SEQ:CAUS],
                                            ALU.add).then_inc(B["dl"], 1)
                    dve.wait_ge(B["dec"], h + 1)
                    nc.vector.scalar_tensor_tensor(out=attnT[:, h, :], in0=S[h % 2][:, 0:CAUS], scalar=SCALE, in1=dec[h % 2],
                                                   op0=ALU.mult, op1=ALU.mult)
                    nc.vector.tensor_tensor(sysT[:, h, :], PT[h % 2][:, 0:CAUS], dec[h % 2], ALU.mult).then_inc(B["dmul"], 1)
                    dve.wait_ge(B["dmul"], h + 1)
                    v = xx[:, 2 * h:2 * h + 2, 1, :]
                    link(nc.vector.tensor_tensor(v, sysT[:, h, :].rearrange("p (k n) -> p k n", n=P)[:, 0:3:2, :],
                                                 const("lev0").unsqueeze(1).to_broadcast([P, 2, P]), ALU.mult))
                    nc.vector.tensor_tensor(v, ident.unsqueeze(1).to_broadcast([P, 2, P]), v, ALU.subtract).then_inc(B["xinit"], 1)
                dve.wait_ge(B["xinit"], GDN_H)
                NZ = (LEVELS - 1) * 2 * GDN_H
                heads = lambda v: v.rearrange("p t (h d) -> p t h d", d=HD)
                wide = lambda v: v.unsqueeze(3).to_broadcast([P, TT, 6, HD])
                hc = heads(mixb[:, :, 640:DM])
                dn = denb[:, MOBA_H:NUB, :].rearrange("p h t -> p t h")

                def mlstm_norm(n):
                    if n == 4:
                        link(nc.vector.scalar_tensor_tensor(out=hst2, in0=dn, scalar=-1.0, in1=dn, op0=ALU.mult, op1=ALU.max))
                        link(nc.vector.tensor_tensor(hst2, hst2, em, ALU.max))
                        link(nc.vector.reciprocal(hst2, hst2))
                        link(nc.vector.tensor_tensor(hc, hc, wide(hst2), ALU.mult))
                    if n == 8:
                        dve.wait_ge(B["act"], 2)
                        link(nc.vector.tensor_tensor(hc, hc, heads(tm[:, :, OC:OC + 384]), ALU.mult))
                    if n == 12:
                        link(nc.vector.tensor_reduce(hst2, hc, AX.X, ALU.add))
                        link(nc.vector.tensor_scalar(hst2, hst2, 1.0 / HD, None, ALU.mult))
                    if n == 16:
                        link(nc.vector.tensor_tensor(hc, hc, wide(hst2), ALU.subtract))
                    if n == 20:
                        link(nc.vector.tensor_tensor(heads(uu), hc, hc, ALU.mult))
                    if n == 24:
                        nc.vector.tensor_reduce(hst3, heads(uu), AX.X, ALU.add).then_inc(B["lvar"], 1)
                    if n == 32:
                        dve.wait_ge(B["lrs"], 1)
                        link(nc.vector.reciprocal(hst3, hst3))
                        link(nc.vector.tensor_tensor(hc, hc, wide(hst3), ALU.mult))
                    if n == 36:
                        nc.vector.tensor_tensor(mixb[:, :, 640:DM], mixb[:, :, 640:DM],
                                                sbp("ml_norm").unsqueeze(1).to_broadcast([P, TT, 384]), ALU.mult).then_inc(B["mix"], 1)

                for n in range(NZ):
                    mlstm_norm(n)
                    dve.wait_ge(B["z"], n + 1)
                    first = 0 if n < NZ - 2 * GDN_H else 1
                    v = xx[:, n % (2 * GDN_H), first:, :]
                    nc.vector.tensor_tensor(v, v, ps[4 + n % 4][:, first * P:SEQ].rearrange("p (k n) -> p k n", n=P),
                                            ALU.subtract).then_inc(B["xx"], 1)
                dve.wait_ge(B["u"], 2)
                vb1 = vb[:, 1, :, :].rearrange("p h d -> p (h d)")
                nc.vector.tensor_tensor(vb1, vb1, ps[1][:, 0:384], ALU.subtract).then_inc(B["w1"], 1)

                dve.wait_ge(B["gsq"], 2)
                nc.vector.tensor_reduce(hst, heads(sq2), AX.X, ALU.add).then_inc(B["gms"], 1)
                dve.wait_ge(B["grs"], 1)
                link(nc.vector.reciprocal(hst, hst))
                oa = heads(mixb[:, :, 0:384])
                for i in range(TT):
                    last = nc.vector.tensor_tensor(oa[:, i], ps[6 + i][:, 0:384].rearrange("p (h d) -> p h d", d=HD),
                                                   hst[:, i, :].unsqueeze(2).to_broadcast([P, 6, HD]), ALU.mult)
                link(last)
                link(nc.vector.tensor_tensor(oa, oa, sbp("gdn_norm").unsqueeze(1).unsqueeze(1).to_broadcast([P, TT, 6, HD]), ALU.mult))
                nc.vector.tensor_tensor(mixb[:, :, 0:384], mixb[:, :, 0:384], tm[:, :, ZC:ZC + 384], ALU.mult).then_inc(B["mix"], 1)
                lo_features(B, 2, None, LATE)
                gate_diagonal(2)
                for c in range(B_WOUT):
                    lo_b(B_S0["wout"] + c + 1)
                    if c >= 2:
                        dve.wait_ge(B["xg"], 2)
                        dve.wait_ge(chunk_mm, split + (B_S0["wout"] + 2 * (c - 1) + NEW))
                        residual(from_wout(c - 2))
                layer_norm(1)
                lo_mod(3)
                ffn(B, split + B_S0["ffn1"], FT, 0)
                residual_down(2, split + (B_N + NEW))
                layer_norm(2)
                dve.drain().then_inc(layer_done, 1)
                dve.wait_ge(layer_go, l + (DEPTH + 1))
    return nc


def pack_first(inputs):
    f = lambda n: np.asarray(inputs[n], np.float32)
    wa = np.zeros((DEPTH, A_N, P, CW), np.float32)
    w_in, w1, w_out, w_up, w_down = f("w_in"), f("cmp_w1"), f("w_out"), f("w_up"), f("w_down")
    tiles = lambda a: a.reshape(KT, P, -1).transpose(1, 0, 2)
    order = np.concatenate([np.arange(SRC[n][0], SRC[n][0] + SRC[n][1]) for n in COL])
    for l in range(DEPTH):
        w = np.zeros((DM, PJW), np.float32)
        w[:, :D_IN] = w_in[l][:, order]
        for c, width in enumerate(WIN_A):
            wa[l, c, :, :KT * width] = tiles(w[:, c * GW:c * GW + width]).reshape(P, -1)
        cmp1 = w1[l].reshape(2, CBLK, HD, P).transpose(0, 2, 1, 3).reshape(P, CBLK * P)
        at = 0
        for n in range(A_N0["cmp"], A_N0["wout"]):
            wa[l, n, :, :a_width(n)] = cmp1[:, at:at + a_width(n)]
            at += a_width(n)
        for c in range(A_WOUT):
            wa[l, A_N0["wout"] + c] = tiles(w_out[l][:, c * GW:(c + 1) * GW]).reshape(P, CW)
        wa[l, A_N0["ffn"]:] = pack_ffn(w_up[l], w_down[l])
    sa = np.zeros((DEPTH, P, SA_W), np.float32)
    col = lambda v: v.reshape(-1, P).T
    for l in range(DEPTH):
        def put(name, a):
            at, w = SA[name]
            sa[l, :, at:at + w] = a.reshape(P, w)
        put("g1", col(f("norm1_g")[l]))
        put("g2", col(f("norm2_g")[l]))
        taps = np.concatenate([f("conv_w")[l], f("conv_b")[l][None]], 0)
        put("conv", taps.reshape(4, FT, P).transpose(2, 1, 0))
        put("pos", f("cmp_pos")[l].transpose(0, 2, 1).reshape(P, CBLK))
        w2 = f("cmp_w2")[l]
        put("w2k", np.concatenate([w2[0], w2[0]], 1))
        put("w2v", w2[1])
        put("ada_b", col(f("ada_b_2")[l])[:, :MOD2])
    wm = f("ada_w_2").reshape(DEPTH, DM, 2 * ADA_N, 2, P).transpose(0, 2, 4, 3, 1).reshape(DEPTH, 2 * ADA_N, P, CW)
    return {"wa": wa, "sa": sa, "wm": wm, "const": CONST, "x": f("x"), "c": f("c_2")[0],
            "final_g": f("final_g")}


def pack_second(inputs):
    f = lambda n: np.asarray(inputs[n + "_2"], np.float32)
    w13, w2, w_in, w_out = f("ffn_w13"), f("ffn_w2"), f("w_in"), f("w_out")
    tiles = lambda a: a.reshape(KT, P, -1).transpose(1, 0, 2)
    r = np.arange
    feat = np.concatenate([r(0, 1152), r(2316, 3084), r(1548, 2060)])
    tok = np.concatenate([r(1164, 1548), r(2060, 2316), r(3084, 3468), r(3480, 3864)])
    gates = np.concatenate([r(1152, 1158), r(3474, 3480), r(1158, 1164), r(3468, 3474)])
    wb = np.zeros((DEPTH, B_N, P, CW), np.float32)
    sb = np.zeros((DEPTH, P, SB_W), np.float32)
    for l in range(DEPTH):
        wb[l, :FFN_N] = pack_ffn(w13[l, 0], w2[l, 0])
        wb[l, B_S0["ffn1"]:] = pack_ffn(w13[l, 1], w2[l, 1])
        for c, (ftiles, at, width) in enumerate(B_WIN):
            cols = np.concatenate([feat[P * k:P * (k + 1)] for k in ftiles] + [tok[at:at + width]]).astype(int) if c else gates
            wb[l, B_S0["win"] + c, :, :KT * len(cols)] = tiles(w_in[l][:, cols]).reshape(P, -1)
        for c in range(B_WOUT):
            wb[l, B_S0["wout"] + c] = tiles(w_out[l][:, c * GW:(c + 1) * GW]).reshape(P, CW)

        def put(name, a):
            at, w = SB[name]
            sb[l, :, at:at + w] = a.reshape(-1, w) if a.ndim == 1 else a.reshape(P, w)
        taps = np.concatenate([f("gdn_conv")[l], f("mlstm_conv")[l]], 1)
        put("conv", taps.reshape(TAPS, 15, P).transpose(2, 1, 0))
        put("gate_bias", np.concatenate([f("gdn_dt_bias")[l], f("mlstm_f_bias")[l], np.zeros(6, np.float32), f("mlstm_i_bias")[l]]))
        put("a_log", f("gdn_a_log")[l])
        put("gdn_norm", f("gdn_norm")[l])
        put("ml_norm", f("mlstm_norm")[l])
        put("ada_b", f("ada_b")[l].reshape(-1, P).T[:, MOD2:])
        for name in ("ln_g", "ln_b"):
            put(name, f(name)[l, :2].reshape(-1, P).T)
    return {"wb": wb, "sb": sb, "ln_g": f("ln_g"), "ln_b": f("ln_b")}


def pack_ffn(up, down):
    out = np.zeros((FFN_N, P, CW), np.float32)
    u = up.reshape(KT, P, 2, FT, P)
    for f in range(FT):
        pos = 0 if f == 0 else 1 + 3 * ((f - 1) // 2) + (f - 1) % 2
        out[pos] = u[:, :, :, f, :].transpose(1, 0, 2, 3).reshape(P, CW)
    d = down.reshape(FT // 2, 2, P, DM)
    for i in range(FT // 2):
        pos = 3 + 3 * i if i < FT // 2 - 1 else FFN_N - 1
        out[pos] = d[i].transpose(1, 0, 2).reshape(P, CW)
    return out


def kernel(**inputs):
    import concourse.bacc as bacc
    from concourse.bass_utils import run_bass_kernel_spmd

    nc = bacc.Bacc("TRN2", target_bir_lowering=False, num_devices=1)
    arrays, tensors = {}, {}
    for name, a in {**pack_first(inputs), **pack_second(inputs)}.items():
        arrays["in_" + name] = np.ascontiguousarray(a)
        tensors[name] = nc.dram_tensor("in_" + name, a.shape, F32, kind="ExternalInput").ap()
    tensors["out"] = nc.dram_tensor("out", (1, SEQ, DM), F32, kind="ExternalOutput").ap()
    build(nc, tensors)
    return run_bass_kernel_spmd(nc, [arrays], core_ids=[0]).results[0]["out"]
```

```python
from contextlib import ExitStack

import numpy as np

import concourse.bass as bass
from concourse import mybir

F32 = mybir.dt.float32
F32R = mybir.dt.float32r
ACT = mybir.ActivationFunctionType
ALU = mybir.AluOpType
AX = mybir.AxisListType

P = 128
SEQ, DM, DEPTH = 256, 1024, 2
TT = SEQ // P
KT = DM // P
HD = 64
SCALE = HD ** -0.5
NEG = -1e30
DFF = 2816
FT = DFF // P
NORM_EPS, LN_EPS = 1e-6, 1e-5
ALPHA = (2 * DEPTH) ** 0.25
CW = 2048
RING = 3
CAUS = P + SEQ

NSA_H, DSA_H, DIL_H, IDX_H, IDX_D = 5, 5, 6, 8, 32
SRC = {}
_o = 0
for _n, _w in (("aq", 320), ("kc", 64), ("vc", 64), ("ks", 64), ("vs", 64), ("kw", 64), ("vw", 64), ("ag", 15),
               ("bq", 320), ("bk", 64), ("bv", 64), ("iq", 256), ("ik", 32), ("iw", 8),
               ("cq", 384), ("ck", 384), ("cv", 384)):
    SRC[_n] = (_o, _w)
    _o += _w
D_IN = _o
COL = {}
_o = 0
for _n in ("aq", "ks", "kw", "bq", "bk", "cq", "ck", "iq", "ik", "kc", "vc", "vs", "vw", "bv", "cv", "ag", "iw"):
    COL[_n] = _o
    _o += SRC[_n][1]
ROT_H = 25
ROT_I = IDX_H + 1
GW = 256
PJW = D_IN + D_IN % 2
WIN_A = [min(GW, PJW - c) for c in range(0, PJW, GW)]
NCMP, CBLK, CSTR = 15, 32, 16
TOPK = SEQ // 4

A_WIN, A_CMP, A_WOUT, FFN_N = len(WIN_A), 3, 4, 33
MOD = 9 * KT
MOD2 = MOD // 2
ADA_N = MOD2 // 2
ADA_T = ADA_N // RING
A_N0 = {"win": 0, "cmp": A_WIN, "wout": A_WIN + A_CMP}
A_N0["ffn"] = A_N0["wout"] + A_WOUT
A_N = A_N0["ffn"] + FFN_N
A_S = A_WIN + A_WOUT + FFN_N
A_D = A_CMP
assert A_N % RING == 0 and A_S % RING == 0 and A_N0["ffn"] % RING == 0 and (A_WIN + A_WOUT) % RING == 0

TB = [("aq", 0, 128, 1), ("aq", 128, 128, 1), ("aq", 256, 128, 1), ("kc", 0, 128, 1),
      ("iq", 0, 128, 1), ("iq", 128, 128, 1), ("ik", 0, 32, 4), ("bk", 0, 64, 2),
      ("bq", 0, 128, 1), ("bq", 128, 128, 1), ("bq", 256, 128, 1), ("ks", 0, 64, 2), ("kw", 0, 64, 2),
      ("aq", 0, 128, 1), ("aq", 128, 128, 1), ("aq", 256, 128, 1),
      ("cq", 0, 128, 1), ("cq", 128, 128, 1), ("cq", 256, 128, 1),
      ("ck", 0, 128, 1), ("ck", 128, 128, 1), ("ck", 256, 128, 1)]
T_AQR, T_KCVC, T_IQ, T_IK, T_BK, T_BQ, T_KS, T_KW, T_AQ, T_CQ, T_CK = 0, 3, 4, 6, 7, 8, 11, 12, 13, 16, 19

CST = {}


def _constants():
    parts, at = [], 0

    def put(name, a):
        nonlocal at
        a = np.asarray(a, np.float32).reshape(a.shape[0], -1)
        if a.shape[0] < P:
            a = np.concatenate([a, np.zeros((P - a.shape[0], a.shape[1]), np.float32)])
        CST[name] = (at, a.shape[1])
        parts.append(a)
        at += a.shape[1]

    i, j = np.arange(P)[:, None], np.arange(P)[None, :]
    put("ident", np.eye(P))
    put("ones", np.ones((P, P)))
    put("upto", (i <= j).astype(np.float32))
    add = lambda ok: np.where(ok, 0.0, NEG)
    full = np.ones((P, P), bool)
    put("causal", np.concatenate([add(j <= i), add(full), add(j <= i)], 1))
    put("causalT", np.concatenate([add(i <= j), add(full), add(i <= j)], 1))
    put("dil0", np.concatenate([add(j <= i), add(j >= i), add(j <= i)], 1))
    for g, r in ((1, 4), (2, 16)):
        step = (i - j) % r == 0
        put(f"dil{g}", np.concatenate([add((j <= i) & step), add(step), add((j <= i) & step)], 1))
    t = np.arange(SEQ).reshape(TT, P).T[:, :, None]
    ok = (np.arange(NCMP) * CSTR + CBLK - 1)[None, None, :] <= t
    put("cmp_add", add(ok))
    put("cmp_keep", ok.astype(np.float32))
    for name, rot in (("h", 16), ("i", 8)):
        inv = 1.0 / (500000.0 ** (np.arange(0, rot, 2, dtype=np.float32) / np.float32(rot)))
        ang = np.arange(SEQ, dtype=np.float32)[:, None] * inv[None, :].astype(np.float32)
        for f, fn in (("cos", np.cos), ("sin", np.sin)):
            put(f + name, fn(ang).astype(np.float32).reshape(TT, P, rot // 2).transpose(1, 0, 2))
    for b in range(7):
        s = 1 << b
        put(f"lev{b}", ((i // (2 * s) == j // (2 * s)) & (j % (2 * s) >= s) & (i % (2 * s) < s)).astype(np.float32))
    put("pair_of", (i // 64 == np.arange(2)[None, :]).astype(np.float32))
    put("quad_of", (i // 32 == np.arange(4)[None, :]).astype(np.float32))
    pair = np.zeros((6, 3, P), np.float32)
    for h in range(6):
        pair[h, h // 2, 64 * (h % 2):64 * (h % 2) + 64] = 1
    put("pair", pair)
    pair12 = np.zeros((12, 6, P), np.float32)
    for h in range(12):
        pair12[h, h // 2, 64 * (h % 2):64 * (h % 2) + 64] = 1
    put("pair12", pair12)
    half = np.zeros((P, 6, 12), np.float32)
    for f in range(6):
        half[:64, f, 2 * f] = 1
        half[64:, f, 2 * f + 1] = 1
    put("half", half)
    return np.ascontiguousarray(np.concatenate(parts, 1))


CONST = _constants()


def a_chunk(n):
    if n < A_N0["cmp"]:
        return "split", n
    if n < A_N0["wout"]:
        return "direct", n - A_N0["cmp"]
    return "split", n - A_D


def a_width(n):
    if n < A_WIN:
        return KT * WIN_A[n]
    return {A_N0["cmp"] + 1: CW // 2, A_N0["cmp"] + 2: CW // 2}.get(n, CW)


def _columns(*names):
    at, out = 0, {}
    for n, w in names:
        out[n] = (at, w)
        at += w
    return out, at


SA, SA_W = _columns(("g1", KT), ("g2", KT), ("conv", FT * 4), ("pos", CBLK), ("w2k", P), ("w2v", HD), ("ada_b", MOD2))


GDN_H, MOBA_H, ML_H = 6, 4, 6
TAPS = 4
F_GQ, F_GK, F_GV, F_LQ, F_LK, F_MQ, F_MK, F_N = 0, 3, 6, 9, 12, 15, 17, 19
F_CONV = list(range(F_MQ))
ZC, VB, VC, OC, TMW = 0, 384, 640, 1024, 1408
GATES = 24
B_WIN = ([((), 0, 0)] + [((f, f + 1), 0, 0) for f in range(0, 14, 2)] + [((14,), 0, 0), ((15, 16), 0, 0), ((17, 18), 0, 0)]
         + [((), 0, P)] + [((), c, GW) for c in range(P, TMW, GW)])
N_FEAT, N_TOK = len([b for b in B_WIN if b[0]]), len([b for b in B_WIN if b[2]])
B_WOUT = 4
B_S0 = {"ffn0": 0, "win": FFN_N, "wout": FFN_N + len(B_WIN)}
B_S0["ffn1"] = B_S0["wout"] + B_WOUT
B_N = B_S0["ffn1"] + FFN_N
assert B_N % RING == 0 and B_S0["ffn1"] % RING == 0
SB, SB_W = _columns(("conv", 15 * TAPS), ("gate_bias", 24), ("a_log", GDN_H), ("gdn_norm", HD), ("ml_norm", ML_H * HD),
                      ("ada_b", MOD2), ("ln_g", 2 * KT), ("ln_b", 2 * KT))


def b_width(n):
    if B_S0["win"] <= n < B_S0["wout"]:
        f, _, w = B_WIN[n - B_S0["win"]]
        return KT * (P * len(f) + w or GATES)
    return CW


def build(nc, t, only_first=False):
    with ExitStack() as ctx:
        def sb(name, shape, dt=F32):
            return ctx.enter_context(nc.sbuf_tensor(name, shape, dt))

        def sem(name):
            return ctx.enter_context(nc.semaphore(name))

        raw = sb("raw", [P, RING, CW])
        w_hi = sb("w_hi", [P, RING, CW], F32R)
        w_lo = sb("w_lo", [P, RING, CW], F32R)
        x = sb("x", [P, TT, DM])
        hT_hi = sb("hT_hi", [P, KT, SEQ], F32R)
        hT_lo = sb("hT_lo", [P, KT, SEQ], F32R)
        hid_hi = sb("hid_hi", [P, 4, SEQ], F32R)
        hid_lo = sb("hid_lo", [P, 4, SEQ], F32R)
        cst = sb("cst", [P, CONST.shape[1]])
        spa = sb("spa", [P, max(SA_W, SB_W)])
        moda = sb("moda", [P, MOD2])
        mod = sb("mod", [P, DEPTH, MOD2])
        modl = sb("modl", [P, MOD])
        gateb = sb("gateb", [P, DM])
        lnw = sb("lnw", [P, 2, DM])
        st = sb("st", [P, 32])
        SCR = 18000
        scratch = sb("scratch", [P, SCR])

        def carver():
            at = 0

            def carve(*dims):
                nonlocal at
                n = int(np.prod(dims))
                v = scratch[:, at:at + n]
                at += n
                assert at <= SCR, at
                if len(dims) == 1:
                    return v
                names = "abcd"[:len(dims)]
                return v.rearrange(f"p ({' '.join(names)}) -> p {' '.join(names)}", **dict(zip(names, dims)))
            return carve

        carve = carver()
        xn, junk = carve(TT, DM), carve(TT, DM)
        carve = carver()
        cv, sg, h32 = carve(2, SEQ), carve(2, SEQ), carve(2, SEQ)
        ada_raw = scratch[:, SCR - RING * CW:SCR].rearrange("p (r n) -> p r n", r=RING)
        cb = scratch[:, SCR - RING * CW - DM:SCR - RING * CW]
        carve = carver()
        pj, tb = carve(TT, PJW), carve(len(TB), SEQ)
        lg, pr, pt = carve(2, CAUS), carve(2, CAUS), carve(2, CAUS)
        mix = carve(TT, DM)
        relu, isc, dmask = carve(2, CAUS), carve(CAUS), carve(CAUS)
        iws, ags, fac = carve(TT, IDX_H), carve(TT, 15), carve(2, 3, TT)
        den, nmax, rden = carve(21, TT), carve(21, TT), carve(2, 3, TT)
        m8, dmin, dexp, dfac = carve(2, 8), carve(2, TT), carve(6, TT), carve(6, TT)
        lc, mc, dc, pc = carve(TT, NSA_H, 16), carve(TT, NSA_H), carve(TT, NSA_H), carve(TT, NSA_H, 32)
        vr, hb = carve(4, 32), carve(4, 2 * NCMP)
        flat = lambda v: v.rearrange("p a b -> p (a b)")
        lent = [gateb[:, :], lnw[:, 1, :]]
        rw = lent[0][:, 0:CBLK * 2 * NCMP].rearrange("p (j n) -> p j n", n=2 * NCMP)
        pcT, pcT4 = (lent[1][:, SEQ * k:SEQ * (k + 1)].rearrange("p (t n) -> p t n", t=TT) for k in range(2))
        vbd = lent[1][:, 2 * SEQ:3 * SEQ].rearrange("p (h d) -> p h d", d=HD)
        kbd = lent[1][:, 3 * SEQ:3 * SEQ + 32].rearrange("p (h n) -> p h n", h=2)
        dup = scratch[:, TT * PJW + len(TB) * SEQ + 2 * CAUS:TT * PJW + len(TB) * SEQ + 2 * CAUS + TT * 4 * P].rearrange("p (t k n) -> p t k n", t=TT, k=4)
        KEYS = (T_BK, T_KS, T_KW, *range(T_CK, T_CK + 3))
        SHARED = KEYS[:3]
        ix_keys = flat(mix)[:, 0:4 * SEQ].rearrange("p (g n) -> p g n", g=4)
        TURNED = [b for b in range(len(TB)) if b not in KEYS]
        dil_zones = [pj[:, :, COL[n]:COL[n] + SEQ] for n in ("kw", "iq", "aq")]
        dil_keys = [z[:, i, :] for z in dil_zones for i in range(TT)]

        def keys_of(b, half):
            n = 2 * KEYS.index(b) + half
            return tb[:, len(TURNED) + n, :] if b in SHARED else dil_keys[n - 2 * len(SHARED)]

        DUP = [k for k, b in enumerate(TB) if b[3] > 1]
        rot = [flat(mix)[:, 512 * k:512 * k + 400] for k in range(4)]

        carve = carver()
        carve(6 * SEQ)
        gdiag, hx, part = carve(KT, P), carve(4, SEQ), carve(2, 512)
        bst, bag, bshift = carve(TT, 2, 6), carve(TT, 2), carve(2, KT)
        carve = carver()
        fm, tm = carve(F_N, SEQ), carve(TT, TMW)
        mixb = carve(TT, DM)
        lgb, prb, ptb = carve(2, CAUS), carve(2, CAUS), carve(2, CAUS)
        kbT, vb = carve(3, SEQ), carve(TT, GDN_H, HD)
        grow = carve(SEQ)
        xx = carve(2 * GDN_H, 2, P)
        gt, ga, gl1, gl = carve(TT, 24), carve(TT, 12), carve(TT, 12), carve(TT, 12)
        cg, ngr, beta, sig = carve(TT, 12), carve(TT, 12), carve(TT, 6), carve(TT, 6)
        bm, em, ealog, negG = carve(TT, 6), carve(TT, 6), carve(6), carve(TT, 6)
        denb, nmaxb, rdenb = carve(10, TT), carve(10, TT), carve(2, TT)
        hst, hst2, hst3 = carve(TT, 6), carve(TT, 6), carve(TT, 6)
        odd_g = carve(F_GV - F_GK, SEQ)
        odd_u = xx.rearrange("p a b c -> p (a b c)")[:, 1024:1024 + 5 * SEQ].rearrange("p (k n) -> p k n", n=SEQ)
        ODD = [(odd_g, F_GK, F_GV - F_GK), (odd_u[:, 0:3, :], F_LK, F_MQ - F_LK), (odd_u[:, 3:5, :], F_MK, F_N - F_MK)]
        EVEN_ROWS, ODD_ROWS = slice(0, HD), slice(HD, P)
        cvb = xx.rearrange("p a b c -> p (a b c)")[:, 0:1024].rearrange("p (a k n) -> p a k n", a=2, k=2)
        row_b, row_f, row_i, row_m = (flat(mixb)[:, 256 * k:256 * k + 256] for k in range(4))
        norm_r, row_g = flat(mixb)[:, 1024:1280], flat(mixb)[:, 1280:1536]
        sq = scratch[:, F_N * SEQ + TT * TMW + TT * DM:F_N * SEQ + TT * TMW + TT * DM + 6 * SEQ].rearrange("p (f n) -> p f n", f=6)
        attnT = fm.rearrange("p f n -> p (f n)")[:, F_LQ * SEQ:F_LQ * SEQ + GDN_H * CAUS].rearrange("p (h n) -> p h n", h=GDN_H)
        sysT = scratch[:, F_N * SEQ + TT * TMW + TT * DM:F_N * SEQ + TT * TMW + TT * DM + GDN_H * CAUS].rearrange(
            "p (h n) -> p h n", h=GDN_H)
        dec = [tm[:, i, VB:VB + CAUS] for i in range(2)]
        atm = tm[:, 0, VB:VB + 512].rearrange("p (k n) -> p k n", k=4)
        ym = tm[:, 1, VB:VB + 512].rearrange("p (k n) -> p k n", k=4)
        uu = kbT.rearrange("p a b -> p (a b)").rearrange("p (t n) -> p t n", t=TT)
        sq2 = xx.rearrange("p a b c -> p (a b c)")[:, 0:768].rearrange("p (t n) -> p t n", t=TT)

        ps = [ctx.enter_context(nc.psum_tensor(f"bank{i}", [P, 512], F32)) for i in range(8)]
        S, PT, O, G = ps[0:2], ps[2:4], ps[4:6], ps[6:8]
        RN = [ps[0], ps[5], ps[4]]
        UP, TP, ACC, GATE = ps[0:2], ps[2:6], ps[4:8], ps[2:4]

        def const(name, parts=P):
            a, w = CST[name]
            return cst[0:parts, a:a + w]

        ident = const("ident")

        def sa(name, i=None):
            a, w = SA[name]
            return spa[:, a:a + w] if i is None else spa[:, a + i:a + i + 1]

        def conv_tap(f, i):
            return spa[:, bass.ds(f * 4 + (SA["conv"][0] + i), 1)]

        def sbp(name, i=None):
            a, w = SB[name]
            return spa[:, a:a + w] if i is None else spa[:, a + i:a + i + 1]

        def modc(sub, which):
            return modl[:, (sub * 3 + which) * KT:(sub * 3 + which + 1) * KT]

        raw_in = [sem(f"raw_in{i}") for i in range(RING)]
        hi_done, lo_done = sem("hi_done"), sem("lo_done")
        chunk_mm = sem("chunk_mm")
        direct_mm = sem("direct_mm")
        NEW = RING
        ada_in = [sem(f"ada_in{i}") for i in range(RING)]
        ada_used = sem("ada_used")
        c_in, c_silu = sem("c_in"), sem("c_silu")
        x_in = sem("x_in")
        start_in, small_in, out_st = sem("start_in"), sem("small_in"), sem("out_st")
        ln_in = sem("ln_in")
        layer_done, layer_go = sem("layer_done"), sem("layer_go")
        FIN = {n: sem("fin_" + n) for n in ("rstd", "x")}
        NEXT = {n: sem("next_" + n) for n in ("ss", "std")}
        A = {n: sem("a_" + n) for n in (
            "ss", "std", "rstd", "xn", "tp", "tp_hi", "tp_lo", "pj", "blk", "blk_ev", "rope_i", "rope_h", "dup",
            "ix", "ix_relu", "ix_acc", "gate", "gate_e", "rw", "cg", "cg_e", "cgel", "ckv", "ckv_ev", "cs", "cnm",
            "cexp", "cp", "cpt", "cpt_ev", "co", "zero", "s", "nm", "e", "pt", "pt_ev", "o", "o_ev",
            "dila", "dila_e", "dve", "x", "c1", "cv1", "cv2", "y0", "sg", "h", "hid_hi", "hid_lo")}

        B = {n: sem("b_" + n) for n in (
            "modl", "gdiag", "gateb", "gateb_ev", "tp", "tp_mod0", "tp_mod1", "tp_hi", "tp_lo", "tap", "conv", "fm", "tm",
            "gcopy", "gtok", "gt", "ge", "gln", "gl", "cum", "cg", "rows", "rows_ev", "scan", "mback", "bm", "em",
            "sq", "ss", "ssr", "rn", "rnb", "rnb_ev", "bb", "kb", "vt", "vb",
            "s", "s_free", "nm", "e", "p", "pt", "pt_ev", "o", "o_ev",
            "zero", "odd", "ds", "dl", "dec", "dmul", "xinit", "xt", "xt_ev", "atm", "y", "y_ev", "z", "xx",
            "u", "u_ev", "w1", "go", "gsq", "gms", "grs", "gout", "lden", "lvar", "lrs", "mix",
            "dve", "act", "std", "nx", "xg", "y0", "sg", "h", "hid_hi", "hid_lo")}
        B_UNITS = [("moba", h) for h in range(MOBA_H)] + [("mlstm", h) for h in range(ML_H)]
        NUB = len(B_UNITS)
        LATE = [3, 4, 5, 6, 7, 0, 1, 2]
        LEVELS = P.bit_length() - 1
        B_LAGP, B_LAGT, B_LAGO, B_LAGV = 1, 2, 3, 4
        N_A, S_A = DEPTH * A_N // RING, DEPTH * A_S

        def arrivals_b(l, n):
            return l * (16 * B_N // RING) + 16 * (N_A + n // RING + 1)

        UNITS = ([("dil", h) for h in range(DIL_H)] + [("slc", h) for h in range(NSA_H)]
                 + [("win", h) for h in range(NSA_H)] + [("dsa", h) for h in range(DSA_H)])
        NU = len(UNITS)
        GROUPS = []
        for n_ in (DIL_H, NSA_H, NSA_H, DSA_H):
            at_ = sum(n for _, n in GROUPS)
            GROUPS += [(at_, min(3, n_)), (at_ + 3, n_ - 3)]
        PLACE = [(g, k) for g, (_, n) in enumerate(GROUPS) for k in range(n)]
        OUT_W = TT * HD
        LAG_T, LAG_O, LAG_V = 2, 3, 4
        HIDDEN_AT, GELU_AT, GELU_E_AT, GELU2_AT, CKV_AT, CKV_EV_AT = 1, 6, 7, 8, 10, 11
        CS_AT, CSM_AT, CEXP_AT, CP_AT, CPT_AT, CPT_EV_AT, CO_AT = 13, 14, 15, 16, 18, 19, 21
        JOIN_AT, SELECT_AT, DIL_AT, DIL_E_AT = 23, 2, 11, 12

        TB_AFTER = {A_WIN - 3: (0, 1), A_WIN - 2: range(2, 5), A_WIN - 1: range(5, len(TB) // 2)}
        PJ_TB = -(-(COL["kc"] + 2 * HD) // GW)

        def unit(u):
            kind, h = UNITS[u]
            if kind == "dil":
                return T_CQ + h // 2, T_CK + h // 2, 64 * (h % 2), COL["cv"] + HD * h, const(f"dil{h // 2}"), 640 + HD * h
            q, k, v, m, o = {"slc": (T_AQ, T_KS, "vs", const("causal"), 0), "win": (T_AQ, T_KW, "vw", const("causal"), 0),
                             "dsa": (T_BQ, T_BK, "bv", dmask, 320)}[kind]
            return q + h // 2, k, 64 * (h % 2), COL[v], m, o + HD * h

        def arrivals(l, n):
            return l * (16 * A_N // RING) + 16 * (n // RING + 1)

        def tap(f, i):
            return sbp("conv", F_CONV.index(f) * TAPS + i)

        def modulated_tile(v, k):
            return B[f"tp_mod{k % 2}"], (v if v < 2 else v - 1) * KT // 2 + k // 2 + 1

        block = ctx.enter_context(nc.Block())

        def load_b(sp, l, j, n0, r):
            n = n0 + r
            sp.wait_ge(lo_done, l * B_N + j * RING + (S_A + n - RING + 1 + NEW))
            sp.dma_start(raw[:, n % RING, :], t["wb"][bass.ds(l, 1), bass.ds(j * RING + n, 1), :, :]
                         .rearrange("o c p n -> (o c p) n")).then_inc(raw_in[n % RING], 16)

        @block.sync
        def _(sp):
            def load_ada(l, part, j, r):
                sp.dma_start(ada_raw[:, r, :], t["wm"][bass.ds(l, 1), bass.ds(j * RING + (part * ADA_N + r), 1), :, :]
                             .rearrange("o c p n -> (o c p) n")).then_inc(ada_in[r], 16)

            def load_ffn(l, part, load):
                for r in range(RING):
                    load(0, r)
                if part == 0:
                    sp.wait_ge(A["x"], A_WOUT)
                else:
                    sp.wait_ge(layer_go, l + DEPTH)
                sp.dma_start(cb, t["c"].partition_broadcast(P)).then_inc(c_in, 16)
                for r in range(RING):
                    load_ada(l, part, 0, r)
                with sp.Fori(0, FFN_N // RING // 2) as j:
                    for i in range(2):
                        for r in range(RING):
                            load(j * 2 + (i + 1), r)
                            if i == 0:
                                sp.wait_ge(ada_used, (l + part * DEPTH) * ADA_N + j * RING + (r + 1))
                                load_ada(l, part, j + 1, r)

            sp.dma_start(x[:, :, :], t["x"].rearrange("o (t p) d -> p (o t) d", p=P)).then_inc(x_in, 16)
            sp.dma_start(cst[:, 0:P], t["const"][:, 0:P]).then_inc(x_in, 16)
            with sp.Fori(0, DEPTH) as l:
                for n in range(A_N0["ffn"]):
                    kind, i = a_chunk(n - RING)
                    if kind == "split":
                        sp.wait_ge(lo_done, l * A_S + (i + 1 + NEW))
                    else:
                        sp.wait_ge(direct_mm, l * A_D + (i + 1))
                    w = a_width(n)
                    sp.dma_start(raw[:, n % RING, 0:w],
                                 t["wa"][bass.ds(l, 1), n, :, 0:w].rearrange("o p n -> (o p) n")).then_inc(raw_in[n % RING], 16)
                def load(j, r):
                    sp.wait_ge(lo_done, l * A_S + j * RING + (A_WIN + A_WOUT + r - RING + 1 + NEW))
                    sp.dma_start(raw[:, r, :], t["wa"][bass.ds(l, 1), bass.ds(j * RING + (A_N0["ffn"] + r), 1), :, :]
                                 .rearrange("o c p n -> (o c p) n")).then_inc(raw_in[r], 16)

                load_ffn(l, 0, load)
            with sp.Fori(0, DEPTH) as l:
                load_ffn(l, 1, lambda j, r: load_b(sp, l, j, 0, r))
                for n in range(B_S0["win"], B_S0["ffn1"]):
                    sp.wait_ge(lo_done, l * B_N + (S_A + n - RING + 1 + NEW))
                    w = b_width(n)
                    sp.dma_start(raw[:, n % RING, 0:w],
                                 t["wb"][bass.ds(l, 1), n, :, 0:w].rearrange("o p n -> (o p) n")).then_inc(raw_in[n % RING], 16)
                with sp.Fori(0, FFN_N // RING) as j:
                    for r in range(RING):
                        load_b(sp, l, j, B_S0["ffn1"], r)
            for i in range(TT):
                sp.wait_ge(FIN["x"], DEPTH * TT + i + 1)
                sp.dma_start(t["out"].rearrange("o (t p) d -> p (o t) d", p=P)[:, i, :], x[:, i, :]).then_inc(out_st, 16)
            sp.wait_ge(out_st, TT * 16)

        def pool_levels(pool):
            for lev in range(1, LEVELS):
                for u in range(2 * GDN_H):
                    n = (lev - 1) * 2 * GDN_H + u
                    if n == 0:
                        pool.wait_ge(B["dmul"], GDN_H)
                    if n >= 4:
                        pool.wait_ge(B["y"], n - 3)
                    at = 0 if u % 2 == 0 else SEQ
                    nc.gpsimd.tensor_tensor(atm[:, n % 4, :], sysT[:, u // 2, at:at + P], const(f"lev{lev}"),
                                            ALU.mult).then_inc(B["atm"], 1)

        def numbers(steps):
            n = [s_.num for s_ in steps.values()]
            assert n == list(range(n[0], n[0] + len(n)))
            return range(n[0], n[0] + len(n))

        @block.gpsimd
        def _(pool):
            pool.wait_ge(raw_in[1], 16)
            pool.dma_start(cst[:, P:], t["const"][:, P:]).then_inc(start_in, 16)
            pool.dma_start(lnw[:, 0, :], t["final_g"].partition_broadcast(P)).then_inc(start_in, 16)
            with pool.Fori(0, DEPTH) as l:
                for v in (rw, kbd, vr, pc):
                    last = nc.gpsimd.memset(v, 0.0)
                last.then_inc(A["zero"], 1)
                nc.gpsimd.memset(tb[:, len(TURNED):, :], 0.0).then_inc(A["zero"], 1)
                pool.wait_ge(A["rope_h"], 1)
                nc.gpsimd.memset(ix_keys, 0.0).then_inc(A["zero"], 1)
                for v, b in zip(dil_zones, (T_KW, T_KW, T_AQ + 2)):
                    pool.wait_ge(A["blk"], b // 2 + 1)
                    nc.gpsimd.memset(v, 0.0).then_inc(A["zero"], 1)
                pool.wait_ge(layer_done, 3)
                pool.sem_clear(layer_done)
                pool.sem_clear(numbers(A))
                pool.sem_inc(layer_go, 1)
            with pool.Fori(0, DEPTH) as l:
                for sub in range(3):
                    if sub == 0:
                        pool.wait_ge(FIN["x"], TT)
                    else:
                        pool.wait_ge(B["xg"], 2 * sub)
                    for k, name in enumerate(("ln_g", "ln_b")):
                        pool.dma_start(lnw[:, k, :], t[name][bass.ds(l, 1), sub, :].rearrange("o n -> (o n)").partition_broadcast(P)
                                       ).then_inc(ln_in, 16)
                    if sub < 2:
                        pool.wait_ge(ln_in, l * 96 + 32 * (sub + 1))
                        pool.wait_ge(B["tp"], (1 + 2 * sub) * KT + KT)
                        for k, op in enumerate((ALU.mult, ALU.add)):
                            if k:
                                pool.wait_ge(B["xg"], 2 * sub + 1)
                            nc.gpsimd.tensor_tensor(x[:, :, :], x[:, :, :], lnw[:, k, :].unsqueeze(1).to_broadcast([P, TT, DM]), op
                                                    ).then_inc(B["xg"], 1)
                    if sub == 0:
                        for odd, _, _ in ODD:
                            nc.gpsimd.memset(odd[EVEN_ROWS], 0.0)
                        nc.gpsimd.memset(grow, 0.0).then_inc(B["zero"], 1)
                        pool.wait_ge(B["odd"], len(ODD))
                        pool.wait_ge(B["kb"], 3)
                        for _, first, n in ODD:
                            last = nc.gpsimd.memset(fm[ODD_ROWS, first:first + n, :], 0.0)
                        last.then_inc(B["zero"], 1)
                        pool_levels(pool)
                pool.wait_ge(layer_done, 3)
                pool.sem_clear(layer_done)
                pool.sem_clear(numbers(B))
                pool.sem_inc(layer_go, 1)

        @block.tensor
        def _(pe):
            pe.sem_inc(chunk_mm, NEW)
            pe.wait_ge(x_in, 32)

            def products(out, pairs, features=None):
                n = len(pairs)
                for i, ((ah, al), (bh, bl)) in enumerate(pairs):
                    if features:
                        pe.wait_ge(features[0]["tp_lo"], features[1] * KT + i + 1)
                    nc.tensor.matmul(out, ah, bh, start=(i == 0), stop=False)
                    nc.tensor.matmul(out, ah, bl, start=False, stop=False)
                    last = nc.tensor.matmul(out, al, bh, start=False, stop=(i == n - 1))
                return last

            def to_features(N, v, src, modulated=False, order=range(KT)):
                for n, k in enumerate(order):
                    if n >= len(TP):
                        if modulated:
                            pe.wait_ge(*modulated_tile(v, n - len(TP)))
                        else:
                            pe.wait_ge(N["tp_lo"], v * KT + n - len(TP) + 1)
                    if k == 0 and n:
                        pe.wait_ge(N["mix"], 2)
                    for i in range(TT):
                        last = nc.tensor.transpose(TP[n % len(TP)][:, i * P:(i + 1) * P], src[:, i, k * P:(k + 1) * P], ident)
                    last.then_inc(N["tp"], 1)

            def token_chunk(out, slot, width, features=None):
                for i in range(TT):
                    rows = slice(i * P, (i + 1) * P)
                    last = products(out[:, i * width:(i + 1) * width],
                                    [((hT_hi[:, k, rows], hT_lo[:, k, rows]),
                                      (w_hi[:, slot, k * width:(k + 1) * width], w_lo[:, slot, k * width:(k + 1) * width]))
                                     for k in range(KT)], features if i == 0 else None)
                return last

            def feature_tile(out, slot, half, stride=2 * P, features=None):
                cols = lambda k: slice(k * stride + half * P, k * stride + half * P + P)
                return products(out, [((w_hi[:, slot, cols(k)], w_lo[:, slot, cols(k)]), (hT_hi[:, k, :], hT_lo[:, k, :]))
                                      for k in range(KT)], features)

            def gate_on_all(sub):
                pe.wait_ge(B["gdiag"], sub + 1)
                for half in range(2):
                    nc.tensor.matmul(GATE[half][:, :], const("ones"), gdiag[:, 4 * half:4 * half + 4, :].rearrange("p k n -> p (k n)"),
                                     start=True, stop=True).then_inc(B["gateb"], 1)

            def ffn(N, split, h0, v, gate=None):
                def up(f, f2, pos, slot, wait_bank=True, features=None):
                    pe.wait_ge(lo_done, pos + (1 + NEW) + split)
                    if wait_bank:
                        pe.wait_ge(N["h"], f + (h0 - 1))
                    feature_tile(UP[f2][:, 0:SEQ], slot, 0, features=features)
                    feature_tile(UP[f2][:, SEQ:2 * SEQ], slot, 1).then_inc(chunk_mm, 1)

                def down(f, f4, pos, slot, first=False, last_one=False):
                    pe.wait_ge(lo_done, pos + (1 + NEW) + split)
                    for k2, i in ((0, 0), (1, 0), (0, 1), (1, 1)) if last_one else ((0, 0), (0, 1), (1, 0), (1, 1)):
                        pe.wait_ge(N["hid_lo"], f + (h0 + k2 + 1))
                        rows = slice(i * P, (i + 1) * P)
                        for half in range(2):
                            cols = slice(k2 * DM + half * 512, k2 * DM + half * 512 + 512)
                            out = ACC[2 * i + half][:, :]
                            ah, al = hid_hi[:, f4 + k2, rows], hid_lo[:, f4 + k2, rows]
                            bh, bl = w_hi[:, slot, cols], w_lo[:, slot, cols]
                            nc.tensor.matmul(out, ah, bh, start=first and k2 == 0, stop=False, skip_group_check=True)
                            nc.tensor.matmul(out, ah, bl, start=False, stop=False, skip_group_check=True)
                            last = nc.tensor.matmul(out, al, bh, start=False, stop=last_one and k2 == 1, skip_group_check=True)
                        if last_one and (k2, i) == (1, 0):
                            last.then_inc(N["y0"], 1)
                    last.then_inc(chunk_mm, 1)

                def turn(j, first=False):
                    for r in range(2):
                        f, pos = j * 4 + 2 * r, j * 6 + (1 + 3 * r)
                        up(f + 1, 1, pos, 1, wait_bank=not (first and r == 0))
                        up(f + 2, 0, pos + 1, 2)
                        down(f, 2 * r, pos + 2, 0, first=first and r == 0)

                up(0, 0, 0, 0, wait_bank=False, features=(N, v))
                if gate is not None:
                    gate_on_all(gate)
                turn(0, first=True)
                with pe.Fori(1, (FT - 2) // 4) as j:
                    turn(j)
                up(FT - 1, 1, FFN_N - 2, (FFN_N - 2) % RING)
                down(FT - 2, 0, FFN_N - 1, (FFN_N - 1) % RING, last_one=True)

            with pe.Fori(0, DEPTH) as l:
                split = l * A_S
                pe.wait_ge(A["xn"], TT)
                to_features(A, 0, xn)
                for c, width in enumerate(WIN_A):
                    pe.wait_ge(lo_done, split + (c + 1 + NEW))
                    if c >= 2:
                        pe.wait_ge(A["pj"], c - 1)
                    token_chunk(G[c % 2], c % RING, width, None if c else (A, 0)).then_inc(chunk_mm, 1)
                    for b in TB_AFTER.get(c, ()):
                        if b == 0:
                            pe.wait_ge(A["pj"], PJ_TB)
                        if b == 2:
                            pe.wait_ge(A["rope_i"], 1)
                        if b == 3:
                            pe.wait_ge(A["dup"], len(DUP))
                        if b >= 2:
                            pe.wait_ge(A["blk_ev"], b - 1)
                        for k in range(2):
                            name, first, width_, copies = TB[2 * b + k]
                            for i in range(TT):
                                src = pj[:, i, COL[name] + first:COL[name] + first + width_]
                                if copies > 1:
                                    src = dup[:, i, DUP.index(2 * b + k), :]
                                last = nc.tensor.transpose(PT[b % 2][:, k * SEQ + i * P:k * SEQ + (i + 1) * P], src, ident)
                        last.then_inc(A["blk"], 1)

                pe.wait_ge(A["blk_ev"], T_IK // 2 + 1)
                for h in range(IDX_H):
                    if h >= 2:
                        pe.wait_ge(A["ix_relu"], h - 1)
                    q = T_IQ + h // 4
                    nc.tensor.matmul(S[h % 2][:, 0:P], tb[:, q, 0:P], ix_keys[:, h % 4, 0:P], start=True, stop=True)
                    nc.tensor.matmul(S[h % 2][:, P:CAUS], tb[:, q, P:SEQ], ix_keys[:, h % 4, :],
                                     start=True, stop=True).then_inc(A["ix"], 1)

                def scores(u):
                    q, k, r, _, _, _ = unit(u)
                    if u >= 2:
                        pe.wait_ge(A["nm"], u - 1)
                    queries, keys = tb[:, TURNED.index(q), :], keys_of(k, r // HD)
                    nc.tensor.matmul(S[u % 2][:, 0:P], queries[:, 0:P], keys[:, 0:P], start=True, stop=True)
                    nc.tensor.matmul(S[u % 2][:, P:CAUS], queries[:, P:SEQ], keys, start=True, stop=True).then_inc(A["s"], 1)

                def turn_weights(u):
                    pe.wait_ge(A["e"], u + 1)
                    if u >= 2:
                        pe.wait_ge(A["pt_ev"], u - 1)
                    for cols in (slice(0, P), slice(P, SEQ), slice(SEQ, CAUS)):
                        last = nc.tensor.transpose(PT[u % 2][:, cols], pr[:, u % 2, cols], ident)
                    last.then_inc(A["pt"], 1)

                def values(u):
                    _, _, _, v, _, _ = unit(u)
                    pe.wait_ge(A["pt_ev"], u + 1)
                    g, k = PLACE[u]
                    if g >= 2 and k == 0:
                        pe.wait_ge(A["o_ev"], g - 1)
                    out, w = O[g % 2][:, k * OUT_W:(k + 1) * OUT_W], pt[:, u % 2, :]
                    nc.tensor.matmul(out[:, 0:HD], w[:, 0:P], pj[:, 0, v:v + HD], start=True, stop=True)
                    nc.tensor.matmul(out[:, HD:2 * HD], w[:, P:SEQ], pj[:, 0, v:v + HD], start=True, stop=False)
                    nc.tensor.matmul(out[:, HD:2 * HD], w[:, SEQ:CAUS], pj[:, 1, v:v + HD],
                                     start=False, stop=True).then_inc(A["o"], 1)

                def hidden(part):
                    if part == 0:
                        pe.wait_ge(A["rw"], 2)
                    d, first = ((0, 0), (0, 8), (1, 0), (2, 0))[part]
                    n = A_N0["cmp"] + d
                    pe.wait_ge(raw_in[n % RING], arrivals(l, n))
                    for jj in range(8):
                        j = 8 * part + jj
                        last = nc.tensor.matmul(G[0][:, 0:2 * NCMP], raw[:, n % RING, (first + jj) * P:(first + jj + 1) * P],
                                                rw[:, j, :], start=(j == 0), stop=(j == CBLK - 1))
                    if part:
                        last.then_inc(direct_mm, 1)

                def compressed(step):
                    if HIDDEN_AT <= step < HIDDEN_AT + 4:
                        hidden(step - HIDDEN_AT)
                    if step == CKV_AT:
                        pe.wait_ge(A["cgel"], 1)
                        nc.tensor.matmul(G[1][:, 0:NCMP], sa("w2k"), hb[:, 3, 0:NCMP], start=True, stop=True)
                        nc.tensor.matmul(G[1][:, HD:2 * HD], flat(vr), sa("w2v"), start=True, stop=True).then_inc(A["ckv"], 1)
                    if step == CS_AT:
                        pe.wait_ge(A["ckv_ev"], 1)
                        for i in range(TT):
                            for b in range(3):
                                at = 32 + (i * 3 + b) * 32
                                last = nc.tensor.matmul(G[0][:, at:at + 32], tb[:, T_AQR + b, i * P:(i + 1) * P], flat(kbd),
                                                        start=True, stop=True)
                        last.then_inc(A["cs"], 1)
                    if step == CPT_AT:
                        pe.wait_ge(A["cp"], 1)
                        for i in range(TT):
                            nc.tensor.transpose(G[1][:, i * P:(i + 1) * P], pc[:, i, 0:4, :], ident)
                            last = nc.tensor.transpose(G[1][0:32, SEQ + i * P:SEQ + (i + 1) * P], pc[:, i, 4, :], ident)
                        last.then_inc(A["cpt"], 1)
                    if step == CO_AT:
                        pe.wait_ge(A["cpt_ev"], 2)
                        for i in range(TT):
                            nc.tensor.matmul(G[0][:, i * SEQ:(i + 1) * SEQ], pcT[:, i, :], flat(vbd), start=True, stop=True)
                        for i in range(TT):
                            last = nc.tensor.matmul(G[1][:, i * HD:(i + 1) * HD], pcT4[0:32, i, :], vbd[0:32, 0, :],
                                                    start=True, stop=True)
                        last.then_inc(A["co"], 1)

                pe.wait_ge(A["pj"], A_WIN)
                pe.wait_ge(A["blk_ev"], len(TB) // 2)
                pe.wait_ge(A["ix_relu"], IDX_H)
                for step in range(NU + LAG_O):
                    if step < NU:
                        scores(step)
                    if LAG_T <= step < NU + LAG_T:
                        turn_weights(step - LAG_T)
                    if step >= LAG_O:
                        values(step - LAG_O)
                    compressed(step)

                pe.wait_ge(A["o_ev"], len(GROUPS))
                to_features(A, 1, mix)
                for c in range(A_WOUT):
                    pe.wait_ge(lo_done, split + (A_WIN + c + 1 + NEW))
                    if c >= 2:
                        pe.wait_ge(A["x"], c - 1)
                    token_chunk(G[c % 2], (A_WIN + c) % RING, GW, None if c else (A, 1)).then_inc(chunk_mm, 1)
                pe.wait_ge(A["xn"], 2 * TT)
                to_features(A, 2, xn)
                ffn(A, split + (A_WIN + A_WOUT), 0, 2)
                pe.drain().then_inc(layer_done, 1)
                pe.wait_ge(layer_go, l + 1)

            pe.wait_ge(start_in, 32)
            pe.wait_ge(FIN["x"], TT)
            with pe.Fori(0, DEPTH) as l:
                split = l * B_N + S_A
                to_features(B, 0, x, modulated=True)
                ffn(B, split, 0, 0, gate=0)
                pe.wait_ge(B["nx"], TT)
                to_features(B, 1, x, modulated=True)

                def prelude(c):
                    if c == 1:
                        pe.wait_ge(B["gcopy"], 1)
                        for i in range(TT):
                            last = nc.tensor.transpose(S[0][:, i * GATES:(i + 1) * GATES], row_g[0:GATES, i * P:(i + 1) * P],
                                                       ident[0:GATES, 0:GATES])
                        last.then_inc(B["gtok"], 1)
                    if c == 5:
                        pe.wait_ge(B["gl"], 1)
                        nc.tensor.matmul(S[1][:, 0:12], const("upto"), gl[:, 0, :], start=True, stop=True)
                        nc.tensor.matmul(S[1][:, 12:24], const("ones"), gl[:, 0, :], start=True, stop=False)
                        nc.tensor.matmul(S[1][:, 12:24], const("upto"), gl[:, 1, :], start=False, stop=True).then_inc(B["cum"], 1)
                    if c == 7:
                        pe.wait_ge(B["cg"], 1)
                        pe.wait_ge(B["gateb_ev"], 4)
                        for i in range(TT):
                            cols = slice(i * P, (i + 1) * P)
                            cols2 = slice(SEQ + i * P, SEQ + (i + 1) * P)
                            nc.tensor.transpose(PT[0][0:12, cols], ngr[:, i, :], ident)
                            nc.tensor.transpose(PT[0][0:6, cols2], beta[:, i, :], ident)
                            nc.tensor.transpose(PT[1][0:6, cols], gl[:, i, 6:12], ident)
                            last = nc.tensor.transpose(PT[1][0:6, cols2], gt[:, i, 18:24], ident)
                        last.then_inc(B["rows"], 1)
                    if c == 9:
                        pe.wait_ge(B["sq"], 1)
                        half = const("half").rearrange("p (f n) -> p f n", f=6)
                        for f in range(6):
                            last = nc.tensor.matmul(O[0][0:12, 0:SEQ], half[:, f, :], sq[:, f, :], start=(f == 0), stop=(f == 5))
                        last.then_inc(B["ss"], 1)
                    if c == 10:
                        pe.wait_ge(B["scan"], 1)
                        for i in range(TT):
                            last = nc.tensor.transpose(S[1][:, 32 + i * 6:32 + i * 6 + 6], row_m[0:6, i * P:(i + 1) * P], ident[0:6, 0:6])
                        last.then_inc(B["mback"], 1)
                    if c == 12:
                        pe.wait_ge(B["rn"], 1)
                        pair12 = const("pair12", 12).rearrange("p (f n) -> p f n", f=6)
                        for f in range(6):
                            last = nc.tensor.matmul(RN[f // 2][:, f % 2 * SEQ:(f % 2 + 1) * SEQ], pair12[:, f, :], norm_r[0:12, :],
                                                    start=True, stop=True)
                            if f % 2:
                                last.then_inc(B["rnb"], 1)
                    if c == 13:
                        pe.wait_ge(B["rows_ev"], 4)
                        pair = const("pair", 6).rearrange("p (f n) -> p f n", f=3)
                        for f in range(3):
                            last = nc.tensor.matmul(PT[f // 2][:, f % 2 * SEQ:(f % 2 + 1) * SEQ], pair[:, f, :], row_b[0:6, :],
                                                    start=True, stop=True)
                        last.then_inc(B["bb"], 1)
                    if c == 15:
                        pe.wait_ge(B["rnb_ev"], 2)
                        pe.wait_ge(B["fm"], N_FEAT)
                        for i in range(TT):
                            for f in range(3):
                                last = nc.tensor.transpose(RN[i][:, f * P:(f + 1) * P], fm[:, F_GV + f, i * P:(i + 1) * P], ident)
                            last.then_inc(B["vt"], 1)

                for c, (ftiles, _, width) in enumerate(B_WIN):
                    s_ = B_S0["win"] + c
                    pe.wait_ge(lo_done, split + (s_ + 1 + NEW))
                    if c >= 2:
                        ftiles_b, _, width_b = B_WIN[c - 2]
                        if width_b:
                            pe.wait_ge(B["tm"], len([1 for b in B_WIN[:c - 1] if b[2]]))
                        elif ftiles_b:
                            pe.wait_ge(B["conv"] if ftiles_b[0] in F_CONV else B["fm"], c - 2)
                        else:
                            pe.wait_ge(B["gcopy"], 1)
                    if c == 0:
                        cols = [slice(k * GATES, (k + 1) * GATES) for k in range(KT)]
                        last = products(G[0][0:GATES, 0:SEQ], [((w_hi[:, s_ % RING, cols[k]], w_lo[:, s_ % RING, cols[k]]),
                                                                (hT_hi[:, k, :], hT_lo[:, k, :])) for k in range(KT)], (B, 1))
                    for k in range(len(ftiles)):
                        last = feature_tile(G[c % 2][:, k * SEQ:(k + 1) * SEQ], s_ % RING, k, P * len(ftiles))
                    if width:
                        last = token_chunk(G[c % 2], s_ % RING, width)
                    last.then_inc(chunk_mm, 1)
                    if c == 0:
                        gate_on_all(1)
                    prelude(c)

                def spread_row(out, r):
                    return nc.tensor.matmul(out, ident[:, r:r + 1].to_broadcast([P, P]), grow, start=True, stop=True)

                def keys_b(first, h):
                    odd = {f: v for v, f, _ in ODD}[first]
                    return odd[:, h // 2, :] if h % 2 else fm[:, first + h // 2, :]

                def scores_b(u):
                    kind, h = B_UNITS[u]
                    if 2 <= u < MOBA_H + 2:
                        pe.wait_ge(B["s_free"], u - 1)
                    elif u >= 2:
                        pe.wait_ge(B["p"], u - 1 - MOBA_H)
                    q, k = (F_MQ, F_MK) if kind == "moba" else (F_LQ, F_LK)
                    queries, keys = fm[:, q + h // 2, :], keys_b(k, h)
                    if kind == "mlstm":
                        spread_row(G[u % 2][:, 0:SEQ], 6 + h)
                    nc.tensor.matmul(S[u % 2][:, 0:P], queries[:, 0:P], keys[:, 0:P], start=True, stop=True)
                    nc.tensor.matmul(S[u % 2][:, P:CAUS], queries[:, P:SEQ], keys, start=True, stop=True).then_inc(B["s"], 1)

                def turn_b(u):
                    if B_UNITS[u][0] == "moba":
                        pe.wait_ge(B["e"], u + 1)
                    else:
                        pe.wait_ge(B["p"], u - MOBA_H + 1)
                    if u >= 2:
                        pe.wait_ge(B["pt_ev"], u - 1)
                    for cols in (slice(0, P), slice(P, SEQ), slice(SEQ, CAUS)):
                        last = nc.tensor.transpose(PT[u % 2][:, cols], prb[:, u % 2, cols], ident)
                    last.then_inc(B["pt"], 1)

                def values_b(u):
                    kind, h = B_UNITS[u]
                    v = (VB if kind == "moba" else VC) + h * HD
                    pe.wait_ge(B["pt_ev"], u + 1)
                    if u >= 2:
                        pe.wait_ge(B["o_ev"], u - 1)
                    out, w = O[u % 2], ptb[:, u % 2, :]
                    nc.tensor.matmul(out[:, 0:HD], w[:, 0:P], tm[:, 0, v:v + HD], start=True, stop=True)
                    nc.tensor.matmul(out[:, HD:2 * HD], w[:, P:SEQ], tm[:, 0, v:v + HD], start=True, stop=False)
                    nc.tensor.matmul(out[:, HD:2 * HD], w[:, SEQ:CAUS], tm[:, 1, v:v + HD], start=False, stop=True).then_inc(B["o"], 1)

                pe.wait_ge(B["fm"], N_FEAT)
                pe.wait_ge(B["tm"], N_TOK)
                pe.wait_ge(B["vb"], TT)
                pe.wait_ge(B["kb"], 3)
                pe.wait_ge(B["em"], 1)
                pe.wait_ge(B["zero"], 2)
                for step in range(NUB + B_LAGO):
                    if step < NUB:
                        scores_b(step)
                    if B_LAGT <= step < NUB + B_LAGT:
                        turn_b(step - B_LAGT)
                    if step >= B_LAGO:
                        values_b(step - B_LAGO)

                pe.wait_ge(B["o_ev"], NUB)
                for h in range(GDN_H):
                    if h >= 2:
                        pe.wait_ge(B["dl"], h - 1)
                    spread_row(G[h % 2][:, 0:SEQ], h)
                    if h >= 2:
                        pe.wait_ge(B["dmul"], h - 1)
                    kT = keys_b(F_GK, h)
                    for bank, other in ((S[h % 2], fm[:, F_GQ + h // 2, :]), (PT[h % 2], kbT[:, h // 2, :])):
                        nc.tensor.matmul(bank[:, 0:SEQ], kT[:, 0:P], other[:, 0:SEQ], start=True, stop=True)
                        last = nc.tensor.matmul(bank[:, SEQ:CAUS], kT[:, P:SEQ], other[:, P:SEQ], start=True, stop=True)
                    last.then_inc(B["ds"], 1)
                pe.wait_ge(B["dmul"], GDN_H)
                NI = 2 * GDN_H
                NZ = (LEVELS - 1) * NI
                for u in range(NI):
                    pe.wait_ge(B["xinit"], u // 2 + 1)
                    last = nc.tensor.transpose(ps[4 + u // 4][:, u % 4 * P:(u % 4 + 1) * P], xx[:, u, 1, :], ident)
                    if u % 4 == 3:
                        last.then_inc(B["xt"], 1)
                pe.wait_ge(B["xt_ev"], NI // 4)

                def inv_y(n):
                    u = n % NI
                    pe.wait_ge(B["atm"], n + 1)
                    if n >= NI:
                        pe.wait_ge(B["xx"], n - NI + 1)
                    if n >= 4:
                        pe.wait_ge(B["y_ev"], n - 3)
                    nc.tensor.matmul(ps[n % 4][:, 0:P], atm[:, n % 4, :], xx[:, u, 0, :], start=True, stop=True).then_inc(B["y"], 1)

                def inv_z(n):
                    u = n % NI
                    pe.wait_ge(B["y_ev"], n + 1)
                    if n >= 4:
                        pe.wait_ge(B["xx"], n - 3)
                    if n < NZ - NI:
                        nc.tensor.matmul(ps[4 + n % 4][:, 0:P], xx[:, u, 1, :], ym[:, n % 4, :], start=True, stop=True)
                    nc.tensor.matmul(ps[4 + n % 4][:, P:SEQ], ym[:, n % 4, :], xx[:, u, 1, :], start=True, stop=True).then_inc(B["z"], 1)

                for n in range(NZ + 2):
                    if n < NZ:
                        inv_y(n)
                    if n >= 2:
                        inv_z(n - 2)
                pe.wait_ge(B["xx"], NZ)
                pe.wait_ge(B["y_ev"], NZ)
                hd = lambda h: slice(h * HD, (h + 1) * HD)
                for h in range(GDN_H):
                    last = nc.tensor.matmul(ps[0][:, hd(h)], xx[:, 2 * h, 1, :], vb[:, 0, h, :], start=True, stop=True)
                last.then_inc(B["u"], 1)
                pe.wait_ge(B["u_ev"], 1)
                for h in range(GDN_H):
                    last = nc.tensor.matmul(ps[1][:, hd(h)], sysT[:, h, P:SEQ], uu[:, 0, hd(h)], start=True, stop=True)
                last.then_inc(B["u"], 1)
                for h in range(GDN_H):
                    last = nc.tensor.matmul(ps[6][:, hd(h)], attnT[:, h, 0:P], uu[:, 0, hd(h)], start=True, stop=True)
                last.then_inc(B["go"], 1)
                pe.wait_ge(B["w1"], 1)
                for h in range(GDN_H):
                    last = nc.tensor.matmul(ps[2][:, hd(h)], xx[:, 2 * h + 1, 1, :], vb[:, 1, h, :], start=True, stop=True)
                last.then_inc(B["u"], 1)
                pe.wait_ge(B["u_ev"], 2)
                for h in range(GDN_H):
                    nc.tensor.matmul(ps[7][:, hd(h)], attnT[:, h, P:SEQ], uu[:, 0, hd(h)], start=True, stop=False)
                    last = nc.tensor.matmul(ps[7][:, hd(h)], attnT[:, h, SEQ:CAUS], uu[:, 1, hd(h)], start=False, stop=True)
                last.then_inc(B["go"], 1)

                pe.wait_ge(B["mix"], 1)
                to_features(B, 2, mixb, order=LATE)
                pe.wait_ge(B["tp_lo"], 3 * KT)
                for c in range(B_WOUT):
                    s_ = B_S0["wout"] + c
                    pe.wait_ge(lo_done, split + (s_ + 1 + NEW))
                    token_chunk(ACC[c][:, :], s_ % RING, GW).then_inc(chunk_mm, 1)
                pe.wait_ge(B["nx"], 2 * TT)
                to_features(B, 3, x, modulated=True)
                ffn(B, split + B_S0["ffn1"], FT, 3, gate=2)
                pe.drain().then_inc(layer_done, 1)
                pe.wait_ge(layer_go, l + (DEPTH + 1))

        @block.scalar
        def _(act):
            act.wait_ge(x_in, 32)

            def load_table(f):
                nc.scalar.activation(st[:, 31:32], ident[:, 0:1], f)

            def silu_c(uses):
                act.wait_ge(c_in, uses * 16)
                nc.scalar.activation(cb, cb, ACT.Silu).then_inc(c_silu, 1)

            def hi(s, slot, raw_slot, raw_wait, width=CW):
                act.wait_ge(raw_in[raw_slot], raw_wait)
                act.wait_ge(chunk_mm, s + 1)
                nc.scalar.activation(w_hi[:, slot, 0:width], raw[:, raw_slot, 0:width], ACT.Copy).then_inc(hi_done, 1)

            def root_mean_square(N, uses, x_ready=None):
                for i in range(TT):
                    if x_ready:
                        act.wait_ge(A["x"], x_ready + i)
                    nc.scalar.activation(junk[:, i, :], x[:, i, :], ACT.Square, accum_out=st[:, i:i + 1]).then_inc(N["ss"], 1)
                act.wait_ge(N["ss"], uses * TT + TT)
                nc.scalar.activation(st[:, 2:4], st[:, 0:2], ACT.Sqrt, scale=1.0 / DM, bias=NORM_EPS).then_inc(N["std"], 1)

            def hi_features(N, v, gain, order=range(KT)):
                for n, k in enumerate(order):
                    act.wait_ge(N["tp"], v * KT + n + 1)
                    nc.scalar.activation(hT_hi[:, k, :], TP[n % len(TP)][:, 0:SEQ], ACT.Copy,
                                         scale=sa(gain, k) if gain else 1.0).then_inc(N["tp_hi"], 1)

            def ffn(N, split, raw0, h0, conv, more):
                def hi_at(pos, slot):
                    hi(pos + split, slot, slot, raw0 + after(pos))

                def after(pos):
                    return 16 * (pos // RING + 1)

                def post(f, f2, f4, pos, ahead):
                    act.wait_ge(chunk_mm, pos + (1 + NEW) + split)
                    if conv:
                        nc.scalar.activation(cv[:, f2, :], UP[f2][:, 0:SEQ], ACT.Identity, scale=conv_tap(f, 2),
                                             bias=conv_tap(f, 3)).then_inc(N["c1"], 1)
                    else:
                        nc.scalar.activation(sg[:, f2, :], UP[f2][:, 0:SEQ], ACT.Silu).then_inc(N["sg"], 1)
                    ahead()
                    if conv:
                        act.wait_ge(N["cv2"], f + (h0 + 1))
                        nc.scalar.activation(sg[:, f2, :], cv[:, f2, :], ACT.Silu).then_inc(N["sg"], 1)
                    act.wait_ge(N["h"], f + (h0 + 1))
                    nc.scalar.activation(hid_hi[:, f4, :], h32[:, f2, :], ACT.Copy).then_inc(N["hid_hi"], 1)

                def turn(j, stop=FFN_N + 2):
                    for q in range(6):
                        def ahead():
                            pos = q + 4
                            if isinstance(j, int):
                                if j * 6 + pos < stop:
                                    hi(split + (j * 6 + pos), pos % RING, pos % RING, raw0 + 16 * ((j * 6 + pos) // RING + 1))
                            else:
                                hi(j * 6 + pos + split, pos % RING, pos % RING, j * 32 + 16 * (pos // RING + 1) + raw0)
                        if q % 3 == 2:
                            ahead()
                        else:
                            f = j * 4 + (1 + q - q // 3)
                            f4 = (1 + q - q // 3) % 4
                            post(f, f4 % 2, f4, j * 6 + (1 + q), ahead)

                hi(split + 2, 2, 2, raw0 + 16)
                post(0, 0, 0, 0, lambda: hi(split + 3, 0, 0, raw0 + 32))
                turns = (FT - 2) // 4
                with act.Fori(0, turns - 1) as j:
                    turn(j)
                turn(turns - 1, FFN_N + more)
                post(FT - 1, 1, 1, FFN_N - 2,
                     (lambda: hi(split + 34, 34 % RING, 34 % RING, raw0 + 16 * 12)) if more else (lambda: None))

            root_mean_square(NEXT, 0)
            with act.Fori(0, DEPTH) as l:
                split = l * A_S

                def hi_a(s):
                    n = s if s < A_WIN else s + A_D
                    hi(split + s, s % RING, n % RING, arrivals(l, n), a_width(n))

                act.dma_start(spa[:, 0:SA_W], t["sa"][bass.ds(l, 1), :, :].rearrange("o p n -> (o p) n")).then_inc(small_in, 16)
                hi_a(0)
                act.wait_ge(small_in, l * 16 + 16)
                hi_features(A, 0, "g1")
                hi_a(1)
                for c, width in enumerate(WIN_A):
                    if c + 2 < A_WIN:
                        hi_a(c + 2)
                    act.wait_ge(chunk_mm, split + (c + 1 + NEW))
                    nc.scalar.activation(pj[:, :, c * GW:c * GW + width],
                                         G[c % 2][:, 0:TT * width].rearrange("p (t n) -> p t n", t=TT),
                                         ACT.Copy).then_inc(A["pj"], 1)
                    for b in TB_AFTER.get(c, ()):
                        act.wait_ge(A["blk"], b + 1)
                        two = [2 * b, 2 * b + 1]
                        if two[0] in TURNED and two[1] in TURNED:
                            to = TURNED.index(two[0])
                            last = nc.scalar.activation(tb[:, to:to + 2, :], PT[b % 2][:, :].rearrange("p (k n) -> p k n", k=2), ACT.Copy)
                        else:
                            for k, block_ in enumerate(two):
                                bank = PT[b % 2][:, k * SEQ:(k + 1) * SEQ]
                                if block_ == T_IK:
                                    act.wait_ge(A["zero"], 3)
                                    for g in range(4):
                                        rows = slice(g * IDX_D, (g + 1) * IDX_D)
                                        nc.scalar.activation(ix_keys[rows, g, :], bank[rows, :], ACT.Copy)
                                    continue
                                if block_ in TURNED:
                                    last = nc.scalar.activation(tb[:, TURNED.index(block_), :], bank, ACT.Copy)
                                    continue
                                act.wait_ge(A["zero"], 2 if block_ in SHARED else 4 + block_ - T_CK)
                                for half in range(2):
                                    rows = slice(half * HD, (half + 1) * HD)
                                    last = nc.scalar.activation(keys_of(block_, half)[rows, :], bank[rows, :], ACT.Copy)
                        last.then_inc(A["blk_ev"], 1)
                        if b == 1:
                            act.wait_ge(A["rope_h"], 1)
                            for k, block_ in enumerate(DUP):
                                name, first, width_, copies = TB[block_]
                                nc.scalar.activation(dup[:, :, k, :].rearrange("p t (c n) -> p t c n", c=copies),
                                                     pj[:, :, COL[name]:COL[name] + width_].unsqueeze(2)
                                                     .to_broadcast([P, TT, copies, width_]), ACT.Copy).then_inc(A["dup"], 1)
                for h in range(IDX_H):
                    act.wait_ge(A["ix"], h + 1)
                    if h >= 2:
                        act.wait_ge(A["ix_acc"], h - 1)
                    nc.scalar.activation(relu[:, h % 2, :], S[h % 2][:, 0:CAUS], ACT.Relu,
                                         scale=IDX_D ** -0.5).then_inc(A["ix_relu"], 1)
                act.wait_ge(A["gate"], 1)
                nc.scalar.activation(ags, ags, ACT.Exp, scale=-1.0).then_inc(A["gate_e"], 1)
                def exponentials(u):
                    act.wait_ge(A["nm"], u + 1)
                    if u >= 2:
                        act.wait_ge(A["pt"], u - 1)
                    nc.scalar.activation(pr[:, u % 2, 0:P], lg[:, u % 2, 0:P], ACT.Exp, bias=nmax[:, u, 0:1],
                                         accum_out=den[:, u, 0:1])
                    nc.scalar.activation(pr[:, u % 2, P:CAUS], lg[:, u % 2, P:CAUS], ACT.Exp, bias=nmax[:, u, 1:2],
                                         accum_out=den[:, u, 1:2]).then_inc(A["e"], 1)

                def copy_weights(u):
                    act.wait_ge(A["pt"], u + 1)
                    if u >= 2:
                        act.wait_ge(A["o"], u - 1)
                    nc.scalar.activation(pt[:, u % 2, :], PT[u % 2][:, 0:CAUS], ACT.Copy).then_inc(A["pt_ev"], 1)

                def compressed(step):
                    if step == GELU_E_AT:
                        act.wait_ge(A["cg"], 1)
                        nc.scalar.activation(hb[:, 2, :], hb[:, 1, :], ACT.Exp, scale=-2.0 * (2.0 / np.pi) ** 0.5).then_inc(A["cg_e"], 1)
                    if step == CEXP_AT:
                        act.wait_ge(A["cnm"], 1)
                        nc.scalar.activation(lc[:, :, :, 0:NCMP], lc[:, :, :, 0:NCMP], ACT.Exp).then_inc(A["cexp"], 1)
                    if step == DIL_E_AT:
                        act.wait_ge(A["dila"], 1)
                        nc.scalar.activation(dexp, dexp, ACT.Exp).then_inc(A["dila_e"], 1)
                    if step == CPT_EV_AT:
                        act.wait_ge(A["cpt"], 1)
                        nc.scalar.activation(pcT, G[1][:, 0:SEQ].rearrange("p (t n) -> p t n", t=TT), ACT.Copy).then_inc(A["cpt_ev"], 1)
                        nc.scalar.activation(pcT4[0:32], G[1][0:32, SEQ:2 * SEQ].rearrange("p (t n) -> p t n", t=TT),
                                             ACT.Copy).then_inc(A["cpt_ev"], 1)

                for step in range(NU + LAG_T):
                    if step < NU:
                        exponentials(step)
                    if step >= LAG_T:
                        copy_weights(step - LAG_T)
                    compressed(step)
                hi_a(A_WIN)
                hi_a(A_WIN + 1)
                hi_features(A, 1, None)
                for c in range(A_WOUT):
                    hi_a(A_WIN + c + 2)
                load_table(ACT.Sqrt)
                act.wait_ge(A["x"], A_WOUT)
                root_mean_square(A, 0)
                hi_features(A, 2, "g2")
                silu_c(l + 1)
                ffn(A, split + (A_WIN + A_WOUT), l * (16 * A_N // RING) + 16 * (A_N0["ffn"] // RING), 0, True, 0)
                load_table(ACT.Sqrt)
                root_mean_square(NEXT, l + 1, A_WOUT + 1)
                act.drain().then_inc(layer_done, 1)
                act.wait_ge(layer_go, l + 1)

            def hi_mod(v, sub):
                def mod_(k):
                    act.wait_ge(B["tp"], v * KT + k + 1)
                    if k >= 4:
                        act.wait_ge(B["tp_lo"], v * KT + k - 3)
                    nc.scalar.activation(hx[:, k % 4, :], TP[k % len(TP)][:, 0:SEQ], ACT.Identity, scale=modc(sub, 1)[:, k:k + 1],
                                         bias=modc(sub, 0)[:, k:k + 1]).then_inc(modulated_tile(v, k)[0], 1)

                def hi_(k):
                    act.wait_ge(*modulated_tile(v, k))
                    nc.scalar.activation(hT_hi[:, k, :], hx[:, k % 4, :], ACT.Copy).then_inc(B["tp_hi"], 1)

                act.wait_ge(B["modl"], min(sub, 1) + 1)
                for k in range(0, KT, 2):
                    mod_(k)
                    if k:
                        hi_(k - 1)
                    hi_(k)
                hi_(KT - 1)

            def gate_copy(sub):
                for half in range(2):
                    act.wait_ge(B["gateb"], sub * 2 + half + 1)
                    nc.scalar.activation(gateb[:, half * 512:half * 512 + 512], GATE[half][:, :], ACT.Copy
                                         ).then_inc(B["gateb_ev"], 1)

            def root(sub):
                act.wait_ge(B["std"], 2 * sub + 1)
                nc.scalar.activation(st[:, 8:10], bag[:, :, 1], ACT.Sqrt, bias=LN_EPS).then_inc(B["std"], 1)

            act.wait_ge(FIN["x"], TT)
            with act.Fori(0, DEPTH) as l:
                split = l * B_N + S_A

                def hi_b(s):
                    hi(split + s, s % RING, s % RING, arrivals_b(l, s), b_width(s))

                act.dma_start(spa[:, 0:SB_W], t["sb"][bass.ds(l, 1), :, :].rearrange("o p n -> (o p) n")).then_inc(small_in, 16)
                hi_b(0)
                hi_mod(0, 0)
                hi_b(1)
                gate_copy(0)
                silu_c(l + (DEPTH + 1))
                ffn(B, split, l * (16 * B_N // RING) + 16 * N_A, 0, False, 2)
                root(0)
                hi_mod(1, 1)
                act.wait_ge(small_in, l * 16 + (DEPTH * 16 + 16))
                silus = []

                def prelude(c):
                    if c == 0:
                        nc.scalar.activation(row_g[0:GATES, :], G[0][0:GATES, 0:SEQ], ACT.Copy).then_inc(B["gcopy"], 1)
                    if c == 3:
                        act.wait_ge(B["gt"], 1)
                        nc.scalar.activation(ga, ga, ACT.Exp, scale=-1.0).then_inc(B["ge"], 1)
                        nc.scalar.activation(beta, sig, ACT.Exp, scale=-1.0).then_inc(B["ge"], 1)
                        nc.scalar.activation(ealog, sbp("a_log"), ACT.Exp).then_inc(B["ge"], 1)
                        act.wait_ge(B["ge"], 3)
                        nc.scalar.activation(gl1, ga, ACT.Ln, bias=1.0).then_inc(B["gln"], 1)
                    if c == 8:
                        act.wait_ge(B["rows"], 1)
                        act.wait_ge(B["zero"], 1)
                        nc.scalar.activation(grow[0:12, :], PT[0][0:12, 0:SEQ], ACT.Copy).then_inc(B["rows_ev"], 1)
                        nc.scalar.activation(row_b[0:6, :], PT[0][0:6, SEQ:2 * SEQ], ACT.Copy).then_inc(B["rows_ev"], 1)
                        nc.scalar.activation(row_f[0:6, :], PT[1][0:6, 0:SEQ], ACT.Copy).then_inc(B["rows_ev"], 1)
                        nc.scalar.activation(row_i[0:6, :], PT[1][0:6, SEQ:2 * SEQ], ACT.Copy).then_inc(B["rows_ev"], 1)
                        act.wait_ge(B["fm"], 3)
                        nc.scalar.activation(sq, fm[:, F_GQ:F_GQ + 6, :], ACT.Square).then_inc(B["sq"], 1)
                    if c == 10:
                        act.wait_ge(B["ss"], 1)
                        nc.scalar.activation(norm_r[0:12, :], O[0][0:12, 0:SEQ], ACT.Sqrt, bias=NORM_EPS).then_inc(B["ssr"], 1)
                    if c == 12:
                        act.wait_ge(B["bm"], 1)
                        nc.scalar.activation(em, S[1][:, 32:44].rearrange("p (t h) -> p t h", t=TT), ACT.Exp, scale=-1.0
                                             ).then_inc(B["em"], 1)

                    if c == 15:
                        act.wait_ge(B["zero"], 1)
                        act.wait_ge(B["fm"], N_FEAT)
                        act.wait_ge(B["rnb_ev"], 3)
                        for odd, first, n in ODD:
                            nc.scalar.activation(odd[ODD_ROWS], fm[ODD_ROWS, first:first + n, :], ACT.Copy).then_inc(B["odd"], 1)

                def silu(c):
                    ftiles = B_WIN[c][0]
                    act.wait_ge(B["conv"], c)
                    nc.scalar.activation(fm[:, ftiles[0]:ftiles[0] + len(ftiles), :], cvb[:, c % 2, 0:len(ftiles), :],
                                         ACT.Silu).then_inc(B["fm"], 1)

                for c, (ftiles, at, width) in enumerate(B_WIN):
                    s_ = B_S0["win"] + c
                    hi_b(s_ + 2)
                    if c == 0:
                        gate_copy(1)
                    if silus and c - silus[0] >= 1:
                        silu(silus.pop(0))
                    act.wait_ge(chunk_mm, split + (s_ + 1 + NEW))
                    bank = G[c % 2]
                    if ftiles and ftiles[0] in F_CONV:
                        for k, f in enumerate(ftiles):
                            if f in F_CONV:
                                nc.scalar.activation(cvb[:, c % 2, k, :], bank[:, k * SEQ:(k + 1) * SEQ], ACT.Copy,
                                                     scale=tap(f, 3)).then_inc(B["tap"], 1)
                        silus.append(c)
                    elif ftiles:
                        nc.scalar.activation(fm[:, ftiles[0]:ftiles[0] + 2, :], bank[:, :].rearrange("p (k n) -> p k n", k=2),
                                             ACT.Copy).then_inc(B["fm"], 1)
                    if width:
                        nc.scalar.activation(tm[:, :, at:at + width], bank[:, 0:TT * width].rearrange("p (t n) -> p t n", t=TT),
                                             ACT.Copy).then_inc(B["tm"], 1)
                    prelude(c)
                for c in silus:
                    silu(c)
                def exp_b(u):
                    kind, h = B_UNITS[u]
                    act.wait_ge(B["nm"], u + 1)
                    if u >= 2:
                        act.wait_ge(B["pt"], u - 1)
                    for i, cols in enumerate((slice(0, P), slice(P, CAUS))):
                        if kind == "moba":
                            last = nc.scalar.activation(prb[:, u % 2, cols], lgb[:, u % 2, cols], ACT.Exp, bias=nmaxb[:, u, i:i + 1],
                                                        accum_out=denb[:, u, i:i + 1])
                        else:
                            last = nc.scalar.activation(prb[:, u % 2, cols], lgb[:, u % 2, cols], ACT.Exp, bias=bm[:, i, h:h + 1])
                    last.then_inc(B["e"], 1)

                def copy_b(u):
                    act.wait_ge(B["pt"], u + 1)
                    if u >= 2:
                        act.wait_ge(B["o"], u - 1)
                    nc.scalar.activation(ptb[:, u % 2, :], PT[u % 2][:, 0:CAUS], ACT.Copy).then_inc(B["pt_ev"], 1)

                for step in range(NUB + B_LAGT):
                    if step < NUB:
                        exp_b(step)
                    if step >= B_LAGT:
                        copy_b(step - B_LAGT)
                act.wait_ge(B["tm"], N_TOK)
                nc.scalar.activation(tm[:, :, ZC:ZC + 384], tm[:, :, ZC:ZC + 384], ACT.Silu).then_inc(B["act"], 1)
                nc.scalar.activation(tm[:, :, OC:OC + 384], tm[:, :, OC:OC + 384], ACT.Sigmoid).then_inc(B["act"], 1)
                for h in range(GDN_H):
                    act.wait_ge(B["dl"], h + 1)
                    nc.scalar.activation(dec[h % 2][:, 0:SEQ], dec[h % 2][:, 0:SEQ], ACT.Exp, bias=negG[:, 0, h:h + 1])
                    nc.scalar.activation(dec[h % 2][:, SEQ:CAUS], dec[h % 2][:, SEQ:CAUS], ACT.Exp, bias=negG[:, 1, h:h + 1]
                                         ).then_inc(B["dec"], 1)
                for k in range(2 * GDN_H // 4):
                    act.wait_ge(B["xt"], k + 1)
                    nc.scalar.activation(xx[:, 4 * k:4 * k + 4, 0, :], ps[4 + k][:, :].rearrange("p (u n) -> p u n", u=4), ACT.Copy
                                         ).then_inc(B["xt_ev"], 1)
                for n in range((LEVELS - 1) * 2 * GDN_H):
                    if n == 30:
                        act.wait_ge(B["lvar"], 1)
                        nc.scalar.activation(hst3, hst3, ACT.Sqrt, scale=1.0 / HD, bias=NORM_EPS).then_inc(B["lrs"], 1)
                    act.wait_ge(B["y"], n + 1)
                    if n >= 4:
                        act.wait_ge(B["z"], n - 3)
                    nc.scalar.activation(ym[:, n % 4, :], ps[n % 4][:, 0:P], ACT.Copy).then_inc(B["y_ev"], 1)
                act.wait_ge(B["u"], 1)
                nc.scalar.activation(uu[:, 0, :], ps[0][:, 0:384], ACT.Copy).then_inc(B["u_ev"], 1)
                act.wait_ge(B["go"], 1)
                nc.scalar.activation(sq2[:, 0, :], ps[6][:, 0:384], ACT.Square).then_inc(B["gsq"], 1)
                act.wait_ge(B["u"], 3)
                nc.scalar.activation(uu[:, 1, :], ps[2][:, 0:384], ACT.Copy).then_inc(B["u_ev"], 1)
                act.wait_ge(B["go"], 2)
                nc.scalar.activation(sq2[:, 1, :], ps[7][:, 0:384], ACT.Square).then_inc(B["gsq"], 1)
                act.wait_ge(B["gms"], TT)
                nc.scalar.activation(hst, hst, ACT.Sqrt, scale=1.0 / HD, bias=NORM_EPS).then_inc(B["grs"], 1)
                hi_features(B, 2, None, LATE)
                for c in range(B_WOUT):
                    hi_b(B_S0["wout"] + c + 2)
                root(1)
                hi_mod(3, 2)
                gate_copy(2)
                ffn(B, split + B_S0["ffn1"], l * (16 * B_N // RING) + 16 * (N_A + B_S0["ffn1"] // RING), FT, False, 0)
                root(2)
                act.drain().then_inc(layer_done, 1)
                act.wait_ge(layer_go, l + (DEPTH + 1))

        @block.vector
        def _(dve):
            dve.sem_inc(lo_done, NEW)
            dve.wait_ge(x_in, 32)

            def modulation(w, half, column):
                w = w[:, half * DM:(half + 1) * DM]
                return nc.vector.scalar_tensor_tensor(out=w, in0=w, scalar=1.0, in1=cb, op0=ALU.mult, op1=ALU.mult,
                                                      accum_out=column)

            def lo(s, slot, raw_slot, width=CW):
                dve.wait_ge(hi_done, s + 1)
                nc.vector.tensor_tensor(w_lo[:, slot, 0:width], raw[:, raw_slot, 0:width],
                                        w_hi[:, slot, 0:width].bitcast(F32), ALU.subtract).then_inc(lo_done, 1)

            def normed(M, uses, N, v):
                dve.wait_ge(M["std"], uses + 1)
                nc.vector.reciprocal(st[:, 4:6], st[:, 2:4]).then_inc(N["rstd"], 1)
                dve.wait_ge(N["rstd"], v + 1)

            def rms_norm(M, uses, N, v):
                normed(M, uses, N, v)
                for i in range(TT):
                    nc.vector.tensor_scalar(xn[:, i, :], x[:, i, :], st[:, 4 + i:5 + i], None, ALU.mult).then_inc(N["xn"], 1)

            def lo_features(N, v, gain, order=range(KT)):
                for n, k in enumerate(order):
                    dve.wait_ge(N["tp_hi"], v * KT + n + 1)
                    nc.vector.scalar_tensor_tensor(out=hT_lo[:, k, :], in0=TP[n % len(TP)][:, 0:SEQ],
                                                   scalar=sa(gain, k) if gain else 1.0, in1=hT_hi[:, k, :].bitcast(F32),
                                                   op0=ALU.mult, op1=ALU.subtract).then_inc(N["tp_lo"], 1)

            def ffn(N, split, h0, more, conv=False, part=None):

                def post(f, f2, f4, ahead):
                    if conv:
                        dve.wait_ge(N["c1"], f + (h0 + 1))
                        nc.vector.scalar_tensor_tensor(out=cv[:, f2, 1:SEQ], in0=UP[f2][:, 0:SEQ - 1], scalar=conv_tap(f, 1),
                                                       in1=cv[:, f2, 1:SEQ], op0=ALU.mult, op1=ALU.add).then_inc(N["cv1"], 1)
                        dve.wait_ge(N["cv1"], f + (h0 + 1))
                        nc.vector.scalar_tensor_tensor(out=cv[:, f2, 2:SEQ], in0=UP[f2][:, 0:SEQ - 2], scalar=conv_tap(f, 0),
                                                       in1=cv[:, f2, 2:SEQ], op0=ALU.mult, op1=ALU.add).then_inc(N["cv2"], 1)
                    ahead()
                    dve.wait_ge(N["sg"], f + (h0 + 1))
                    nc.vector.tensor_tensor(h32[:, f2, :], sg[:, f2, :], UP[f2][:, SEQ:2 * SEQ], ALU.mult).then_inc(N["h"], 1)
                    dve.wait_ge(N["hid_hi"], f + (h0 + 1))
                    nc.vector.tensor_tensor(hid_lo[:, f4, :], h32[:, f2, :], hid_hi[:, f4, :].bitcast(F32),
                                            ALU.subtract).then_inc(N["hid_lo"], 1)

                def ada(j, k):
                    r, half = k // 2, k % 2
                    if half == 0:
                        dve.wait_ge(ada_in[r], part * (16 * ADA_T) + j * 16 + 16)
                    last = modulation(ada_raw[:, r, :], half, moda[:, bass.ds(j * (2 * RING) + k, 1)])
                    if half:
                        last.then_inc(ada_used, 1)

                def turn(j):
                    for q in range(6):
                        ahead = lambda: lo(j * 6 + (q + 3) + split, q % RING, q % RING)
                        if q % 3 == 2:
                            ahead()
                        else:
                            f4 = (1 + q - q // 3) % 4
                            post(j * 4 + (1 + q - q // 3), f4 % 2, f4, ahead)
                        if part is not None:
                            for k in ((), (0,), (1, 2), (), (3,), (4, 5))[q]:
                                ada(j + 1, k)

                lo(split + 1, 1, 1)
                if part is not None:
                    dve.wait_ge(c_silu, part + 1)
                    for k in range(2 * RING):
                        ada(0, k)
                post(0, 0, 0, lambda: lo(split + 2, 2, 2))
                with dve.Fori(0, (FT - 2) // 4) as j:
                    turn(j)
                post(FT - 1, 1, 1, (lambda: lo(split + FFN_N, 0, 0)) if more else (lambda: None))

            with dve.Fori(0, DEPTH) as l:
                split = l * A_S
                steps = 0

                def mark(ins):
                    nonlocal steps
                    steps += 1
                    ins.then_inc(A["dve"], 1)
                    return steps

                def link(ins):
                    dve.wait_ge(A["dve"], mark(ins))

                def lo_a(s):
                    n = s if s < A_WIN else s + A_D
                    lo(split + s, s % RING, n % RING, a_width(n))

                rms_norm(NEXT, l, A, 0)
                lo_a(0)
                dve.wait_ge(small_in, l * 16 + 16)
                lo_features(A, 0, "g1")
                for c in range(1, A_WIN):
                    lo_a(c)

                def rotate(first, heads, width, table, done):
                    r = CST["cos" + table][1] // TT
                    v = pj[:, :, first:first + heads * width].rearrange("p t (h d) -> p t h d", d=width)
                    x1, x2 = v[:, :, :, 0:r], v[:, :, :, r:2 * r]
                    cos, sin = (const(f + table).rearrange("p (t r) -> p t r", t=TT).unsqueeze(2)
                                .to_broadcast([P, TT, heads, r]) for f in ("cos", "sin"))
                    tmp = [b[:, 0:TT * heads * r].rearrange("p (t h r) -> p t h r", t=TT, h=heads) for b in rot]
                    for out, a, b in zip(tmp, (x1, x2, x2, x1), (cos, sin, cos, sin)):
                        last = nc.vector.tensor_tensor(out, a, b, ALU.mult)
                    link(last)
                    nc.vector.tensor_tensor(x1, tmp[0], tmp[1], ALU.subtract)
                    nc.vector.tensor_tensor(x2, tmp[2], tmp[3], ALU.add).then_inc(done, 1)
                    dve.wait_ge(done, 1)

                dve.wait_ge(start_in, 32)
                dve.wait_ge(A["pj"], PJ_TB)
                rotate(COL["iq"], ROT_I, IDX_D, "i", A["rope_i"])
                dve.wait_ge(A["blk"], 2)
                rotate(COL["aq"], ROT_H, HD, "h", A["rope_h"])
                dve.wait_ge(A["blk_ev"], T_KCVC // 2 + 1)
                dve.wait_ge(A["zero"], 1)
                kcvc = tb[:, T_KCVC, :].rearrange("p (m j) -> p m j", j=CSTR)
                for half in range(CBLK // CSTR):
                    js = slice(half * CSTR, (half + 1) * CSTR)
                    for kv in range(2):
                        rows, cols = slice(64 * kv, 64 * kv + 64), slice(kv * NCMP, (kv + 1) * NCMP)
                        last = nc.vector.tensor_tensor(rw[rows, js, cols], kcvc[rows, half:half + NCMP, :].rearrange("p m j -> p j m"),
                                                       sa("pos")[rows, js].unsqueeze(2).to_broadcast([64, CSTR, NCMP]), ALU.add)
                    last.then_inc(A["rw"], 1)
                dve.wait_ge(A["pj"], A_WIN)
                nc.vector.tensor_scalar(ags, pj[:, :, COL["ag"]:COL["ag"] + 15], -80.0, None, ALU.max).then_inc(A["gate"], 1)
                link(nc.vector.tensor_scalar(iws, pj[:, :, COL["iw"]:COL["iw"] + IDX_H], IDX_H ** -0.5, None, ALU.mult))
                for h in range(IDX_H):
                    dve.wait_ge(A["ix_relu"], h + 1)
                    if h:
                        dve.wait_ge(A["ix_acc"], h)
                    for i, cols in enumerate((slice(0, P), slice(P, CAUS))):
                        if h == 0:
                            last = nc.vector.tensor_scalar(isc[:, cols], relu[:, 0, cols], iws[:, i, 0:1], None, ALU.mult)
                        else:
                            last = nc.vector.scalar_tensor_tensor(out=isc[:, cols], in0=relu[:, h % 2, cols],
                                                                  scalar=iws[:, i, h:h + 1], in1=isc[:, cols],
                                                                  op0=ALU.mult, op1=ALU.add)
                    last.then_inc(A["ix_acc"], 1)
                dve.wait_ge(A["gate_e"], 1)
                link(nc.vector.tensor_scalar(ags, ags, 1.0, None, ALU.add))
                link(nc.vector.reciprocal(ags, ags))
                gates = ags.rearrange("p t (h g) -> p t h g", g=3)
                hv = [hb[:, k, :] for k in range(4)]
                per_head = lambda name: (const(name).rearrange("p (t n) -> p t n", t=TT).unsqueeze(2)
                                         .to_broadcast([P, TT, NSA_H, NCMP]))
                lcv = lc[:, :, :, 0:NCMP]

                def compressed(step):
                    if step == GELU_AT:
                        dve.wait_ge(direct_mm, l * A_D + A_CMP)
                        link(nc.vector.tensor_copy(hv[0], G[0][:, 0:2 * NCMP]))
                        link(nc.vector.tensor_tensor(hv[1], hv[0], hv[0], ALU.mult))
                        link(nc.vector.tensor_scalar(hv[1], hv[1], 0.044715, 1.0, ALU.mult, ALU.add))
                        link(nc.vector.tensor_tensor(hv[1], hv[1], hv[0], ALU.mult))
                        nc.vector.tensor_scalar(hv[1], hv[1], -50.0, None, ALU.max).then_inc(A["cg"], 1)
                    if step == GELU2_AT:
                        dve.wait_ge(A["cg_e"], 1)
                        link(nc.vector.tensor_scalar(hv[2], hv[2], 1.0, None, ALU.add))
                        link(nc.vector.reciprocal(hv[2], hv[2]))
                        link(nc.vector.tensor_tensor(hv[3], hv[0], hv[2], ALU.mult))
                        nc.vector.tensor_copy(vr[:, :, 0:NCMP], hb[:, 3, NCMP:2 * NCMP].unsqueeze(1).to_broadcast([P, 4, NCMP])
                                              ).then_inc(A["cgel"], 1)
                    if step == CKV_EV_AT:
                        dve.wait_ge(A["ckv"], 1)
                        nc.vector.tensor_tensor(kbd[:, :, 0:NCMP], G[1][:, 0:NCMP].unsqueeze(1).to_broadcast([P, 2, NCMP]),
                                                const("pair_of").unsqueeze(2).to_broadcast([P, 2, NCMP]), ALU.mult)
                        nc.vector.tensor_tensor(vbd, G[1][:, HD:2 * HD].unsqueeze(1).to_broadcast([P, 4, HD]),
                                                const("quad_of").unsqueeze(2).to_broadcast([P, 4, HD]), ALU.mult).then_inc(A["ckv_ev"], 1)
                    if step == CSM_AT:
                        dve.wait_ge(A["cs"], 1)
                        sc = G[0][:, 32:32 + TT * 6 * 16].rearrange("p (t h n) -> p t h n", t=TT, h=6)[:, :, 0:NSA_H, 0:NCMP]
                        for i in range(TT):
                            last = nc.vector.scalar_tensor_tensor(out=lcv[:, i], in0=sc[:, i], scalar=SCALE,
                                                                  in1=per_head("cmp_add")[:, i], op0=ALU.mult, op1=ALU.add)
                        link(last)
                        link(nc.vector.tensor_reduce(mc, lcv, AX.X, ALU.max))
                        nc.vector.tensor_tensor(lcv, lcv, mc.unsqueeze(3).to_broadcast([P, TT, NSA_H, NCMP]),
                                                ALU.subtract).then_inc(A["cnm"], 1)
                    if step == CP_AT:
                        dve.wait_ge(A["cexp"], 1)
                        nc.vector.tensor_tensor(pc[:, :, :, 0:NCMP], lcv, per_head("cmp_keep"), ALU.mult).then_inc(A["cp"], 1)
                        dve.wait_ge(A["cp"], 1)
                        link(nc.vector.tensor_reduce(dc, pc[:, :, :, 0:NCMP], AX.X, ALU.add))
                        link(nc.vector.tensor_scalar(dc, dc, 1e-30, None, ALU.max))
                        link(nc.vector.reciprocal(dc, dc))
                        link(nc.vector.tensor_tensor(dc, dc, gates[:, :, :, 0], ALU.mult))

                    if step == JOIN_AT:
                        dve.wait_ge(A["co"], 1)
                        dve.wait_ge(A["o_ev"], PLACE[DIL_H + 2 * NSA_H][0])
                        for h in range(NSA_H):
                            for i in range(TT):
                                out, at = mix[:, i, h * HD:(h + 1) * HD], (i * SEQ + h * HD if h < 4 else i * HD)
                                nc.vector.scalar_tensor_tensor(out=out, in0=G[h // 4][:, at:at + HD], scalar=dc[:, i, h:h + 1],
                                                               in1=out, op0=ALU.mult, op1=ALU.add)

                nm = nmax[:, 0:DIL_H, :].rearrange("p (g h) t -> p g (h t)", g=3)
                dn = den[:, 0:DIL_H, :].rearrange("p (g h) t -> p g (h t)", g=3)
                ex, fc = (v.rearrange("p (g h) t -> p g (h t)", g=3) for v in (dexp, dfac))
                low = dmin.rearrange("p h t -> p (h t)")
                spread = low.unsqueeze(1).to_broadcast([P, 3, 2 * TT])

                def dilations(step):
                    if step == DIL_AT:
                        link(nc.vector.tensor_tensor(low, nm[:, 0, :], nm[:, 1, :], ALU.min))
                        link(nc.vector.tensor_tensor(low, low, nm[:, 2, :], ALU.min))
                        nc.vector.tensor_tensor(ex, spread, nm, ALU.subtract).then_inc(A["dila"], 1)
                    if step == DIL_E_AT + 1:
                        dve.wait_ge(A["dila_e"], 1)
                        link(nc.vector.tensor_tensor(fc, ex, dn, ALU.mult))
                        link(nc.vector.tensor_tensor(low, fc[:, 0, :], fc[:, 1, :], ALU.add))
                        link(nc.vector.tensor_tensor(low, low, fc[:, 2, :], ALU.add))
                        link(nc.vector.reciprocal(low, low))
                        link(nc.vector.tensor_tensor(fc, ex, spread, ALU.mult))
                        dve.wait_ge(A["o_ev"], PLACE[DIL_H][0])
                        for i in range(TT):
                            o = mix[:, i, 640:DM].rearrange("p (h d) -> p h d", d=HD)
                            nc.vector.tensor_tensor(o, o, dfac[:, :, i].unsqueeze(2).to_broadcast([P, DIL_H, HD]), ALU.mult)

                TAKEN = -3e38

                def largest(part):
                    if part == 0:
                        link(nc.vector.tensor_tensor(isc, isc, const("causal"), ALU.add))
                    if 0 < part <= TOPK // 8:
                        dve.wait_ge(A["dve"], taken)
                    if 0 <= part < TOPK // 8:
                        nc.vector.max(m8[:, 0, :], isc[:, 0:P])
                        return mark(nc.vector.max(m8[:, 1, :], isc[:, P:CAUS]))

                def take(part, found):
                    if 0 <= part < TOPK // 8:
                        dve.wait_ge(A["dve"], found)
                        nc.vector.match_replace(isc[:, 0:P], m8[:, 0, :], isc[:, 0:P], TAKEN)
                        return mark(nc.vector.match_replace(isc[:, P:CAUS], m8[:, 1, :], isc[:, P:CAUS], TAKEN))
                    if part == TOPK // 8:
                        link(nc.vector.tensor_scalar(dmask, isc, 0.5 * TAKEN, NEG, ALU.is_gt, ALU.mult))
                        link(nc.vector.tensor_tensor(dmask, dmask, const("causal"), ALU.add))

                def logits(u):
                    dve.wait_ge(A["s"], u + 1)
                    if u >= 2:
                        dve.wait_ge(A["e"], u - 1)
                    return mark(nc.vector.scalar_tensor_tensor(out=lg[:, u % 2, :], in0=S[u % 2][:, 0:CAUS], scalar=SCALE,
                                                               in1=unit(u)[4], op0=ALU.mult, op1=ALU.add))

                def maxima(u, there):
                    dve.wait_ge(A["dve"], there)
                    nc.vector.tensor_reduce(nmax[:, u, 0:1], lg[:, u % 2, 0:P], AX.X, ALU.max, negate=True)
                    nc.vector.tensor_reduce(nmax[:, u, 1:2], lg[:, u % 2, P:CAUS], AX.X, ALU.max, negate=True).then_inc(A["nm"], 1)

                def denominators(g):
                    first, n = GROUPS[g]
                    dve.wait_ge(A["o"], first + n)
                    if UNITS[first][0] != "dil":
                        return mark(nc.vector.reciprocal(rden[:, g % 2, 0:n, :], den[:, first:first + n, :]))

                def factors(g, there):
                    first, n = GROUPS[g]
                    kind, h = UNITS[first]
                    if kind not in ("slc", "win"):
                        return there
                    dve.wait_ge(A["dve"], there)
                    gate = gates[:, :, h:h + n, 1 if kind == "slc" else 2].rearrange("p t h -> p h t")
                    return mark(nc.vector.tensor_tensor(fac[:, g % 2, 0:n, :], rden[:, g % 2, 0:n, :], gate, ALU.mult))

                def outputs(g, there):
                    first, n = GROUPS[g]
                    kind, at = UNITS[first][0], unit(first)[5]
                    split_heads = lambda v: v.rearrange("p (h t d) -> p h t d", t=TT, d=HD)
                    out = mix[:, :, at:at + n * HD].rearrange("p t (h d) -> p h t d", d=HD)
                    o = split_heads(O[g % 2][:, 0:n * OUT_W])
                    if kind == "dil":
                        nc.vector.tensor_copy(out, o).then_inc(A["o_ev"], 1)
                        return
                    dve.wait_ge(A["dve"], there)
                    f = (rden if kind == "dsa" else fac)[:, g % 2, 0:n, :].unsqueeze(3).to_broadcast([P, n, TT, HD])
                    if kind == "win":
                        branch = split_heads(relu[:, 0, 0:n * OUT_W])
                        link(nc.vector.tensor_tensor(branch, o, f, ALU.mult))
                        dve.wait_ge(A["o_ev"], g)
                        last = nc.vector.tensor_tensor(out, out, branch, ALU.add)
                    else:
                        last = nc.vector.tensor_tensor(out, o, f, ALU.mult)
                    last.then_inc(A["o_ev"], 1)

                for step in range(NU + LAG_V):
                    u, eight = step - LAG_V, step - SELECT_AT
                    through = u >= 0 and PLACE[u][1] == GROUPS[PLACE[u][0]][1] - 1
                    if step < NU:
                        there = logits(step)
                    if through:
                        inverse = denominators(PLACE[u][0])
                    if step < NU:
                        maxima(step, there)
                    if through:
                        factor = factors(PLACE[u][0], inverse)
                    found = largest(eight)
                    if through:
                        outputs(PLACE[u][0], factor)
                    taken = take(eight, found)
                    compressed(step)
                    dilations(step)
                lo_a(A_WIN)
                lo_features(A, 1, None)
                for c in range(A_WOUT):
                    lo_a(A_WIN + c + 1)
                    dve.wait_ge(chunk_mm, split + (A_WIN + c + 1 + NEW))
                    cols = slice(c * GW, (c + 1) * GW)
                    nc.vector.tensor_tensor(x[:, :, cols], x[:, :, cols], G[c % 2][:, :].rearrange("p (t n) -> p t n", t=TT),
                                            ALU.add).then_inc(A["x"], 1)
                rms_norm(A, 0, A, 1)
                lo_features(A, 2, "g2")
                ffn(A, split + (A_WIN + A_WOUT), 0, 0, conv=True, part=l)
                dve.wait_ge(ada_used, l * ADA_N + ADA_N)
                nc.vector.tensor_tensor(mod[:, bass.ds(l, 1), :].rearrange("p o n -> p (o n)"), moda[:, :], sa("ada_b"), ALU.add)
                for i in range(TT):
                    if i == 0:
                        dve.wait_ge(A["y0"], 1)
                    else:
                        dve.wait_ge(chunk_mm, split + (A_S + NEW))
                    for half in range(2):
                        cols = slice(half * 512, half * 512 + 512)
                        last = nc.vector.tensor_tensor(x[:, i, cols], x[:, i, cols], ACC[2 * i + half][:, :], ALU.add)
                    last.then_inc(A["x"], 1)
                dve.drain().then_inc(layer_done, 1)
                dve.wait_ge(layer_go, l + 1)
            normed(NEXT, DEPTH, FIN, 0)
            for i in range(TT):
                nc.vector.scalar_tensor_tensor(out=x[:, i, :], in0=x[:, i, :], scalar=st[:, 4 + i:5 + i], in1=lnw[:, 0, :],
                                               op0=ALU.mult, op1=ALU.mult).then_inc(FIN["x"], 1)

            def gate_diagonal(sub):
                nc.vector.tensor_tensor(gdiag, ident.unsqueeze(1).to_broadcast([P, KT, P]),
                                        modc(sub, 2).unsqueeze(2).to_broadcast([P, KT, P]), ALU.mult).then_inc(B["gdiag"], 1)

            def lo_mod(v, sub):
                def mod_(k):
                    dve.wait_ge(B["tp"], v * KT + k + 1)
                    if k >= 4:
                        dve.wait_ge(B["tp_lo"], v * KT + k - 3)
                    nc.vector.tensor_scalar(hx[:, k % 4, :], TP[k % len(TP)][:, 0:SEQ], modc(sub, 1)[:, k:k + 1],
                                            modc(sub, 0)[:, k:k + 1], ALU.mult, ALU.add).then_inc(modulated_tile(v, k)[0], 1)

                def lo_(k):
                    dve.wait_ge(B["tp_hi"], v * KT + k + 1)
                    nc.vector.tensor_tensor(hT_lo[:, k, :], hx[:, k % 4, :], hT_hi[:, k, :].bitcast(F32),
                                            ALU.subtract).then_inc(B["tp_lo"], 1)

                dve.wait_ge(B["modl"], min(sub, 1) + 1)
                for k in range(0, KT, 2):
                    mod_(k + 1)
                    if k:
                        lo_(k - 1)
                    lo_(k)
                lo_(KT - 1)

            dve.wait_ge(FIN["x"], TT)
            with dve.Fori(0, DEPTH) as l:
                split = l * B_N + S_A
                steps = 0

                def mark(ins):
                    nonlocal steps
                    steps += 1
                    ins.then_inc(B["dve"], 1)
                    return steps

                def link(ins):
                    nonlocal steps
                    steps += 1
                    ins.then_inc(B["dve"], 1)
                    dve.wait_ge(B["dve"], steps)

                def lo_b(s):
                    lo(split + s, s % RING, s % RING, b_width(s))

                def residual(pieces):
                    done = []
                    for k, (i, half, ys) in enumerate(pieces):
                        for xc, y in ys:
                            at = xc.start - half * 512
                            last = nc.vector.tensor_tensor(part[:, k, at:at + xc.stop - xc.start], y, gateb[:, xc], ALU.mult)
                        done.append(mark(last))
                    for k, (i, half, _) in enumerate(pieces):
                        cols = slice(half * 512, half * 512 + 512)
                        dve.wait_ge(B["dve"], done[k])
                        done.append(mark(nc.vector.scalar_tensor_tensor(out=x[:, i, cols], in0=x[:, i, cols], scalar=ALPHA,
                                                                        in1=part[:, k, :], op0=ALU.mult, op1=ALU.add)))
                    for k, (i, half, _) in enumerate(pieces):
                        dve.wait_ge(B["dve"], done[2 + k])
                        last = nc.vector.bn_stats(bst[:, i, half, :], x[:, i, half * 512:half * 512 + 512])
                    link(last)

                def from_down(i):
                    return [(i, half, [(slice(half * 512, half * 512 + 512), ACC[2 * i + half][:, :])]) for half in range(2)]

                def from_wout(half):
                    cols = lambda c: slice(half * 512 + c * GW, half * 512 + (c + 1) * GW)
                    return [(i, half, [(cols(c), ACC[2 * half + c][:, i * GW:(i + 1) * GW]) for c in range(2)]) for i in range(TT)]

                def residual_down(sub, done):
                    if sub:
                        dve.wait_ge(B["xg"], 2 * sub)
                    dve.wait_ge(B["y0"], sub // 2 + 1)
                    residual(from_down(0))
                    dve.wait_ge(chunk_mm, done)
                    residual(from_down(1))

                def layer_norm(sub):
                    for i in range(TT):
                        last = nc.vector.bn_aggr(bag[:, i, :], bst[:, i, :, :].rearrange("p a b -> p (a b)"))
                    last.then_inc(B["std"], 1)
                    dve.wait_ge(B["std"], 2 * sub + 2)
                    link(nc.vector.reciprocal(st[:, 10:12], st[:, 8:10]))
                    for i in range(TT):
                        nc.vector.tensor_scalar(x[:, i, :], x[:, i, :], bag[:, i, 0:1], st[:, 10 + i:11 + i],
                                                ALU.subtract, ALU.mult).then_inc(B["nx"], 1)

                def last_layer_norm(sub):
                    for i in range(TT):
                        last = nc.vector.bn_aggr(bag[:, i, :], bst[:, i, :, :].rearrange("p a b -> p (a b)"))
                    last.then_inc(B["std"], 1)
                    dve.wait_ge(B["std"], 2 * sub + 1)
                    dve.wait_ge(ln_in, l * 96 + 32 * (sub + 1))
                    done = [mark(nc.vector.scalar_tensor_tensor(out=x[:, i, :], in0=x[:, i, :], scalar=bag[:, i, 0:1],
                                                                in1=lnw[:, 0, :], op0=ALU.subtract, op1=ALU.mult)) for i in range(TT)]
                    dve.wait_ge(B["std"], 2 * sub + 2)
                    link(nc.vector.reciprocal(st[:, 10:12], st[:, 8:10]))
                    for i in range(TT):
                        dve.wait_ge(B["dve"], done[i])
                        nc.vector.scalar_tensor_tensor(out=x[:, i, :], in0=x[:, i, :], scalar=st[:, 10 + i:11 + i],
                                                       in1=lnw[:, 1, :], op0=ALU.mult, op1=ALU.add).then_inc(FIN["x"], 1)

                link(nc.vector.tensor_copy(modl[:, 0:MOD2], mod[:, bass.ds(l, 1), :].rearrange("p o n -> p (o n)")))
                by_kind = modl[:, :].rearrange("p (s w n) -> p s w n", s=3, w=3)
                link(nc.vector.tensor_scalar(by_kind[:, 0, 1:3, :], by_kind[:, 0, 1:3, :], 1.0, None, ALU.add))
                nc.vector.tensor_scalar(modc(0, 2), modc(0, 2), 0.5, None, ALU.mult).then_inc(B["modl"], 1)
                dve.wait_ge(B["modl"], 1)
                gate_diagonal(0)
                lo_b(0)
                lo_mod(0, 0)
                ffn(B, split, 0, 2, part=l + DEPTH)
                dve.wait_ge(small_in, l * 16 + (DEPTH * 16 + 16))
                dve.wait_ge(ada_used, (l + DEPTH) * ADA_N + ADA_N)
                link(nc.vector.tensor_tensor(modl[:, MOD2:MOD], moda[:, :], sbp("ada_b"), ALU.add))
                link(nc.vector.tensor_scalar(by_kind[:, 1:3, 1:3, :], by_kind[:, 1:3, 1:3, :], 1.0, None, ALU.add))
                link(nc.vector.tensor_scalar(modc(2, 2), modc(2, 2), 0.5, None, ALU.mult))
                scales = by_kind[:, 1:3, 1, :]
                link(nc.vector.tensor_tensor(bshift, sbp("ln_b").rearrange("p (s n) -> p s n", s=2), scales, ALU.mult))
                nc.vector.tensor_tensor(by_kind[:, 1:3, 0, :], by_kind[:, 1:3, 0, :], bshift, ALU.add)
                nc.vector.tensor_tensor(scales, scales, sbp("ln_g").rearrange("p (s n) -> p s n", s=2), ALU.mult
                                        ).then_inc(B["modl"], 1)
                gate_diagonal(1)
                residual_down(0, split + (FFN_N + NEW))
                layer_norm(0)
                lo_mod(1, 1)

                def prelude(c):
                    if c == 2:
                        dve.wait_ge(B["gtok"], 1)
                        link(nc.vector.tensor_tensor(gt, S[0][:, 0:TT * GATES].rearrange("p (t n) -> p t n", t=TT),
                                                     sbp("gate_bias").unsqueeze(1).to_broadcast([P, TT, GATES]), ALU.add))
                        nc.vector.tensor_scalar(sig, gt[:, :, 12:18], -80.0, None, ALU.max)
                        nc.vector.scalar_tensor_tensor(out=ga, in0=gt[:, :, 0:12], scalar=-1.0, in1=gt[:, :, 0:12], op0=ALU.mult,
                                                       op1=ALU.max).then_inc(B["gt"], 1)
                    if c == 4:
                        dve.wait_ge(B["gln"], 1)
                        link(nc.vector.scalar_tensor_tensor(out=gl[:, :, 0:6], in0=gt[:, :, 0:6], scalar=0.0, in1=gl1[:, :, 0:6],
                                                            op0=ALU.max, op1=ALU.add))
                        link(nc.vector.scalar_tensor_tensor(out=gl[:, :, 0:6], in0=gl[:, :, 0:6], scalar=-1.0,
                                                            in1=ealog.unsqueeze(1).to_broadcast([P, TT, 6]), op0=ALU.mult, op1=ALU.mult))
                        nc.vector.scalar_tensor_tensor(out=gl[:, :, 6:12], in0=gt[:, :, 6:12], scalar=0.0, in1=gl1[:, :, 6:12],
                                                       op0=ALU.min, op1=ALU.subtract).then_inc(B["gl"], 1)
                        link(nc.vector.tensor_scalar(beta, beta, 1.0, None, ALU.add))
                        link(nc.vector.reciprocal(beta, beta))
                    if c == 6:
                        dve.wait_ge(B["cum"], 1)
                        link(nc.vector.tensor_copy(cg, S[1][:, 0:24].rearrange("p (t n) -> p t n", t=TT)))
                        nc.vector.tensor_copy(ngr[:, :, 0:6], cg[:, :, 0:6])
                        nc.vector.tensor_scalar(negG, cg[:, :, 0:6], -1.0, None, ALU.mult)
                        nc.vector.tensor_tensor(ngr[:, :, 6:12], gt[:, :, 18:24], cg[:, :, 6:12], ALU.subtract).then_inc(B["cg"], 1)
                    if c == 9:
                        dve.wait_ge(B["rows_ev"], 4)
                        nc.vector.tensor_tensor_scan(row_m[0:6, :], row_f[0:6, :], row_i[0:6, :], 0.0, ALU.add, ALU.max
                                                     ).then_inc(B["scan"], 1)
                    if c == 11:
                        dve.wait_ge(B["ssr"], 1)
                        nc.vector.reciprocal(norm_r[0:12, :], norm_r[0:12, :]).then_inc(B["rn"], 1)
                        dve.wait_ge(B["mback"], 1)
                        nc.vector.tensor_tensor(bm, cg[:, :, 6:12], S[1][:, 32:44].rearrange("p (t h) -> p t h", t=TT),
                                                ALU.subtract).then_inc(B["bm"], 1)
                    if c == 13:
                        for f in range(3):
                            dve.wait_ge(B["rnb"], f + 1)
                            qk = fm[:, 2 * f:2 * f + 2, :]
                            nc.vector.tensor_tensor(qk, qk, RN[f][:, :].rearrange("p (k n) -> p k n", k=2), ALU.mult
                                                    ).then_inc(B["rnb_ev"], 1)
                    if c == 14:
                        dve.wait_ge(B["rnb_ev"], 3)
                        dve.wait_ge(B["bb"], 1)
                        for f in range(3):
                            nc.vector.tensor_tensor(kbT[:, f, :], fm[:, F_GK + f, :], PT[f // 2][:, f % 2 * SEQ:(f % 2 + 1) * SEQ],
                                                    ALU.mult).then_inc(B["kb"], 1)
                    if c == 16:
                        for i in range(TT):
                            dve.wait_ge(B["vt"], i + 1)
                            nc.vector.tensor_tensor(vb[:, i, :, :], RN[i][:, 0:384].rearrange("p (h d) -> p h d", d=HD),
                                                    beta[:, i, :].unsqueeze(2).to_broadcast([P, GDN_H, HD]), ALU.mult).then_inc(B["vb"], 1)

                ntap = 0
                for c, (ftiles, _, _) in enumerate(B_WIN):
                    lo_b(B_S0["win"] + c + 1)
                    if ftiles and ftiles[0] in F_CONV:
                        ntap += len(ftiles)
                        dve.wait_ge(B["tap"], ntap)
                        for d in range(1, TAPS):
                            for k, f in enumerate(ftiles):
                                last = nc.vector.scalar_tensor_tensor(
                                    out=cvb[:, c % 2, k, d:SEQ], in0=G[c % 2][:, k * SEQ:(k + 1) * SEQ - d], scalar=tap(f, TAPS - 1 - d),
                                    in1=cvb[:, c % 2, k, d:SEQ], op0=ALU.mult, op1=ALU.add)
                            if d < TAPS - 1:
                                link(last)
                        last.then_inc(B["conv"], 1)
                    prelude(c)

                def logits_b(u):
                    kind, h = B_UNITS[u]
                    dve.wait_ge(B["s"], u + 1)
                    if u >= 2:
                        dve.wait_ge(B["e"], u - 1)
                    if kind == "moba":
                        ins = nc.vector.scalar_tensor_tensor(out=lgb[:, u % 2, :], in0=S[u % 2][:, 0:CAUS], scalar=SCALE,
                                                             in1=const("causal"), op0=ALU.mult, op1=ALU.add)
                        ins.then_inc(B["s_free"], 1)
                        dve.wait_ge(B["s_free"], u + 1)
                        nc.vector.tensor_reduce(nmaxb[:, u, 0:1], lgb[:, u % 2, 0:P], AX.X, ALU.max, negate=True)
                        nc.vector.tensor_reduce(nmaxb[:, u, 1:2], lgb[:, u % 2, P:CAUS], AX.X, ALU.max, negate=True).then_inc(B["nm"], 1)
                    else:
                        nc.vector.tensor_tensor(lgb[:, u % 2, 0:P], G[u % 2][:, 0:P], const("causal")[:, 0:P], ALU.add)
                        nc.vector.tensor_tensor(lgb[:, u % 2, P:CAUS], G[u % 2][:, 0:SEQ], const("causal")[:, P:CAUS],
                                                ALU.add).then_inc(B["nm"], 1)

                def weigh(u):
                    if not 0 <= u < NUB or B_UNITS[u][0] != "mlstm":
                        return
                    dve.wait_ge(B["e"], u + 1)
                    for i, cols in enumerate((slice(0, P), slice(P, CAUS))):
                        last = nc.vector.scalar_tensor_tensor(out=prb[:, u % 2, cols], in0=S[u % 2][:, cols], scalar=SCALE,
                                                              in1=prb[:, u % 2, cols], op0=ALU.mult, op1=ALU.mult,
                                                              accum_out=denb[:, u, i:i + 1])
                    last.then_inc(B["p"], 1)

                def outputs_b(u):
                    kind, h = B_UNITS[u]
                    dve.wait_ge(B["o"], u + 1)
                    o = O[u % 2][:, 0:TT * HD].rearrange("p (t d) -> p t d", t=TT)
                    if kind == "moba":
                        link(nc.vector.reciprocal(rdenb[:, u % 2, :], denb[:, u, :]))
                        nc.vector.tensor_tensor(mixb[:, :, 384 + h * HD:384 + (h + 1) * HD], o,
                                                rdenb[:, u % 2, :].unsqueeze(2).to_broadcast([P, TT, HD]), ALU.mult).then_inc(B["o_ev"], 1)
                    else:
                        nc.vector.tensor_copy(mixb[:, :, 640 + h * HD:640 + (h + 1) * HD], o).then_inc(B["o_ev"], 1)

                dve.wait_ge(B["rows_ev"], 4)
                for step in range(NUB + B_LAGV):
                    weigh(step - B_LAGP)
                    if step < NUB:
                        logits_b(step)
                    if step >= B_LAGV:
                        outputs_b(step - B_LAGV)

                def log_decays(h):
                    dve.wait_ge(B["ds"], h + 1)
                    nc.vector.tensor_tensor(dec[h % 2][:, 0:SEQ], G[h % 2][:, 0:SEQ], const("causalT")[:, 0:SEQ], ALU.add)
                    nc.vector.tensor_tensor(dec[h % 2][:, SEQ:CAUS], G[h % 2][:, P:SEQ], const("causalT")[:, SEQ:CAUS],
                                            ALU.add).then_inc(B["dl"], 1)

                log_decays(0)
                for h in range(GDN_H):
                    if h + 1 < GDN_H:
                        log_decays(h + 1)
                    dve.wait_ge(B["dec"], h + 1)
                    nc.vector.scalar_tensor_tensor(out=attnT[:, h, :], in0=S[h % 2][:, 0:CAUS], scalar=SCALE, in1=dec[h % 2],
                                                   op0=ALU.mult, op1=ALU.mult)
                    nc.vector.tensor_tensor(sysT[:, h, :], PT[h % 2][:, 0:CAUS], dec[h % 2], ALU.mult).then_inc(B["dmul"], 1)
                    dve.wait_ge(B["dmul"], h + 1)
                    v = xx[:, 2 * h:2 * h + 2, 1, :]
                    link(nc.vector.tensor_tensor(v, sysT[:, h, :].rearrange("p (k n) -> p k n", n=P)[:, 0:3:2, :],
                                                 const("lev0").unsqueeze(1).to_broadcast([P, 2, P]), ALU.mult))
                    nc.vector.tensor_tensor(v, ident.unsqueeze(1).to_broadcast([P, 2, P]), v, ALU.subtract).then_inc(B["xinit"], 1)
                dve.wait_ge(B["xinit"], GDN_H)
                NZ = (LEVELS - 1) * 2 * GDN_H
                heads = lambda v: v.rearrange("p t (h d) -> p t h d", d=HD)
                wide = lambda v: v.unsqueeze(3).to_broadcast([P, TT, 6, HD])
                hc = heads(mixb[:, :, 640:DM])
                dn = denb[:, MOBA_H:NUB, :].rearrange("p h t -> p t h")

                def mlstm_norm(n):
                    if n == 4:
                        link(nc.vector.scalar_tensor_tensor(out=hst2, in0=dn, scalar=-1.0, in1=dn, op0=ALU.mult, op1=ALU.max))
                        link(nc.vector.tensor_tensor(hst2, hst2, em, ALU.max))
                        link(nc.vector.reciprocal(hst2, hst2))
                        link(nc.vector.tensor_tensor(hc, hc, wide(hst2), ALU.mult))
                    if n == 8:
                        dve.wait_ge(B["act"], 2)
                        link(nc.vector.tensor_tensor(hc, hc, heads(tm[:, :, OC:OC + 384]), ALU.mult))
                    if n == 12:
                        link(nc.vector.tensor_reduce(hst2, hc, AX.X, ALU.add))
                        link(nc.vector.tensor_scalar(hst2, hst2, 1.0 / HD, None, ALU.mult))
                    if n == 16:
                        link(nc.vector.tensor_tensor(hc, hc, wide(hst2), ALU.subtract))
                    if n == 20:
                        link(nc.vector.tensor_tensor(heads(uu), hc, hc, ALU.mult))
                    if n == 24:
                        nc.vector.tensor_reduce(hst3, heads(uu), AX.X, ALU.add).then_inc(B["lvar"], 1)
                    if n == 32:
                        dve.wait_ge(B["lrs"], 1)
                        link(nc.vector.reciprocal(hst3, hst3))
                        link(nc.vector.tensor_tensor(hc, hc, wide(hst3), ALU.mult))
                    if n == 40:
                        dve.wait_ge(B["act"], 2)
                        z = heads(tm[:, :, ZC:ZC + 384])
                        link(nc.vector.tensor_tensor(z, z, sbp("gdn_norm").unsqueeze(1).unsqueeze(1).to_broadcast([P, TT, 6, HD]),
                                                     ALU.mult))
                    if n == 36:
                        nc.vector.tensor_tensor(mixb[:, :, 640:DM], mixb[:, :, 640:DM],
                                                sbp("ml_norm").unsqueeze(1).to_broadcast([P, TT, 384]), ALU.mult).then_inc(B["mix"], 1)

                for n in range(NZ):
                    mlstm_norm(n)
                    dve.wait_ge(B["z"], n + 1)
                    first = 0 if n < NZ - 2 * GDN_H else 1
                    v = xx[:, n % (2 * GDN_H), first:, :]
                    nc.vector.tensor_tensor(v, v, ps[4 + n % 4][:, first * P:SEQ].rearrange("p (k n) -> p k n", n=P),
                                            ALU.subtract).then_inc(B["xx"], 1)
                dve.wait_ge(B["u"], 2)
                vb1 = vb[:, 1, :, :].rearrange("p h d -> p (h d)")
                nc.vector.tensor_tensor(vb1, vb1, ps[1][:, 0:384], ALU.subtract).then_inc(B["w1"], 1)

                oa = heads(mixb[:, :, 0:384])
                for i in range(TT):
                    dve.wait_ge(B["gsq"], i + 1)
                    nc.vector.tensor_reduce(hst[:, i, :], heads(sq2)[:, i], AX.X, ALU.add).then_inc(B["gms"], 1)
                    gated = mark(nc.vector.tensor_tensor(mixb[:, i, 0:384], ps[6 + i][:, 0:384], tm[:, i, ZC:ZC + 384], ALU.mult))
                dve.wait_ge(B["grs"], 1)
                link(nc.vector.reciprocal(hst, hst))
                dve.wait_ge(B["dve"], gated)
                nc.vector.tensor_tensor(oa, oa, wide(hst), ALU.mult).then_inc(B["mix"], 1)
                lo_features(B, 2, None, LATE)
                gate_diagonal(2)
                for c in range(B_WOUT):
                    lo_b(B_S0["wout"] + c + 1)
                    if c >= 2:
                        dve.wait_ge(B["xg"], 2)
                        dve.wait_ge(chunk_mm, split + (B_S0["wout"] + 2 * (c - 1) + NEW))
                        residual(from_wout(c - 2))
                layer_norm(1)
                lo_mod(3, 2)
                ffn(B, split + B_S0["ffn1"], FT, 0)
                residual_down(2, split + (B_N + NEW))
                last_layer_norm(2)
                dve.drain().then_inc(layer_done, 1)
                dve.wait_ge(layer_go, l + (DEPTH + 1))
    return nc


def pack_first(inputs):
    f = lambda n: np.asarray(inputs[n], np.float32)
    wa = np.zeros((DEPTH, A_N, P, CW), np.float32)
    w_in, w1, w_out, w_up, w_down = f("w_in"), f("cmp_w1"), f("w_out"), f("w_up"), f("w_down")
    tiles = lambda a: a.reshape(KT, P, -1).transpose(1, 0, 2)
    order = np.concatenate([np.arange(SRC[n][0], SRC[n][0] + SRC[n][1]) for n in COL])
    for l in range(DEPTH):
        w = np.zeros((DM, PJW), np.float32)
        w[:, :D_IN] = w_in[l][:, order]
        for c, width in enumerate(WIN_A):
            wa[l, c, :, :KT * width] = tiles(w[:, c * GW:c * GW + width]).reshape(P, -1)
        cmp1 = w1[l].reshape(2, CBLK, HD, P).transpose(0, 2, 1, 3).reshape(P, CBLK * P)
        at = 0
        for n in range(A_N0["cmp"], A_N0["wout"]):
            wa[l, n, :, :a_width(n)] = cmp1[:, at:at + a_width(n)]
            at += a_width(n)
        for c in range(A_WOUT):
            wa[l, A_N0["wout"] + c] = tiles(w_out[l][:, c * GW:(c + 1) * GW]).reshape(P, CW)
        wa[l, A_N0["ffn"]:] = pack_ffn(w_up[l], w_down[l])
    sa = np.zeros((DEPTH, P, SA_W), np.float32)
    col = lambda v: v.reshape(-1, P).T
    for l in range(DEPTH):
        def put(name, a):
            at, w = SA[name]
            sa[l, :, at:at + w] = a.reshape(P, w)
        put("g1", col(f("norm1_g")[l]))
        put("g2", col(f("norm2_g")[l]))
        taps = np.concatenate([f("conv_w")[l], f("conv_b")[l][None]], 0)
        put("conv", taps.reshape(4, FT, P).transpose(2, 1, 0))
        put("pos", f("cmp_pos")[l].transpose(0, 2, 1).reshape(P, CBLK))
        w2 = f("cmp_w2")[l]
        put("w2k", np.concatenate([w2[0], w2[0]], 1))
        put("w2v", w2[1])
        put("ada_b", col(f("ada_b_2")[l])[:, :MOD2])
    wm = f("ada_w_2").reshape(DEPTH, DM, 2 * ADA_N, 2, P).transpose(0, 2, 4, 3, 1).reshape(DEPTH, 2 * ADA_N, P, CW)
    return {"wa": wa, "sa": sa, "wm": wm, "const": CONST, "x": f("x"), "c": f("c_2")[0],
            "final_g": f("final_g")}


def pack_second(inputs):
    f = lambda n: np.asarray(inputs[n + "_2"], np.float32)
    w13, w2, w_in, w_out = f("ffn_w13"), f("ffn_w2"), f("w_in"), f("w_out")
    tiles = lambda a: a.reshape(KT, P, -1).transpose(1, 0, 2)
    r = np.arange
    feat = np.concatenate([r(0, 1152), r(2316, 3084), r(1548, 2060)])
    tok = np.concatenate([r(1164, 1548), r(2060, 2316), r(3084, 3468), r(3480, 3864)])
    gates = np.concatenate([r(1152, 1158), r(3474, 3480), r(1158, 1164), r(3468, 3474)])
    wb = np.zeros((DEPTH, B_N, P, CW), np.float32)
    sb = np.zeros((DEPTH, P, SB_W), np.float32)
    for l in range(DEPTH):
        wb[l, :FFN_N] = pack_ffn(w13[l, 0], w2[l, 0])
        wb[l, B_S0["ffn1"]:] = pack_ffn(w13[l, 1], w2[l, 1])
        for c, (ftiles, at, width) in enumerate(B_WIN):
            cols = np.concatenate([feat[P * k:P * (k + 1)] for k in ftiles] + [tok[at:at + width]]).astype(int) if c else gates
            wb[l, B_S0["win"] + c, :, :KT * len(cols)] = tiles(w_in[l][:, cols]).reshape(P, -1)
        for c in range(B_WOUT):
            wb[l, B_S0["wout"] + c] = tiles(w_out[l][:, c * GW:(c + 1) * GW]).reshape(P, CW)

        def put(name, a):
            at, w = SB[name]
            sb[l, :, at:at + w] = a.reshape(-1, w) if a.ndim == 1 else a.reshape(P, w)
        taps = np.concatenate([f("gdn_conv")[l], f("mlstm_conv")[l]], 1)
        put("conv", taps.reshape(TAPS, 15, P).transpose(2, 1, 0))
        put("gate_bias", np.concatenate([f("gdn_dt_bias")[l], f("mlstm_f_bias")[l], np.zeros(6, np.float32), f("mlstm_i_bias")[l]]))
        put("a_log", f("gdn_a_log")[l])
        put("gdn_norm", f("gdn_norm")[l])
        put("ml_norm", f("mlstm_norm")[l])
        put("ada_b", f("ada_b")[l].reshape(-1, P).T[:, MOD2:])
        for name in ("ln_g", "ln_b"):
            put(name, f(name)[l, :2].reshape(-1, P).T)
    return {"wb": wb, "sb": sb, "ln_g": f("ln_g"), "ln_b": f("ln_b")}


def pack_ffn(up, down):
    out = np.zeros((FFN_N, P, CW), np.float32)
    u = up.reshape(KT, P, 2, FT, P)
    for f in range(FT):
        pos = 0 if f == 0 else 1 + 3 * ((f - 1) // 2) + (f - 1) % 2
        out[pos] = u[:, :, :, f, :].transpose(1, 0, 2, 3).reshape(P, CW)
    d = down.reshape(FT // 2, 2, P, DM)
    for i in range(FT // 2):
        pos = 3 + 3 * i if i < FT // 2 - 1 else FFN_N - 1
        out[pos] = d[i].transpose(1, 0, 2).reshape(P, CW)
    return out


def kernel(**inputs):
    import concourse.bacc as bacc
    from concourse.bass_utils import run_bass_kernel_spmd

    nc = bacc.Bacc("TRN2", target_bir_lowering=False, num_devices=1)
    arrays, tensors = {}, {}
    for name, a in {**pack_first(inputs), **pack_second(inputs)}.items():
        arrays["in_" + name] = np.ascontiguousarray(a)
        tensors[name] = nc.dram_tensor("in_" + name, a.shape, F32, kind="ExternalInput").ap()
    tensors["out"] = nc.dram_tensor("out", (1, SEQ, DM), F32, kind="ExternalOutput").ap()
    build(nc, tensors)
    return run_bass_kernel_spmd(nc, [arrays], core_ids=[0]).results[0]["out"]
```
